# Optimizing a Trainium2 kernel written in Bass

```python
import math
import jax, jax.numpy as jnp
from jax import lax
import numpy as np

D_MODEL = 1024
BATCH = 1
SEQ = 1024
DEPTH = 1

ATT_HEADS = 4
ATT_QK_DIM = D_MODEL // 16
ATT_V_DIM = 2 * ATT_QK_DIM
ATT_WIDTH = ATT_HEADS * ATT_V_DIM
Q_COLS = ATT_HEADS * 2 * ATT_QK_DIM
Q_BLOCK = 128
LRU_WIDTH = D_MODEL // 4
LRU_BLOCKS = 4
LRU_BLOCK_DIM = LRU_WIDTH // LRU_BLOCKS
LRU_CONV = 4
LRU_C = 8.0
CONV_WIDTH = D_MODEL // 4
CONV_KERNEL = 31
COL_WIDTHS = (Q_COLS, Q_COLS, ATT_WIDTH, LRU_WIDTH, LRU_WIDTH, CONV_WIDTH, CONV_WIDTH)
IN_COLS = sum(COL_WIDTHS)
SPLIT_POINTS = tuple(sum(COL_WIDTHS[:i + 1]) for i in range(len(COL_WIDTHS) - 1))
V_START = 2 * Q_COLS
V_END = V_START + ATT_WIDTH
D_MIX = ATT_WIDTH + LRU_WIDTH + CONV_WIDTH
N_EXPERTS = 32
TOP_K = 4
D_EXPERT = D_MODEL
SWIGLU_LIMIT = 7.0
SWIGLU_ALPHA = 1.702
MOE_BLOCK = 128
LN_EPS = 1e-5

kernel_name = "hymba_style_diffattn_rglru_conformer_moe_deepnorm"

def layer_norm(x, g, b):
    xf = x.astype(jnp.float32)
    mu = jnp.mean(xf, axis=-1, keepdims=True)
    var = jnp.mean(jnp.square(xf - mu), axis=-1, keepdims=True)
    y = (xf - mu) * lax.rsqrt(var + LN_EPS)
    return (y * g.astype(jnp.float32) + b.astype(jnp.float32)).astype(x.dtype)

def causal_depthwise_conv(x, w, b):
    k = w.shape[0]
    y = lax.conv_general_dilated(
        x, w.astype(x.dtype)[:, None, :], window_strides=(1,),
        padding=[(k - 1, 0)], dimension_numbers=('NWC', 'WIO', 'NWC'),
        feature_group_count=x.shape[-1])
    return y + b.astype(x.dtype)

def diff_attention(q, k, v, lam, slopes):
    B, S, H, _, DK = q.shape
    nqb = S // Q_BLOCK
    scale = DK ** -0.5
    qb = q.reshape(B, nqb, Q_BLOCK, H, 2, DK).transpose(1, 0, 2, 3, 4, 5)
    k_pos = jnp.arange(S)

    def block(args):
        q_blk, i = args
        q_pos = i * Q_BLOCK + jnp.arange(Q_BLOCK)
        s = jnp.einsum('bqhcd,bkhcd->bhcqk', q_blk, k).astype(jnp.float32) * scale
        dist = (q_pos[:, None] - k_pos[None, :]).astype(jnp.float32)
        s = s - (slopes[:, None, None] * dist[None])[None, :, None]
        s = jnp.where((dist >= 0)[None, None, None], s, -jnp.inf)
        p = jax.nn.softmax(s, axis=-1)
        attn = p[:, :, 0] - lam * p[:, :, 1]
        return jnp.einsum('bhqk,bkhd->bqhd', attn.astype(v.dtype), v)

    o = lax.map(block, (qb, jnp.arange(nqb)))
    return o.transpose(1, 0, 2, 3, 4).reshape(B, S, H, v.shape[-1])

def rg_lru(xc, wa, ba, wx, bx, lam_param):
    B, S, C = xc.shape
    xr = xc.reshape(B, S, LRU_BLOCKS, LRU_BLOCK_DIM)
    gate_a = jax.nn.sigmoid(jnp.einsum('bsnc,ncd->bsnd', xr, wa).reshape(B, S, C) + ba).astype(jnp.float32)
    gate_x = jax.nn.sigmoid(jnp.einsum('bsnc,ncd->bsnd', xr, wx).reshape(B, S, C) + bx).astype(jnp.float32)
    log_a = -LRU_C * gate_a * jax.nn.softplus(-lam_param.astype(jnp.float32))
    a = jnp.exp(log_a)
    mult = jnp.sqrt(1.0 - jnp.exp(2.0 * log_a))
    bterm = mult * gate_x * xc.astype(jnp.float32)

    def combine(left, right):
        a_l, b_l = left
        a_r, b_r = right
        return a_l * a_r, a_r * b_l + b_r

    _, h = lax.associative_scan(combine, (a, bterm), axis=1)
    return h.astype(xc.dtype)

def moe(x, router_w, router_b, w1, b1, w2, b2):
    B, S, D = x.shape
    T = B * S
    xf = x.reshape(T, D)
    logits = (xf @ router_w + router_b).astype(jnp.float32)
    top_vals, top_idx = lax.top_k(logits, TOP_K)
    gates = jax.nn.softmax(top_vals, axis=-1)
    n_assign = T * TOP_K
    expert_flat = top_idx.reshape(-1)
    token_flat = jnp.arange(n_assign) // TOP_K
    order = jnp.argsort(expert_flat)
    s_expert = expert_flat[order]
    s_token = token_flat[order]
    s_gate = gates.reshape(-1)[order]
    counts = jnp.bincount(expert_flat, length=N_EXPERTS)
    starts = jnp.cumsum(counts) - counts
    padded = (counts + MOE_BLOCK - 1) // MOE_BLOCK * MOE_BLOCK
    padded_end = jnp.cumsum(padded)
    padded_start = padded_end - padded
    dest = padded_start[s_expert] + jnp.arange(n_assign) - starts[s_expert]
    n_blocks = -(-(n_assign + N_EXPERTS * (MOE_BLOCK - 1)) // MOE_BLOCK)
    rows = n_blocks * MOE_BLOCK
    x_disp = jnp.zeros((rows, D), x.dtype).at[dest].set(xf[s_token])
    block_expert = jnp.minimum(
        jnp.searchsorted(padded_end, jnp.arange(n_blocks) * MOE_BLOCK, side='right'), N_EXPERTS - 1)

    def expert_block(args):
        xb, e = args
        hdn = xb @ w1[e] + b1[e]
        glu, lin = jnp.split(hdn, 2, axis=-1)
        glu = jnp.minimum(glu, SWIGLU_LIMIT)
        lin = jnp.clip(lin, -SWIGLU_LIMIT, SWIGLU_LIMIT)
        act = glu * jax.nn.sigmoid(SWIGLU_ALPHA * glu) * (lin + 1.0)
        return act @ w2[e] + b2[e]

    y_disp = lax.map(expert_block, (x_disp.reshape(n_blocks, MOE_BLOCK, D), block_expert)).reshape(rows, D)
    y = y_disp[dest] * s_gate[:, None].astype(x.dtype)
    out = jax.ops.segment_sum(y, s_token, num_segments=T)
    return out.reshape(B, S, D)

def setup_inputs(seed: int = 0) -> dict:
    key = jax.random.key(seed)
    ks = jax.random.split(key, 32)
    L, D = DEPTH, D_MODEL
    beta = (8.0 * DEPTH) ** -0.25

    def nrm(k, shape, scale):
        return jax.random.normal(k, shape, jnp.float32) * scale

    x = nrm(ks[0], (BATCH, SEQ, D), 1.0)
    ln_in_g = 1.0 + nrm(ks[1], (D,), 0.02)
    ln_in_b = nrm(ks[2], (D,), 0.02)
    col_scale = jnp.ones((IN_COLS,), jnp.float32).at[V_START:V_END].set(beta)
    w_in = nrm(ks[3], (L, D, IN_COLS), D ** -0.5) * col_scale
    lam_q1 = nrm(ks[4], (L, ATT_QK_DIM), 0.1)
    lam_k1 = nrm(ks[5], (L, ATT_QK_DIM), 0.1)
    lam_q2 = nrm(ks[6], (L, ATT_QK_DIM), 0.1)
    lam_k2 = nrm(ks[7], (L, ATT_QK_DIM), 0.1)
    subln_g = 1.0 + nrm(ks[8], (L, ATT_V_DIM), 0.02)
    lru_conv_w = nrm(ks[9], (L, LRU_CONV, LRU_WIDTH), LRU_CONV ** -0.5)
    lru_conv_b = nrm(ks[10], (L, LRU_WIDTH), 0.01)
    lru_wa = nrm(ks[11], (L, LRU_BLOCKS, LRU_BLOCK_DIM, LRU_BLOCK_DIM), LRU_BLOCK_DIM ** -0.5)
    lru_ba = nrm(ks[12], (L, LRU_WIDTH), 0.01)
    lru_wx = nrm(ks[13], (L, LRU_BLOCKS, LRU_BLOCK_DIM, LRU_BLOCK_DIM), LRU_BLOCK_DIM ** -0.5)
    lru_bx = nrm(ks[14], (L, LRU_WIDTH), 0.01)
    u = jax.random.uniform(ks[15], (L, LRU_WIDTH), jnp.float32, minval=0.9, maxval=0.999)
    sig = u ** (1.0 / LRU_C)
    lru_lambda = jnp.log(sig) - jnp.log1p(-sig)
    cf_conv_w = nrm(ks[16], (L, CONV_KERNEL, CONV_WIDTH), CONV_KERNEL ** -0.5)
    cf_conv_b = nrm(ks[17], (L, CONV_WIDTH), 0.01)
    cf_ln_g = 1.0 + nrm(ks[18], (L, CONV_WIDTH), 0.02)
    cf_ln_b = nrm(ks[19], (L, CONV_WIDTH), 0.02)
    w_out = nrm(ks[20], (L, D_MIX, D), D_MIX ** -0.5 * beta)
    ln1_g = 1.0 + nrm(ks[21], (L, D), 0.02)
    ln1_b = nrm(ks[22], (L, D), 0.02)
    router_w = nrm(ks[23], (L, D, N_EXPERTS), D ** -0.5)
    router_b = nrm(ks[24], (L, N_EXPERTS), 0.01)
    moe_w1 = nrm(ks[25], (L, N_EXPERTS, D, 2 * D_EXPERT), D ** -0.5)
    moe_b1 = nrm(ks[26], (L, N_EXPERTS, 2 * D_EXPERT), 0.01)
    moe_w2 = nrm(ks[27], (L, N_EXPERTS, D_EXPERT, D), D_EXPERT ** -0.5 * beta)
    moe_b2 = nrm(ks[28], (L, N_EXPERTS, D), 0.01)
    ln2_g = 1.0 + nrm(ks[29], (L, D), 0.02)
    ln2_b = nrm(ks[30], (L, D), 0.02)
    return {"x": x, "ln_in_g": ln_in_g, "ln_in_b": ln_in_b, "w_in": w_in,
            "lam_q1": lam_q1, "lam_k1": lam_k1, "lam_q2": lam_q2, "lam_k2": lam_k2,
            "subln_g": subln_g, "lru_conv_w": lru_conv_w, "lru_conv_b": lru_conv_b,
            "lru_wa": lru_wa, "lru_ba": lru_ba, "lru_wx": lru_wx, "lru_bx": lru_bx,
            "lru_lambda": lru_lambda, "cf_conv_w": cf_conv_w, "cf_conv_b": cf_conv_b,
            "cf_ln_g": cf_ln_g, "cf_ln_b": cf_ln_b, "w_out": w_out,
            "ln1_g": ln1_g, "ln1_b": ln1_b, "router_w": router_w, "router_b": router_b,
            "moe_w1": moe_w1, "moe_b1": moe_b1, "moe_w2": moe_w2, "moe_b2": moe_b2,
            "ln2_g": ln2_g, "ln2_b": ln2_b}

def reference(x, ln_in_g, ln_in_b, w_in, lam_q1, lam_k1, lam_q2, lam_k2, subln_g,
              lru_conv_w, lru_conv_b, lru_wa, lru_ba, lru_wx, lru_bx, lru_lambda,
              cf_conv_w, cf_conv_b, cf_ln_g, cf_ln_b, w_out, ln1_g, ln1_b,
              router_w, router_b, moe_w1, moe_b1, moe_w2, moe_b2, ln2_g, ln2_b):
    B, S, D = x.shape
    alpha = (2.0 * DEPTH) ** 0.25
    slopes = jnp.exp2(-8.0 * (jnp.arange(ATT_HEADS, dtype=jnp.float32) + 1.0) / ATT_HEADS)
    h = layer_norm(x, ln_in_g, ln_in_b)
    for l in range(DEPTH):
        u = h @ w_in[l]
        q, k, v, lru_x, lru_y, cf_a, cf_b = jnp.split(u, SPLIT_POINTS, axis=-1)
        lam_init = 0.8 - 0.6 * math.exp(-0.3 * l)
        lam = (jnp.exp(jnp.sum(lam_q1[l].astype(jnp.float32) * lam_k1[l].astype(jnp.float32)))
               - jnp.exp(jnp.sum(lam_q2[l].astype(jnp.float32) * lam_k2[l].astype(jnp.float32)))
               + lam_init)
        att = diff_attention(q.reshape(B, S, ATT_HEADS, 2, ATT_QK_DIM),
                             k.reshape(B, S, ATT_HEADS, 2, ATT_QK_DIM),
                             v.reshape(B, S, ATT_HEADS, ATT_V_DIM), lam, slopes)
        af = att.astype(jnp.float32)
        af = af * lax.rsqrt(jnp.mean(jnp.square(af), axis=-1, keepdims=True) + LN_EPS)
        att = (af * subln_g[l].astype(jnp.float32) * (1.0 - lam_init)).astype(h.dtype).reshape(B, S, ATT_WIDTH)
        xc = causal_depthwise_conv(lru_x, lru_conv_w[l], lru_conv_b[l])
        rec = rg_lru(xc, lru_wa[l], lru_ba[l], lru_wx[l], lru_bx[l], lru_lambda[l]) * jax.nn.gelu(lru_y)
        c = cf_a * jax.nn.sigmoid(cf_b)
        c = causal_depthwise_conv(c, cf_conv_w[l], cf_conv_b[l])
        c = jax.nn.silu(layer_norm(c, cf_ln_g[l], cf_ln_b[l]))
        mix = jnp.concatenate([att, rec, c], axis=-1) @ w_out[l]
        h = layer_norm(alpha * h + mix, ln1_g[l], ln1_b[l])
        ff = moe(h, router_w[l], router_b[l], moe_w1[l], moe_b1[l], moe_w2[l], moe_b2[l])
        h = layer_norm(alpha * h + ff, ln2_g[l], ln2_b[l])
    return h


_drawn_inputs = setup_inputs


def setup_inputs(seed=0):
    import zlib

    import numpy as np

    out = dict(_drawn_inputs(seed))
    spreads = {}
    factors = {'lam_k1': 3.421,
     'lam_q2': 3.202,
     'subln_g': 4.171,
     'lru_conv_b': 2.956,
     'lru_ba': 200.0,
     'lru_bx': 162.97,
     'cf_conv_b': 8.0,
     'cf_ln_g': 6.707,
     'cf_ln_b': 15.542,
     'router_b': 2.669,
     'moe_b1': 8.0,
     'moe_b2': 8.0,
     'ln2_g': 25.263,
     'ln2_b': 23.811}
    for name, (base, spread) in spreads.items():
        noise = np.random.default_rng([zlib.crc32(name.encode()), seed]).standard_normal(out[name].shape)
        drawn = base * np.exp(spread * noise) if base else spread * noise
        out[name] = __import__('jax').numpy.asarray(drawn.astype(out[name].dtype))
    for name, factor in factors.items():
        out[name] = (out[name] * factor).astype(out[name].dtype)
    return out
```

```python
import math
from contextlib import ExitStack

import concourse.bass as bass
from concourse import mybir

F32 = mybir.dt.float32
F16 = mybir.dt.float16
BF16 = mybir.dt.bfloat16
I32 = mybir.dt.int32
U32 = mybir.dt.uint32
ALU = mybir.AluOpType
ACT = mybir.ActivationFunctionType
AX = mybir.AxisListType

P = 128
D = 1024
S = 1024
KT = D // P
TT = S // P
HALF = 512
EPS = 1e-5
ALPHA = 2.0 ** 0.25

HEADS = 4
DK = D // 16
DV = 2 * DK
SCALE = DK ** -0.5
SLOPES = [2.0 ** (-8.0 * (h + 1) / HEADS) for h in range(HEADS)]
LAM_INIT = 0.8 - 0.6 * math.exp(0.0)
MASKED = -1.0e30

GROUP = D // 4
CT = GROUP // P
LRU_TAPS, CF_TAPS = 4, 31
LRU_C = 8.0

EXPERTS = 32
TOP_K = 4
LIMIT = 7.0
SWIGLU_ALPHA = 1.702
CAP = 256
PIECE = 256
PIECES = 12
MAX_BLOCKS = (S * TOP_K + EXPERTS * CAP) // CAP
TABLE = MAX_BLOCKS + 1
WIDTHS = (128, 144, 160, 192, 256)
BIG = 1 << 20

IN_PIECES = ["cf_a", "cf_b", "lru_x", "lru_y", "v0", "v1", "q0", "q1", "k0", "k1"]
IN_COLUMN = {"q0": 0, "q1": 256, "k0": 512, "k1": 768, "v0": 1024, "v1": 1280,
             "lru_x": 1536, "lru_y": 1792, "cf_a": 2048, "cf_b": 2304}
FRONT_SLOTS = 4

ROW_LRU_W, ROW_LRU_B, ROW_BA, ROW_BX, ROW_LAMBDA = 0, 4, 5, 6, 7
ROW_CF_W, ROW_CF_B, ROW_CF_G, ROW_CF_BETA, CHAN_ROWS = 8, 39, 40, 41, 42


def evacuation_jobs():
    jobs = [("chan", "act"), ("dpar", "act"), ("b1T", "act")]
    jobs += [(("hT", 0, k), "act" if k % 2 else "dve") for k in range(KT)]
    jobs += [(("in", p, c, 0), "act") for p in ("cf_a", "cf_b") for c in range(CT)]
    jobs += [(("hT", 1, k), "act" if k % 2 else "dve") for k in range(KT)]
    jobs += [(("in", p, c, 1), "act") for p in ("cf_a", "cf_b") for c in range(CT)]
    jobs += [(("in", p, c, h), "act") for p in ("lru_x", "lru_y") for c in range(CT) for h in range(2)]
    jobs += [(("v", t), "act") for t in range(4)]
    jobs += [(("mean", h), "dve") for h in range(2)]
    jobs += [(("v", t), "act") for t in (4, 5)]
    jobs += [(("gate", 0, w, h), "act") for w in ("a", "x") for h in range(2)]
    jobs += [(("v", t), "act") for t in (6, 7)]
    jobs += [(("var", h), "act") for h in range(2)]
    jobs += [(("in", "q0", c, h), "act") for c in range(CT) for h in range(2)]
    jobs += [(("gate", 1, w, h), "act") for w in ("a", "x") for h in range(2)]
    jobs += [(("in", p, c, h), "act") for p in ("q1", "k0", "k1") for c in range(CT) for h in range(2)]
    units = [(h, q) for h in range(HEADS) for q in range(TT)]
    for h, q in units:
        jobs += [(("pT", h, q, g), "act") for g in range(q // 4 + 1)]
        jobs += [(("o", h, q), "dve")]
    jobs += [(("oT", h, g), "act") for h in range(HEADS) for g in range(2)]
    for t in range(TT + 1):
        if t < TT:
            jobs += [(("mix", t, c), "dve") for c in range(2)]
        if t:
            jobs += [(("h1T", t - 1, g), "act") for g in range(2)] + [(("logit", t - 1), "dve")]
    jobs += [("rank", "dve")]
    for t in range(TT):
        jobs += [(("gT", t), "act")] + [(("b2", t, c), "dve") for c in range(2)]
    return jobs


def hybrid_layer(nc, x, ln_in_g, ln_in_b, w_in, lam_q1, lam_k1, lam_q2, lam_k2, subln_g,
                 lru_conv_w, lru_conv_b, lru_wa, lru_ba, lru_wx, lru_bx, lru_lambda,
                 cf_conv_w, cf_conv_b, cf_ln_g, cf_ln_b, w_out, ln1_g, ln1_b,
                 router_w, router_b, moe_w1, moe_b1, moe_w2, moe_b2, ln2_g, ln2_b, out):
    JOBS = evacuation_jobs()
    NUMBER = {name: n for n, (name, _) in enumerate(JOBS)}
    ORDINAL = {}
    for engine in ("act", "dve"):
        for n, name in enumerate(name for name, by in JOBS if by == engine):
            ORDINAL[name] = n
    READER = dict(JOBS)
    UNITS = [(h, q) for h in range(HEADS) for q in range(TT)]

    h1_rows = nc.dram_tensor("h1_rows", [S, D], F32).ap()
    y_rows = nc.dram_tensor("y_rows", [S * TOP_K + CAP, D], F32).ap()

    x_tiles = x[0].rearrange("(t p) d -> p t d", p=P)
    out_tiles = out[0].rearrange("(t p) d -> p t d", p=P)
    h1_tiles = h1_rows.rearrange("(t p) d -> p t d", p=P)
    w_in_v = w_in[0].rearrange("(k p) n -> p k n", p=P)
    w_out_v = w_out[0].rearrange("(k p) n -> p k n", p=P)
    w1_v = moe_w1[0].rearrange("e (k p) n -> e p k n", p=P)
    w2_v = moe_w2[0].rearrange("e (k p) n -> e p k n", p=P)

    ctx = ExitStack()
    with ctx:
        def sb(name, shape, dt=F32):
            return ctx.enter_context(nc.sbuf_tensor(name, shape, dt))

        def sem(name):
            return ctx.enter_context(nc.semaphore(name))

        ring = sb("ring", [P, PIECES, KT * PIECE])
        h_res = sb("h_res", [P, TT, D])
        big = sb("big", [P, KT, S])
        scr = sb("scr", [P, 4, S])
        cfb = sb("cfb", [P, CT, S])
        lrx = sb("lrx", [P, CT, S])

        def slot(s):
            return ring[:, s, :].rearrange("p (k n) -> p k n", k=KT)

        x_in = ring[:, 6:10, :].rearrange("p s (t d) -> p (s t) d", d=D)
        b1_rows = ring[0:EXPERTS, 10, :]
        chan_rows = ring[0:CHAN_ROWS, 11, 0:GROUP]
        dpar_rows = ring[0:2 * KT + 1, 11, GROUP:GROUP + P]
        lam_in = ring[:, 11, HALF:HALF + 4 * DK].rearrange("p (a n) -> p a n", a=4)
        qT = ring[:, 6:8, :].rearrange("p s (h t) -> p (s h) t", h=2)
        kT = ring[:, 8:10, :].rearrange("p s (h t) -> p (s h) t", h=2)
        v = ring[:, 10:12, :].rearrange("p s (t n) -> p (s t) n", n=HALF)
        lry = ring[:, 4, :].rearrange("p (i s) -> p i s", i=CT)
        cfa = ring[:, 5, :].rearrange("p (i s) -> p i s", i=CT)
        pT = ring[:, 5, :].rearrange("p (b k q) -> p b k q", b=2, k=TT)
        hT = big
        oT = big[:, 0:HEADS, :]
        maps = big[:, HEADS:, :].rearrange("p (b c) s -> p b c s", b=2)
        norm_rows = scr[:, 0:2, :]
        xc, ga, gx, mul = (scr[:, i, :] for i in range(4))
        alibi = scr[:, 2, :]
        h1T = big[:, 4, :].rearrange("p (k q) -> p k q", k=KT)
        one_hot = big[:, 5, :].rearrange("p (k t e) -> p k t e", k=TOP_K, e=EXPERTS)
        cmp = big[:, 6:8, :].rearrange("p a s -> p (a s)")[:, 0:TABLE * EXPERTS]\
            .rearrange("p (g e) -> p g e", e=EXPERTS)
        b2_rows = scr[0:EXPERTS, 3, :]
        by_expert = big[:, 4, :].rearrange("p (a t e) -> p a t e", a=4, e=EXPERTS)
        mask, gate_m, rows_at = by_expert[:, 0], by_expert[:, 1], by_expert[:, 2]
        gate_t = big[0:EXPERTS, 3, 0:2 * P].rearrange("p (a n) -> p a n", a=2)
        mask_b = big[:, 4, 3 * TT * EXPERTS:].bitcast(BF16)[:, 0:TT * EXPERTS].rearrange("p (t e) -> p t e", e=EXPERTS)
        xT = big[:, 0:2, :].rearrange("p a (k n) -> p (a k) n", n=CAP)
        actT = big[:, 2:4, :].rearrange("p a (k n) -> p (a k) n", n=CAP)
        yT = big[:, 4:6, :].rearrange("p a (k n) -> p (a k) n", n=CAP)
        x_rows = big[:, 6:8, :]
        y_out = lrx
        glu = cfb[:, 0, :].rearrange("p (b f n) -> p b f n", b=2, f=2)
        sig = cfb[:, 1, :].rearrange("p (b f n) -> p b f n", b=2, f=2)
        lin = scr[:, 3, :].rearrange("p (b f n) -> p b f n", b=2, f=2)
        pick = scr[:, 2, :].bitcast(F16).rearrange("p (t s) -> p t s", t=TT)
        y_got = big[:, :, :].rearrange("p (b k) s -> p b k s", b=2)

        ident = sb("ident", [P, P])
        eps_t = sb("eps_t", [P, 1])
        pad = sb("pad", [P, 16])
        chan_mean = sb("chan_mean", [P, P])
        before = sb("before", [P, P], BF16)
        ones = sb("ones", [P, P], BF16)
        chan = sb("chan", [P, CT, CHAN_ROWS])
        dpar = sb("dpar", [P, 2 * KT + 1])
        b1T = sb("b1T", [P, EXPERTS, 2 * KT])
        b1_now = sb("b1_now", [P, 2 * KT])
        gate_w = sb("gate_w", [P, 2, CT, P])
        router = sb("router", [P, KT, EXPERTS])
        router_bias = sb("router_bias", [P, EXPERTS])
        lam_s = sb("lam_s", [P, 8])
        soft = sb("soft", [P, 6, CT])
        decay = sb("decay", [P, 2, CT])
        gain_o = sb("gain_o", [P, 1])
        stats = sb("stats", [P, 2, 12])
        mv = sb("mv", [P, TT, 2])
        std = sb("std", [P, TT])
        inv = sb("inv", [P, TT])
        shift = sb("shift", [P, TT])
        top = sb("top", [P, 2, 2])
        ntop = sb("ntop", [P, 2, 2])
        mass = sb("mass", [P, 2, 2])
        rmass = sb("rmass", [P, 2, 2])
        coef = sb("coef", [P, 2, 1])
        o_sq = sb("o_sq", [P, HEADS * TT])
        o_std = sb("o_std", [P, HEADS * TT])
        o_inv = sb("o_inv", [P, HEADS * TT])
        sq_out = sb("sq_out", [P, P])
        logits = sb("logits", [P, TT, EXPERTS])
        best = sb("best", [P, TT, 8])
        best_at = sb("best_at", [P, TT, 8], U32)
        chosen = sb("chosen", [P, TT, TOP_K])
        gates = sb("gates", [P, TT, TOP_K])
        gsum = sb("gsum", [P, TT])
        rank_of = sb("rank_of", [P, EXPERTS, TT])
        rank_now = sb("rank_now", [P, TT])
        count = sb("count", [P, EXPERTS])
        blocks = sb("blocks", [P, EXPERTS])
        ends = sb("ends", [P, EXPERTS])
        starts = sb("starts", [P, EXPERTS])
        dest = sb("dest", [P, TT, TOP_K])
        dest_i = sb("dest_i", [P, TT, TOP_K], I32)
        expert_f = sb("expert_f", [P, TABLE])
        offset_f = sb("offset_f", [P, TABLE])
        left_f = sb("left_f", [P, TABLE])
        expert_i = sb("expert_i", [1, TABLE], I32)
        left_i = sb("left_i", [1, TABLE], I32)
        row_f = sb("row_f", [P, 2, TABLE])
        row_i = sb("row_i", [1, TABLE], I32)
        ones_t = sb("ones_t", [P, TABLE])
        first = sb("first", [P, EXPERTS])
        ends_i = sb("ends_i", [1, EXPERTS], I32)
        token_no = sb("token_no", [P, TT], F16)
        iota_e = sb("iota_e", [P, EXPERTS])
        iota_g = sb("iota_g", [P, TABLE])
        iota_s = sb("iota_s", [P, CAP], F16)
        token_at = sb("token_at", [P, 2], I32)

        ps = ctx.enter_context(nc.psum_tensor("ps", [P, 8, HALF], F32))

        def bank(name):
            return ps[:, 4 + NUMBER[name] % 4, :]

        x_loaded = [sem(f"x_loaded{i}") for i in range(4)]
        params_loaded = sem("params_loaded")
        gate_w_loaded = sem("gate_w_loaded")
        gather_go = sem("gather_go")
        w_loaded = [sem(f"w_loaded{i}") for i in range(PIECES)]
        norm_loaded = [sem(f"norm_loaded{i}") for i in range(3)]
        b2_loaded = sem("b2_loaded")
        const_ready = sem("const_ready")
        pool_step = sem("pool_step")
        dve_step = sem("dve_step")
        act_step = sem("act_step")
        job_full = sem("job_full")
        read_by = {"act": sem("read_by_act"), "dve": sem("read_by_dve")}
        eps_ready = sem("eps_ready")
        mean_ready = sem("mean_ready")
        std_ready = sem("std_ready")
        norm_ready = sem("norm_ready")
        normed = sem("normed")
        h_rows_ready = sem("h_rows_ready")
        glu_cf = sem("glu_cf")
        conv_out = sem("conv_out")
        squared = sem("squared")
        cf_scaled = sem("cf_scaled")
        cf_ready = sem("cf_ready")
        xc_ready = sem("xc_ready")
        decays = sem("decays")
        one_minus = sem("one_minus")
        root = sem("root")
        lru_ready = sem("lru_ready")
        decay_ready = sem("decay_ready")
        soft_s = sem("soft_s")
        lam_s1 = sem("lam_s1")
        alibi_ready = sem("alibi_ready")
        score_full = sem("score_full")
        score_read = sem("score_read")
        top_ready = sem("top_ready")
        exp_ready = sem("exp_ready")
        map_ready = sem("map_ready")
        o_ready = sem("o_ready")
        o_root = sem("o_root")
        o_scaled = sem("o_scaled")
        mix_mean = sem("mix_mean")
        mix_std = sem("mix_std")
        mix_norm = sem("mix_norm")
        mix_normed = sem("mix_normed")
        h1_gain = sem("h1_gain")
        h1_ready = sem("h1_ready")
        h1_stored = sem("h1_stored")
        gate_diff = sem("gate_diff")
        gate_exp = sem("gate_exp")
        mask_ready = sem("mask_ready")
        gate_m_ready = sem("gate_m_ready")
        tables_ready = sem("tables_ready")
        resid_ready = sem("resid_ready")
        pick_ready = sem("pick_ready")
        slots_full = sem("slots_full")
        slots_ready = sem("slots_ready")
        x_got = sem("x_got")
        xT_full = sem("xT_full")
        xT_read = sem("xT_read")
        piece_done = sem("piece_done")
        hidden_read = sem("hidden_read")
        lin_step = sem("lin_step")
        sig_ready = sem("sig_ready")
        swish_step = sem("swish_step")
        act_ready = sem("act_ready")
        yT_ready = sem("yT_ready")
        y_full = sem("y_full")
        y_read = sem("y_read")
        y_stored = sem("y_stored")
        rank_step = sem("rank_step")
        b1_step = sem("b1_step")
        got = [sem(f"got{i}") for i in range(8)]
        summed = sem("summed")
        fin_std = sem("fin_std")
        fin_norm = sem("fin_norm")
        fin_normed = sem("fin_normed")
        fin_gain = sem("fin_gain")
        out_ready = sem("out_ready")
        out_stored = sem("out_stored")

        def by_width(eng, left, body, at=0):
            if at == len(WIDTHS) - 1:
                body(WIDTHS[at])
                return
            with eng.If(left < WIDTHS[at] + 1):
                body(WIDTHS[at])
            with eng.Else():
                by_width(eng, left, body, at + 1)

        LAST_USE = {p: ("v", TT - 1) if p[0] == "v" else ("in", p, CT - 1, 1) for p in IN_PIECES}
        USES = [sum(n % FRONT_SLOTS == i for n in range(len(IN_PIECES))) for i in range(FRONT_SLOTS)]
        BEFORE = [16 * (USES[p] + 1) if p < FRONT_SLOTS else 0 for p in range(PIECES)]
        PARAM_LOADS = 16 * 19

        block = ctx.enter_context(nc.Block())

        def full(eng, name):
            eng.wait_ge(job_full, NUMBER[name] + 1)

        def was_read(eng, name):
            eng.wait_ge(read_by[READER[name]], ORDINAL[name] + 1)


        @block.sync
        def _(sp):
            def w_in_piece(i):
                name = IN_PIECES[i]
                if i >= FRONT_SLOTS:
                    full(sp, LAST_USE[IN_PIECES[i - FRONT_SLOTS]])
                c = IN_COLUMN[name]
                sp.dma_start(slot(i % FRONT_SLOTS), w_in_v[:, :, c:c + PIECE]).then_inc(w_loaded[i % FRONT_SLOTS], 16)

            for i in range(4):
                sp.dma_start(x_in[:, 2 * i:2 * i + 2, :], x_tiles[:, 2 * i:2 * i + 2, :]).then_inc(x_loaded[i], 16)
            for i in range(len(IN_PIECES)):
                w_in_piece(i)
                if i == 1:
                    sp.dma_start(norm_rows[:, 0, :], ln_in_g.partition_broadcast(P)).then_inc(norm_loaded[0], 16)
                    sp.dma_start(norm_rows[:, 1, :], ln_in_b.partition_broadcast(P)).then_inc(norm_loaded[0], 16)
            for i in range(4):
                last = max(n for n in range(len(IN_PIECES)) if n % FRONT_SLOTS == i)
                full(sp, LAST_USE[IN_PIECES[last]])
                sp.dma_start(slot(i), w_out_v[:, :, i * PIECE:(i + 1) * PIECE]).then_inc(w_loaded[i], 16)
            full(sp, ("o",) + UNITS[-1])
            sp.wait_ge(score_read, 2 * len(UNITS))
            sp.dma_start(norm_rows[:, 0, :], ln1_g[0].partition_broadcast(P)).then_inc(norm_loaded[1], 16)
            sp.dma_start(norm_rows[:, 1, :], ln1_b[0].partition_broadcast(P)).then_inc(norm_loaded[1], 16)
            sp.dma_start(b2_rows, moe_b2[0]).then_inc(b2_loaded, 16)

            def expert_piece(e, p):
                if p < 8:
                    c = (p % 2) * D + (p // 2) * PIECE
                    src = w1_v[e, :, :, c:c + PIECE]
                else:
                    c = (p - 8) * PIECE
                    src = w2_v[e, :, :, c:c + PIECE]
                if not isinstance(e, int):
                    src = src.rearrange("a p k n -> (a p) k n")
                sp.dma_start(slot(p), src).then_inc(w_loaded[p], 16)

            for p in range(4, PIECES):
                expert_piece(0, p)
            for t in range(TT):
                sp.wait_ge(h1_ready, t + 1)
                sp.dma_start(h1_tiles[:, t, :], h_res[:, t, :]).then_inc(h1_stored, 16)
            full(sp, ("mix", TT - 1, 1))
            for p in range(4):
                expert_piece(0, p)
            sp.dma_start(norm_rows[:, 0, :], ln2_g[0].partition_broadcast(P)).then_inc(norm_loaded[2], 16)
            sp.dma_start(norm_rows[:, 1, :], ln2_b[0].partition_broadcast(P)).then_inc(norm_loaded[2], 16)
            sp.wait_ge(tables_ready, 1)
            with sp.Fori(1, EXPERTS) as e:
                end = sp.value_load(ends_i[0:1, bass.ds(e - 1, 1)], min_val=1, max_val=MAX_BLOCKS)
                for p in range(PIECES):
                    sp.wait_ge(piece_done, end * PIECES + (p + 1))
                    expert_piece(bass.ds(e, 1), p)
            for t in range(TT):
                sp.wait_ge(out_ready, t + 1)
                sp.dma_start(out_tiles[:, t, :], h_res[:, t, :]).then_inc(out_stored, 16)
            sp.wait_ge(out_stored, 16 * TT)
            sp.wait_ge(h1_stored, 16 * TT)

        @block.gpsimd
        def _(pool):
            n = [0]

            def step(ins):
                n[0] += 1
                ins.then_inc(pool_step, 1)
                pool.wait_ge(pool_step, n[0])

            step(nc.gpsimd.memset(ident[:, :], 0.0))
            nc.gpsimd.affine_select(out=ident[:, :], in_=ident[:, :], compare_op=ALU.not_equal, fill=1.0,
                                    base=0, pattern=[[-1, P]], channel_multiplier=1).then_inc(const_ready, 1)
            step(nc.gpsimd.memset(gate_w[:, :, :, :], 0.0))
            for w, src in enumerate((lru_wa, lru_wx)):
                for i in range(CT):
                    for b in range(2):
                        pool.dma_start(gate_w[64 * b:64 * b + 64, w, i, 64 * b:64 * b + 64],
                                       src[0, 2 * i + b]).then_inc(gate_w_loaded, 16)
            nc.gpsimd.memset(chan_mean[:, :], 1.0 / GROUP)
            nc.gpsimd.memset(ones_t[:, :], 1.0)
            step(nc.gpsimd.memset(ones[:, :], 1.0))
            nc.gpsimd.affine_select(out=before[:, :], in_=ones[:, :], compare_op=ALU.is_gt, fill=0.0,
                                    base=0, pattern=[[1, P]], channel_multiplier=-1)
            nc.gpsimd.iota(iota_e[:, :], pattern=[[1, EXPERTS]], base=0, channel_multiplier=0,
                           allow_small_or_imprecise_dtypes=True)
            nc.gpsimd.iota(iota_g[:, :], pattern=[[1, TABLE]], base=0, channel_multiplier=0,
                           allow_small_or_imprecise_dtypes=True)
            nc.gpsimd.iota(iota_s[:, :], pattern=[[1, CAP]], base=0, channel_multiplier=0,
                           allow_small_or_imprecise_dtypes=True)
            nc.gpsimd.iota(token_no[:, :], pattern=[[P, TT]], base=0, channel_multiplier=1,
                           allow_small_or_imprecise_dtypes=True).then_inc(const_ready, 1)

            pool.wait_ge(norm_loaded[0], 32)
            full(pool, ("hT", 1, KT - 1))
            for t in range(TT):
                step(nc.gpsimd.tensor_tensor(h_res[:, t, :], h_res[:, t, :], norm_rows[:, 0, :], ALU.mult))
                nc.gpsimd.tensor_tensor(h_res[:, t, :], h_res[:, t, :], norm_rows[:, 1, :],
                                        ALU.add).then_inc(h_rows_ready, 1)

            pool.wait_ge(lru_ready, 2)
            step(nc.gpsimd.iota(alibi, pattern=[[1, S]], base=-(S - P), channel_multiplier=-1,
                                allow_small_or_imprecise_dtypes=True))
            step(nc.gpsimd.affine_select(out=alibi, in_=alibi, compare_op=ALU.is_ge, fill=MASKED,
                                         base=S - P, pattern=[[-1, S]], channel_multiplier=1))
            for h in range(HEADS):
                if h >= 2:
                    pool.wait_ge(score_read, 2 * TT * (h - 1))
                nc.gpsimd.tensor_scalar(scr[:, h % 2, :], alibi, SLOPES[h] / SCALE, None,
                                        ALU.mult).then_inc(alibi_ready, 1)

            nc.gpsimd.memset(pad[:, 0:1], 0.0).then_inc(xT_full, 4)
            nc.gpsimd.memset(pad[:, 1:2], 0.0).then_inc(piece_done, PIECES)
            def held():
                pool.sem_inc(gather_go, 1)

            pool.wait_ge(h1_stored, 16 * TT)
            pool.wait_ge(tables_ready, 1)
            total = pool.value_load(ends_i[0:1, EXPERTS - 1:EXPERTS], min_val=EXPERTS, max_val=MAX_BLOCKS)
            with pool.Fori(0, total + 1) as g:
                pool.wait_ge(xT_full, g * 4 + 4)
                pool.wait_ge(slots_ready, g + 1)
                held()
                for th in range(2):
                    pool.indirect_dma_start(
                        out=x_rows[:, th, :], out_offset=None, in_=h1_rows[:, :],
                        in_offset=bass.IndirectOffsetOnAxis(ap=token_at[:, th:th + 1], axis=0)
                    ).then_inc(x_got, 16)

            pool.wait_ge(xT_read, total * 4 + 4)
            pool.wait_ge(y_stored, total * 32 + 32)
            held()
            for t in range(TT):
                if t >= 2:
                    pool.wait_ge(summed, t - 1)
                for k in range(TOP_K):
                    pool.indirect_dma_start(
                        out=y_got[:, t % 2, k, :], out_offset=None, in_=y_rows[0:S * TOP_K, :],
                        in_offset=bass.IndirectOffsetOnAxis(ap=dest_i[:, t, k:k + 1], axis=0)
                    ).then_inc(got[4 * (t % 2) + k], 16)

        @block.scalar
        def _(act):
            n = [0]

            def step(ins):
                n[0] += 1
                ins.then_inc(act_step, 1)
                act.wait_ge(act_step, n[0])

            loads = [
                (chan_rows[ROW_LRU_W:ROW_LRU_W + LRU_TAPS, :], lru_conv_w[0]), (chan_rows[ROW_LRU_B:ROW_LRU_B + 1, :], lru_conv_b),
                (chan_rows[ROW_BA:ROW_BA + 1, :], lru_ba), (chan_rows[ROW_BX:ROW_BX + 1, :], lru_bx),
                (chan_rows[ROW_LAMBDA:ROW_LAMBDA + 1, :], lru_lambda),
                (chan_rows[ROW_CF_W:ROW_CF_W + CF_TAPS, :], cf_conv_w[0]), (chan_rows[ROW_CF_B:ROW_CF_B + 1, :], cf_conv_b),
                (chan_rows[ROW_CF_G:ROW_CF_G + 1, :], cf_ln_g), (chan_rows[ROW_CF_BETA:ROW_CF_BETA + 1, :], cf_ln_b),
                (dpar_rows[0:KT, :], ln_in_g.rearrange("(k p) -> k p", p=P)),
                (dpar_rows[KT:2 * KT, :], ln_in_b.rearrange("(k p) -> k p", p=P)),
                (dpar_rows[2 * KT:2 * KT + 1, :], subln_g), (b1_rows, moe_b1[0]),
                (router[:, :, :], router_w[0].rearrange("(k p) e -> p k e", p=P)),
                (router_bias[:, :], router_b[0].partition_broadcast(P)),
            ] + [(lam_in[:, i, :], a[0].partition_broadcast(P)) for i, a in enumerate((lam_q1, lam_k1, lam_q2, lam_k2))]
            for dst, src in loads:
                act.dma_start(dst, src).then_inc(params_loaded, 16)

            def finish(ins, name):
                ins.then_inc(read_by["act"], 1)

            act.wait_ge(eps_ready, 1)
            for hf in range(2):
                act.wait_ge(mean_ready, hf + 1)
                nc.scalar.activation(std[:, 4 * hf:4 * hf + 4], mv[:, 4 * hf:4 * hf + 4, 1], ACT.Sqrt,
                                     bias=eps_t[:, 0:1]).then_inc(std_ready, 1)
                act.wait_ge(norm_ready, hf + 1)
                for t in range(4 * hf, 4 * hf + 4):
                    nc.scalar.activation(h_res[:, t, :], x_in[:, t, :], ACT.Identity, bias=shift[:, t:t + 1],
                                         scale=inv[:, t:t + 1]).then_inc(normed, 1)

            full(act, "chan")
            finish(nc.scalar.copy(chan[:, :, :], bank("chan")[:, 0:CT * CHAN_ROWS].rearrange("p (i r) -> p i r", i=CT)), "chan")
            full(act, "dpar")
            finish(nc.scalar.copy(dpar[:, :], bank("dpar")[:, 0:2 * KT + 1]), "dpar")
            full(act, "b1T")
            finish(nc.scalar.copy(b1T[:, :, :].rearrange("p e k -> p k e"),
                                  bank("b1T").rearrange("p (k e) -> p k e", e=EXPERTS)), "b1T")
            act.wait_ge(read_by["act"], ORDINAL["b1T"] + 1)
            step(nc.scalar.mul(gain_o[:, :], dpar[:, 2 * KT:2 * KT + 1], 1.0 - LAM_INIT))

            def hT_read(hf, k):
                full(act, ("hT", hf, k))
                finish(nc.scalar.activation(hT[:, k, hf * HALF:(hf + 1) * HALF], bank(("hT", hf, k)), ACT.Identity,
                                            bias=dpar[:, KT + k:KT + k + 1], scale=dpar[:, k:k + 1]), None)

            lam_c = chan[:, :, ROW_LAMBDA]
            act.wait_ge(soft_s, 1)
            nc.scalar.activation(soft[:, 1, :], soft[:, 0, :], ACT.Exp).then_inc(soft_s, 1)
            act.wait_ge(soft_s, 3)
            nc.scalar.activation(soft[:, 3, :], soft[:, 2, :], ACT.Ln).then_inc(soft_s, 1)
            act.wait_ge(lam_s1, 1)
            nc.scalar.activation(lam_s[:, 2:4], lam_s[:, 0:2], ACT.Exp).then_inc(lam_s1, 1)

            for k in range(1, KT, 2):
                hT_read(0, k)

            def in_read(p, c, h):
                name = ("in", p, c, h)
                cols = slice(h * HALF, (h + 1) * HALF)
                full(act, name)
                if p == "cf_a":
                    finish(nc.scalar.copy(cfa[:, c, cols], bank(name)), name)
                elif p == "cf_b":
                    finish(nc.scalar.activation(cfb[:, c, cols], bank(name), ACT.Sigmoid), name)
                elif p == "lru_x":
                    finish(nc.scalar.copy(lrx[:, c, cols], bank(name)), name)
                elif p == "lru_y":
                    finish(nc.scalar.activation(lry[:, c, cols], bank(name), ACT.Gelu_apprx_tanh), name)
                else:
                    dst = qT if p[0] == "q" else kT
                    finish(nc.scalar.copy(dst[:, 2 * int(p[1]) + c, cols], bank(name)), name)

            def v_read(t):
                full(act, ("v", t))
                finish(nc.scalar.copy(v[:, t, :], bank(("v", t))), None)

            def gate_read(i):
                for w, dst, row in (("a", ga, ROW_BA), ("x", gx, ROW_BX)):
                    for h in range(2):
                        full(act, ("gate", i, w, h))
                        if i and w == "a" and not h:
                            act.wait_ge(lru_ready, i)
                        finish(nc.scalar.activation(dst[:, h * HALF:(h + 1) * HALF], bank(("gate", i, w, h)),
                                                    ACT.Sigmoid, bias=chan[:, i, row:row + 1]), None)
                act.wait_ge(read_by["act"], ORDINAL[("gate", i, "x", 1)] + 1)
                if not i:
                    act.wait_ge(decay_ready, 1)
                step(nc.scalar.activation(mul, ga, ACT.Exp, scale=decay[:, 1, i:i + 1]))
                nc.scalar.activation(ga, ga, ACT.Exp, scale=decay[:, 0, i:i + 1]).then_inc(decays, 1)
                act.wait_ge(one_minus, i + 1)
                nc.scalar.activation(mul, mul, ACT.Sqrt).then_inc(root, 1)

            for p in ("cf_a", "cf_b"):
                for c in range(CT):
                    in_read(p, c, 0)
            for k in range(1, KT, 2):
                hT_read(1, k)
            for p in ("cf_a", "cf_b"):
                for c in range(CT):
                    in_read(p, c, 1)
            for p in ("lru_x", "lru_y"):
                for c in range(CT):
                    for h in range(2):
                        in_read(p, c, h)
            for t in range(6):
                v_read(t)
            gate_read(0)
            for h in range(2):
                was_read(act, ("mean", h))
                nc.scalar.activation(cfa[:, :, h * HALF:(h + 1) * HALF], cfb[:, :, h * HALF:(h + 1) * HALF],
                                     ACT.Square).then_inc(squared, 1)
            v_read(6)
            v_read(7)
            for h in range(2):
                if not h:
                    full(act, ("var", 1))
                finish(nc.scalar.activation(cfa[:, 0, h * HALF:(h + 1) * HALF], bank(("var", h)), ACT.Sqrt,
                                            bias=eps_t[:, 0:1]), None)
            for c in range(CT):
                for h in range(2):
                    in_read("q0", c, h)
            gate_read(1)
            act.wait_ge(cf_scaled, 1)
            for i in range(CT):
                nc.scalar.activation(cfb[:, i, :], cfb[:, i, :], ACT.Silu, bias=chan[:, i, ROW_CF_BETA:ROW_CF_BETA + 1],
                                     scale=chan[:, i, ROW_CF_G:ROW_CF_G + 1]).then_inc(cf_ready, 1)
            for p in ("q1", "k0", "k1"):
                for c in range(CT):
                    for h in range(2):
                        in_read(p, c, h)

            def exps(u):
                h, q = UNITS[u]
                act.wait_ge(top_ready, u + 1)
                for c in range(2):
                    m = maps[:, u % 2, c, 0:(q + 1) * P]
                    nc.scalar.activation(m, m, ACT.Exp, bias=ntop[:, u % 2, c:c + 1], scale=SCALE,
                                         accum_out=mass[:, u % 2, c:c + 1]).then_inc(exp_ready, 1)

            def map_read(u):
                h, q = UNITS[u]
                for g in range(q // 4 + 1):
                    k = min(4, q + 1 - 4 * g)
                    full(act, ("pT", h, q, g))
                    finish(nc.scalar.copy(pT[:, u % 2, 4 * g:4 * g + k, :],
                                          bank(("pT", h, q, g))[:, 0:k * P].rearrange("p (k q) -> p k q", q=P)), None)

            for u in range(len(UNITS)):
                exps(u)
                if u:
                    map_read(u - 1)
            map_read(len(UNITS) - 1)
            act.wait_ge(o_ready, HEADS * TT)
            nc.scalar.activation(o_std[:, :], o_sq[:, :], ACT.Sqrt, bias=eps_t[:, 0:1], scale=1.0 / DV).then_inc(o_root, 1)
            for h in range(HEADS):
                for g in range(2):
                    full(act, ("oT", h, g))
                    finish(nc.scalar.activation(oT[:, h, g * HALF:(g + 1) * HALF], bank(("oT", h, g)), ACT.Copy,
                                                scale=gain_o[:, 0:1]), None)

            def h1T_read(t):
                for g in range(2):
                    full(act, ("h1T", t, g))
                    finish(nc.scalar.copy(h1T[:, 4 * g:4 * g + 4, :],
                                          bank(("h1T", t, g)).rearrange("p (k q) -> p k q", q=P)), None)

            for t in range(TT):
                act.wait_ge(mix_mean, t + 1)
                nc.scalar.activation(std[:, t:t + 1], mv[:, t, 1:2], ACT.Sqrt, bias=eps_t[:, 0:1]).then_inc(mix_std, 1)
                act.wait_ge(mix_norm, t + 1)
                nc.scalar.activation(h_res[:, t, :], h_res[:, t, :], ACT.Identity, bias=shift[:, t:t + 1],
                                     scale=inv[:, t:t + 1]).then_inc(mix_normed, 1)
                if t:
                    h1T_read(t - 1)
            h1T_read(TT - 1)

            act.wait_ge(gate_diff, 1)
            nc.scalar.activation(gates[:, :, :], gates[:, :, :], ACT.Exp).then_inc(gate_exp, 1)
            for t in range(TT):
                full(act, ("gT", t))
                finish(nc.scalar.copy(gate_t[:, t % 2, :], bank(("gT", t))[0:EXPERTS, 0:P]), None)

            nc.scalar.copy(pad[:, 2:3], eps_t[:, :]).then_inc(yT_ready, 4)
            nc.scalar.copy(pad[:, 3:4], eps_t[:, :]).then_inc(y_read, 1)
            nc.scalar.copy(pad[:, 4:5], eps_t[:, :]).then_inc(y_stored, 32)
            act.wait_ge(tables_ready, 1)
            total = act.value_load(ends_i[0:1, EXPERTS - 1:EXPERTS], min_val=EXPERTS, max_val=MAX_BLOCKS)
            with act.Fori(0, total) as g:
                left = act.value_load(left_i[0:1, bass.ds(g, 1)], min_val=-BIG, max_val=BIG)
                row = act.value_load(row_i[0:1, bass.ds(g, 1)], min_val=0, max_val=S * TOP_K)

                def body(w):
                    for i in range(4):
                        act.wait_ge(hidden_read, g * 8 + (2 * i + 1))
                        if i >= 2:
                            act.wait_ge(act_ready, g * 4 + (i - 1))
                        nc.scalar.activation(sig[:, i % 2, :, 0:w], glu[:, i % 2, :, 0:w], ACT.Sigmoid,
                                             scale=SWIGLU_ALPHA).then_inc(sig_ready, 1)

                    def yT_read(q):
                        act.wait_ge(piece_done, g * PIECES + (PIECES + 8 + q + 1))
                        nc.scalar.copy(yT[:, 2 * q:2 * q + 2, 0:w],
                                       ps[:, q, :].rearrange("p (f n) -> p f n", f=2)[:, :, 0:w]).then_inc(yT_ready, 1)

                    def rows_read(q):
                        act.wait_ge(y_full, g * 4 + (q + 1))
                        b = (4, 5, 6, 5)[q]
                        cols = slice(q * PIECE, (q + 1) * PIECE)
                        if w > P:
                            nc.scalar.copy(y_out[0:w - P, 1, cols], ps[0:w - P, b, PIECE:2 * PIECE])
                        nc.scalar.copy(y_out[:, 0, cols], ps[:, b, 0:PIECE]).then_inc(y_read, 1)

                    yT_read(0)
                    yT_read(1)
                    act.wait_ge(y_stored, g * 32 + 32)
                    rows_read(0)
                    yT_read(2)
                    rows_read(1)
                    yT_read(3)
                    rows_read(2)
                    rows_read(3)
                    act.wait_ge(y_read, g * 4 + 5)
                    if w > P:
                        act.dma_start(y_rows[bass.ds(row + P, w - P), :], y_out[0:w - P, 1, :]).then_inc(y_stored, 16)
                    else:
                        act.sem_inc(y_stored, 16)
                    act.dma_start(y_rows[bass.ds(row, P), :], y_out[:, 0, :]).then_inc(y_stored, 16)

                by_width(act, left, body)

            for t in range(TT):
                act.wait_ge(summed, t + 1)
                nc.scalar.activation(std[:, t:t + 1], mv[:, t, 1:2], ACT.Sqrt, bias=eps_t[:, 0:1]).then_inc(fin_std, 1)
                act.wait_ge(fin_norm, t + 1)
                nc.scalar.activation(h_res[:, t, :], h_res[:, t, :], ACT.Identity, bias=shift[:, t:t + 1],
                                     scale=inv[:, t:t + 1]).then_inc(fin_normed, 1)

        @block.vector
        def _(dve):
            V = nc.vector
            n = [0]

            def mark(ins):
                n[0] += 1
                ins.then_inc(dve_step, 1)

            def settle(behind=0):
                dve.wait_ge(dve_step, n[0] - behind)

            def step(ins):
                mark(ins)
                settle()

            def finish(ins):
                ins.then_inc(read_by["dve"], 1)

            V.memset(eps_t[:, :], EPS).then_inc(eps_ready, 1)

            def row_stats(src, t):
                for c in range(2):
                    mark(V.bn_stats(stats[:, t % 2, 6 * c:6 * c + 6], src[:, c * HALF:(c + 1) * HALF]))
                settle()
                return V.bn_aggr(mv[:, t, :], stats[:, t % 2, :])

            def norm_terms(a, b):
                step(V.reciprocal(inv[:, a:b], std[:, a:b]))
                return V.scalar_tensor_tensor(shift[:, a:b], mv[:, a:b, 0], -1.0, inv[:, a:b], ALU.mult, ALU.mult)

            for hf in range(2):
                for t in range(4 * hf, 4 * hf + 4):
                    dve.wait_ge(x_loaded[t // 2], 16)
                    last = row_stats(x_in[:, t, :], t)
                    if t % 4 < 3:
                        mark(last)
                    else:
                        last.then_inc(mean_ready, 1)
                dve.wait_ge(mean_ready, hf + 1)
                dve.wait_ge(std_ready, hf + 1)
                norm_terms(4 * hf, 4 * hf + 4).then_inc(norm_ready, 1)

            dve.wait_ge(params_loaded, PARAM_LOADS)
            for i in range(2):
                ins = V.tensor_tensor_reduce(out=sq_out[:, 0:DK], in0=lam_in[:, 2 * i, :], in1=lam_in[:, 2 * i + 1, :],
                                             scale=1.0, scalar=0.0, op0=ALU.mult, op1=ALU.add,
                                             accum_out=lam_s[:, i:i + 1])
                if i:
                    ins.then_inc(lam_s1, 1)
                else:
                    step(ins)
            was_read(dve, "dpar")
            was_read(dve, "chan")
            lam_c = chan[:, :, ROW_LAMBDA]
            step(V.tensor_scalar(soft[:, 4, :], lam_c, -1.0, None, ALU.mult))
            V.tensor_tensor(soft[:, 0, :], lam_c, soft[:, 4, :], ALU.min).then_inc(soft_s, 1)
            dve.wait_ge(soft_s, 2)
            V.tensor_scalar(soft[:, 2, :], soft[:, 1, :], 1.0, None, ALU.add).then_inc(soft_s, 1)
            dve.wait_ge(soft_s, 4)
            step(V.tensor_scalar(soft[:, 5, :], soft[:, 2, :], -1.0, 1e-30, ALU.add, ALU.max))
            step(V.reciprocal(soft[:, 5, :], soft[:, 5, :]))
            step(V.tensor_tensor(soft[:, 5, :], soft[:, 5, :], soft[:, 3, :], ALU.mult))
            step(V.scalar_tensor_tensor(soft[:, 2, :], soft[:, 2, :], 1.0, soft[:, 5, :], ALU.is_equal, ALU.add))
            step(V.tensor_tensor(soft[:, 2, :], soft[:, 2, :], soft[:, 1, :], ALU.mult))
            step(V.scalar_tensor_tensor(soft[:, 2, :], soft[:, 4, :], 0.0, soft[:, 2, :], ALU.max, ALU.add))
            V.tensor_scalar(decay[:, 0, :], soft[:, 2, :], -LRU_C, None, ALU.mult)
            V.tensor_scalar(decay[:, 1, :], soft[:, 2, :], -2.0 * LRU_C, None, ALU.mult).then_inc(decay_ready, 1)
            dve.wait_ge(lam_s1, 2)
            step(V.tensor_tensor(lam_s[:, 4:5], lam_s[:, 3:4], lam_s[:, 2:3], ALU.subtract))
            step(V.tensor_scalar(lam_s[:, 5:6], lam_s[:, 4:5], -LAM_INIT, None, ALU.add))
            neg_lam = lam_s[:, 5:6]

            def hT_read(hf, k):
                full(dve, ("hT", hf, k))
                finish(V.tensor_scalar(hT[:, k, hf * HALF:(hf + 1) * HALF], bank(("hT", hf, k)),
                                       dpar[:, k:k + 1], dpar[:, KT + k:KT + k + 1], ALU.mult, ALU.add))

            for hf in range(2):
                for k in range(0, KT, 2):
                    hT_read(hf, k)

            was_read(dve, ("in", "cf_b", 1, 1))
            for i in range(CT):
                mark(V.tensor_tensor(cfa[:, i, :], cfa[:, i, :], cfb[:, i, :], ALU.mult))
            settle()

            def tap(out_t, in_t, i, row, back, first_bias=None):
                w = chan[:, i, row:row + 1]
                if first_bias is not None:
                    return V.tensor_scalar(out_t, in_t, w, chan[:, i, first_bias:first_bias + 1], ALU.mult, ALU.add)
                return V.scalar_tensor_tensor(out_t[:, back:], in_t[:, :S - back], w, out_t[:, back:], ALU.mult, ALU.add)

            for j in range(CF_TAPS):
                for i in range(CT):
                    if j:
                        settle(behind=1)
                    mark(tap(cfb[:, i, :], cfa[:, i, :], i, ROW_CF_W + CF_TAPS - 1 - j, j, None if j else ROW_CF_B))
            settle(behind=1)
            settle()
            V.engine_nop().then_inc(conv_out, 1)

            def lru_conv(i):
                for j in range(LRU_TAPS):
                    ins = tap(xc, lrx[:, i, :], i, ROW_LRU_W + LRU_TAPS - 1 - j, j, None if j else ROW_LRU_B)
                    if j < LRU_TAPS - 1:
                        step(ins)
                    else:
                        ins.then_inc(xc_ready, 1)

            def lru(i):
                dve.wait_ge(decays, i + 1)
                step(V.tensor_scalar(mul, mul, -1.0, 1.0, ALU.mult, ALU.add))
                V.tensor_scalar(mul, mul, 1e-30, None, ALU.max).then_inc(one_minus, 1)
                step(V.tensor_tensor(gx, gx, xc, ALU.mult))
                dve.wait_ge(root, i + 1)
                step(V.tensor_tensor(gx, gx, mul, ALU.mult))
                step(V.tensor_tensor_scan(lrx[:, i, :], ga, gx, 0.0, ALU.mult, ALU.add))
                V.tensor_tensor(lrx[:, i, :], lrx[:, i, :], lry[:, i, :], ALU.mult).then_inc(lru_ready, 1)

            was_read(dve, ("in", "lru_y", 1, 1))
            dve.wait_ge(h_rows_ready, TT)
            lru_conv(0)
            for h in range(2):
                full(dve, ("mean", h))
                cols = slice(h * HALF, (h + 1) * HALF)
                mark(V.tensor_tensor(cfb[:, 0, cols], cfb[:, 0, cols], bank(("mean", h)), ALU.subtract))
                finish(V.tensor_tensor(cfb[:, 1, cols], cfb[:, 1, cols], bank(("mean", h)), ALU.subtract))
            dve.wait_ge(xc_ready, 1)
            lru(0)
            was_read(dve, ("var", 1))
            step(V.reciprocal(cfa[:, 0, :], cfa[:, 0, :]))
            was_read(dve, ("mean", 1))
            mark(V.tensor_tensor(cfb[:, 0, :], cfb[:, 0, :], cfa[:, 0, :], ALU.mult))
            V.tensor_tensor(cfb[:, 1, :], cfb[:, 1, :], cfa[:, 0, :], ALU.mult).then_inc(cf_scaled, 1)
            lru_conv(1)
            dve.wait_ge(xc_ready, 2)
            lru(1)

            def score_read_unit(u):
                h, q = UNITS[u]
                nk = (q + 1) * P
                dve.wait_ge(alibi_ready, h + 1)
                if u >= 2:
                    full(dve, ("o",) + UNITS[u - 2])
                for c in range(2):
                    dve.wait_ge(score_full, 2 * u + c + 1)
                    V.tensor_tensor_reduce(
                        out=maps[:, u % 2, c, 0:nk],
                        in0=ps[:, 2 * c:2 * c + 2, :].rearrange("p b n -> p (b n)")[:, 0:nk],
                        in1=scr[:, h % 2, S - nk:S], scale=1.0, scalar=-3.0e38, op0=ALU.add, op1=ALU.max,
                        accum_out=top[:, u % 2, c:c + 1]).then_inc(score_read, 1)
                dve.wait_ge(score_read, 2 * u + 2)
                V.tensor_scalar(ntop[:, u % 2, :], top[:, u % 2, :], -SCALE, None, ALU.mult).then_inc(top_ready, 1)

            def combine(u):
                h, q = UNITS[u]
                nk = (q + 1) * P
                dve.wait_ge(exp_ready, 2 * u + 2)
                step(V.reciprocal(rmass[:, u % 2, :], mass[:, u % 2, :]))
                step(V.scalar_tensor_tensor(coef[:, u % 2, :], mass[:, u % 2, 0:1], neg_lam, rmass[:, u % 2, 1:2],
                                            ALU.mult, ALU.mult))
                V.scalar_tensor_tensor(maps[:, u % 2, 0, 0:nk], maps[:, u % 2, 1, 0:nk], coef[:, u % 2, :],
                                       maps[:, u % 2, 0, 0:nk], ALU.mult, ALU.add).then_inc(map_ready, 1)

            def o_read(u):
                h, q = UNITS[u]
                o = oT[:, h, q * P:(q + 1) * P]
                full(dve, ("o", h, q))
                finish(V.tensor_scalar(o, bank(("o", h, q))[:, 0:P], rmass[:, u % 2, 0:1], None, ALU.mult))
                was_read(dve, ("o", h, q))
                V.tensor_tensor_reduce(out=sq_out[:, :], in0=o, in1=o, scale=1.0, scalar=0.0, op0=ALU.mult,
                                       op1=ALU.add, accum_out=o_sq[:, u:u + 1]).then_inc(o_ready, 1)

            score_read_unit(0)
            for u in range(len(UNITS)):
                if u + 1 < len(UNITS):
                    score_read_unit(u + 1)
                combine(u)
                if u:
                    o_read(u - 1)
            o_read(len(UNITS) - 1)
            dve.wait_ge(o_root, 1)
            step(V.reciprocal(o_inv[:, :], o_std[:, :]))
            for h in range(HEADS):
                o = oT[:, h, :].rearrange("p (q n) -> p q n", n=P)
                V.tensor_tensor(o, o, o_inv[:, h * TT:(h + 1) * TT].unsqueeze(2).broadcast_to([P, TT, P]),
                                ALU.mult).then_inc(o_scaled, 1)

            def mix_read(t):
                for c in range(2):
                    full(dve, ("mix", t, c))
                    cols = slice(c * HALF, (c + 1) * HALF)
                    finish(V.scalar_tensor_tensor(h_res[:, t, cols], h_res[:, t, cols], ALPHA,
                                                  bank(("mix", t, c)), ALU.mult, ALU.add))
                was_read(dve, ("mix", t, 1))
                row_stats(h_res[:, t, :], t).then_inc(mix_mean, 1)
                dve.wait_ge(mix_mean, t + 1)
                dve.wait_ge(mix_std, t + 1)
                norm_terms(t, t + 1).then_inc(mix_norm, 1)
                dve.wait_ge(norm_loaded[1], 32)
                dve.wait_ge(mix_normed, t + 1)
                step(V.tensor_tensor(h_res[:, t, :], h_res[:, t, :], norm_rows[:, 0, :], ALU.mult))
                V.tensor_tensor(h_res[:, t, :], h_res[:, t, :], norm_rows[:, 1, :], ALU.add).then_inc(h1_ready, 1)

            def logit_read(t):
                full(dve, ("logit", t))
                finish(V.tensor_tensor(logits[:, t, :], bank(("logit", t))[:, 0:EXPERTS], router_bias[:, :], ALU.add))
                was_read(dve, ("logit", t))
                step(V.max(best[:, t, :], logits[:, t, :]))
                step(V.max_index(best_at[:, t, :], best[:, t, :], logits[:, t, :]))

            for t in range(TT):
                mix_read(t)
                if t:
                    logit_read(t - 1)
            logit_read(TT - 1)

            V.tensor_tensor(gates[:, :, :], best[:, :, 0:TOP_K], best[:, :, 0:1].broadcast_to([P, TT, TOP_K]),
                            ALU.subtract).then_inc(gate_diff, 1)
            step(V.tensor_copy(chosen[:, :, :], best_at[:, :, 0:TOP_K]))
            wide = [P, TT, EXPERTS]
            for k in range(TOP_K):
                mark(V.tensor_tensor(one_hot[:, k, :, :], iota_e[:, :].unsqueeze(1).broadcast_to(wide),
                                     chosen[:, :, k:k + 1].broadcast_to(wide), ALU.is_equal))
            settle()
            step(V.tensor_tensor(mask[:, :, :], one_hot[:, 0, :, :], one_hot[:, 1, :, :], ALU.add))
            step(V.tensor_tensor(mask[:, :, :], mask[:, :, :], one_hot[:, 2, :, :], ALU.add))
            step(V.tensor_tensor(mask[:, :, :], mask[:, :, :], one_hot[:, 3, :, :], ALU.add))
            V.tensor_copy(mask_b[:, :, :], mask[:, :, :]).then_inc(mask_ready, 1)
            full(dve, "rank")
            ranks = bank("rank")[:, 0:TT * EXPERTS].rearrange("p (t e) -> p t e", e=EXPERTS)
            step(V.tensor_copy(count[:, :], bank("rank")[:, TT * EXPERTS:(TT + 1) * EXPERTS]))
            step(V.tensor_scalar(blocks[:, :], count[:, :], float(CAP), 1.0, ALU.is_gt, ALU.add))
            step(V.scalar_tensor_tensor(blocks[:, :], count[:, :], 2.0 * CAP, blocks[:, :], ALU.is_gt, ALU.add))
            step(V.scalar_tensor_tensor(blocks[:, :], count[:, :], 3.0 * CAP, blocks[:, :], ALU.is_gt, ALU.add))
            step(V.tensor_tensor_scan(ends[:, :], ones_t[:, 0:EXPERTS], blocks[:, :], 0.0, ALU.mult, ALU.add))
            mark(V.tensor_tensor(starts[:, :], ends[:, :], blocks[:, :], ALU.subtract))
            mark(V.tensor_copy(ends_i[:, :], ends[0:1, :]))
            table = [P, TABLE, EXPERTS]
            step(V.tensor_tensor(cmp, ends[:, :].unsqueeze(1).broadcast_to(table),
                                 iota_g[:, :].unsqueeze(2).broadcast_to(table), ALU.is_le))
            step(V.tensor_reduce(expert_f[:, :], cmp, AX.X, ALU.add))
            step(V.tensor_scalar(expert_f[:, :], expert_f[:, :], EXPERTS - 1.0, None, ALU.min))
            mark(V.tensor_copy(expert_i[:, :], expert_f[0:1, :]))
            step(V.tensor_tensor(cmp, iota_e[:, :].unsqueeze(1).broadcast_to(table),
                                 expert_f[:, :].unsqueeze(2).broadcast_to(table), ALU.is_equal))
            step(V.tensor_tensor(cmp, cmp, starts[:, :].unsqueeze(1).broadcast_to(table), ALU.mult))
            step(V.tensor_reduce(offset_f[:, :], cmp, AX.X, ALU.add))
            step(V.tensor_tensor(offset_f[:, :], offset_f[:, :], iota_g[:, :], ALU.subtract))
            step(V.tensor_scalar(offset_f[:, :], offset_f[:, :], float(CAP), None, ALU.mult))
            step(V.tensor_tensor(cmp, iota_e[:, :].unsqueeze(1).broadcast_to(table),
                                 expert_f[:, :].unsqueeze(2).broadcast_to(table), ALU.is_equal))
            step(V.tensor_tensor(cmp, cmp, count[:, :].unsqueeze(1).broadcast_to(table), ALU.mult))
            step(V.tensor_reduce(left_f[:, :], cmp, AX.X, ALU.add))
            step(V.tensor_tensor(left_f[:, :], left_f[:, :], offset_f[:, :], ALU.add))
            mark(V.tensor_copy(left_i[:, :], left_f[0:1, :]))
            step(V.tensor_scalar(row_f[:, 0, :], left_f[:, :], float(CAP), None, ALU.min))
            step(V.tensor_tensor_scan(row_f[:, 1, :], ones_t[:, :], row_f[:, 0, :], 0.0, ALU.mult, ALU.add))
            step(V.tensor_tensor(row_f[:, 1, :], row_f[:, 1, :], row_f[:, 0, :], ALU.subtract))
            mark(V.tensor_copy(row_i[:, :], row_f[0:1, 1, :]))
            step(V.scalar_tensor_tensor(rank_of[:, :, :].rearrange("p e t -> p t e"), ranks, 1.0, mask[:, :, :],
                                        ALU.add, ALU.mult))
            step(V.tensor_scalar(rank_of[:, :, :], rank_of[:, :, :], -1.0, None, ALU.add))
            step(V.tensor_tensor_scan(first[:, :], ones_t[:, 0:EXPERTS], count[:, :], 0.0, ALU.mult, ALU.add))
            step(V.tensor_tensor(first[:, :], first[:, :], count[:, :], ALU.subtract))
            finish(V.tensor_tensor(rows_at[:, :, :], ranks, first[:, :].unsqueeze(1).broadcast_to(wide), ALU.add))
            was_read(dve, "rank")
            for k in range(TOP_K):
                step(V.tensor_tensor(cmp[:, 0:TT, :], one_hot[:, k, :, :], rows_at[:, :, :], ALU.mult))
                step(V.tensor_reduce(dest[:, :, k], cmp[:, 0:TT, :], AX.X, ALU.add))
            step(V.tensor_copy(dest_i[:, :, :], dest[:, :, :]))
            V.engine_nop().then_inc(tables_ready, 1)

            def pick_block(g, expert):
                own = rank_of[:, bass.ds(expert, 1), :].rearrange("p e t -> p (e t)")
                V.tensor_scalar(rank_now[:, :], own, offset_f[:, bass.ds(g, 1)], None, ALU.add).then_inc(rank_step, 1)
                dve.wait_ge(rank_step, g + 1)
                wide_s = [P, TT, CAP]
                V.tensor_tensor(pick, iota_s[:, :].unsqueeze(1).broadcast_to(wide_s),
                                rank_now[:, :].unsqueeze(2).broadcast_to(wide_s), ALU.is_equal).then_inc(pick_ready, 1)

            def slots_read(g):
                dve.wait_ge(slots_full, g + 1)
                V.tensor_copy(token_at[:, :], ps[:, 7, 0:2]).then_inc(slots_ready, 1)

            def xT_take(g):
                for j in range(4):
                    th, kh = j // 2, j % 2
                    b = (4, 5, 6, 4)[j]
                    dve.wait_ge(xT_full, g * 4 + (5 + j))
                    V.tensor_copy(xT[:, 4 * kh:4 * kh + 4, th * P:(th + 1) * P],
                                  ps[:, b, :].rearrange("p (k n) -> p k n", n=P)).then_inc(xT_read, 1)

            expert = dve.value_load(expert_i[0:1, 0:1], min_val=0, max_val=EXPERTS - 1)
            pick_block(0, expert)
            slots_read(0)
            V.tensor_copy(b1_now[:, :], b1T[:, bass.ds(expert, 1), :].rearrange("p e k -> p (e k)")).then_inc(b1_step, 1)
            dve.wait_ge(gate_exp, 1)
            step(V.tensor_reduce(gsum[:, :], gates[:, :, :], AX.X, ALU.add))
            step(V.reciprocal(gsum[:, :], gsum[:, :]))
            step(V.tensor_tensor(gates[:, :, :], gates[:, :, :], gsum[:, :].unsqueeze(2).broadcast_to([P, TT, TOP_K]), ALU.mult))
            for k in range(TOP_K):
                mark(V.tensor_tensor(one_hot[:, k, :, :], one_hot[:, k, :, :], gates[:, :, k:k + 1].broadcast_to(wide), ALU.mult))
            settle()
            step(V.tensor_tensor(gate_m[:, :, :], one_hot[:, 0, :, :], one_hot[:, 1, :, :], ALU.add))
            step(V.tensor_tensor(gate_m[:, :, :], gate_m[:, :, :], one_hot[:, 2, :, :], ALU.add))
            V.tensor_tensor(gate_m[:, :, :], gate_m[:, :, :], one_hot[:, 3, :, :], ALU.add).then_inc(gate_m_ready, 1)
            dve.wait_ge(h1_stored, 16 * TT)
            for t in range(TT):
                for c in range(2):
                    full(dve, ("b2", t, c))
                    cols = slice(c * HALF, (c + 1) * HALF)
                    finish(V.scalar_tensor_tensor(h_res[:, t, cols], h_res[:, t, cols], ALPHA, bank(("b2", t, c)),
                                                  ALU.mult, ALU.add))
            xT_take(0)

            total = dve.value_load(ends_i[0:1, EXPERTS - 1:EXPERTS], min_val=EXPERTS, max_val=MAX_BLOCKS)
            with dve.Fori(0, total) as g:
                left = dve.value_load(left_i[0:1, bass.ds(g, 1)], min_val=-BIG, max_val=BIG)
                after = dve.value_load(expert_i[0:1, bass.ds(g + 1, 1)], min_val=0, max_val=EXPERTS - 1)

                def body(w):
                    def biased(i):
                        if i >= 2:
                            dve.wait_ge(act_ready, g * 4 + (i - 1))
                        for part in range(2):
                            dve.wait_ge(piece_done, g * PIECES + (PIECES + 2 * i + part + 1))
                            dst = (glu, lin)[part]
                            for f in range(2):
                                b = KT * part + 2 * i + f
                                ins = V.tensor_scalar(dst[:, i % 2, f, 0:w],
                                                      ps[:, (2 * i + part) % 4, f * CAP:f * CAP + w],
                                                      b1_now[:, b:b + 1], LIMIT, ALU.add, ALU.min)
                            ins.then_inc(hidden_read, 1)
                        dve.wait_ge(hidden_read, g * 8 + (2 * i + 2))
                        V.tensor_scalar(lin[:, i % 2, :, 0:w], lin[:, i % 2, :, 0:w], -LIMIT, 1.0,
                                        ALU.max, ALU.add).then_inc(lin_step, 1)

                    def product(i):
                        dve.wait_ge(sig_ready, g * 4 + (i + 1))
                        V.tensor_tensor(sig[:, i % 2, :, 0:w], sig[:, i % 2, :, 0:w], glu[:, i % 2, :, 0:w],
                                        ALU.mult).then_inc(swish_step, 1)
                        dve.wait_ge(lin_step, g * 4 + (i + 1))
                        dve.wait_ge(swish_step, g * 4 + (i + 1))
                        V.tensor_tensor(actT[:, 2 * i:2 * i + 2, 0:w], sig[:, i % 2, :, 0:w], lin[:, i % 2, :, 0:w],
                                        ALU.mult).then_inc(act_ready, 1)

                    dve.wait_ge(b1_step, g + 1)
                    biased(0)
                    pick_block(g + 1, after)
                    biased(1)
                    product(0)
                    slots_read(g + 1)
                    biased(2)
                    product(1)
                    biased(3)
                    product(2)
                    product(3)
                    dve.wait_ge(act_ready, g * 4 + 4)
                    V.tensor_copy(b1_now[:, :], b1T[:, bass.ds(after, 1), :].rearrange("p e k -> p (e k)"))\
                        .then_inc(b1_step, 1)
                    xT_take(g + 1)

                by_width(dve, left, body)

            dve.wait_ge(norm_loaded[2], 32)
            for t in range(TT + 1):
                if t < TT:
                    for k in range(TOP_K):
                        dve.wait_ge(got[4 * (t % 2) + k], 16 * (t // 2 + 1))
                        step(V.scalar_tensor_tensor(h_res[:, t, :], y_got[:, t % 2, k, :], gates[:, t, k:k + 1],
                                                    h_res[:, t, :], ALU.mult, ALU.add))
                    row_stats(h_res[:, t, :], t).then_inc(summed, 1)
                    dve.wait_ge(summed, t + 1)
                    dve.wait_ge(fin_std, t + 1)
                    norm_terms(t, t + 1).then_inc(fin_norm, 1)
                if t:
                    dve.wait_ge(fin_normed, t)
                    step(V.tensor_tensor(h_res[:, t - 1, :], h_res[:, t - 1, :], norm_rows[:, 0, :], ALU.mult))
                    V.tensor_tensor(h_res[:, t - 1, :], h_res[:, t - 1, :], norm_rows[:, 1, :], ALU.add).then_inc(out_ready, 1)

        @block.tensor
        def _(pe):
            T = nc.tensor

            def begin(name):
                if NUMBER[name] >= 4:
                    was_read(pe, JOBS[NUMBER[name] - 4][0])

            def end(ins):
                ins.then_inc(job_full, 1)

            pe.wait_ge(const_ready, 1)
            pe.wait_ge(params_loaded, PARAM_LOADS)
            for i in range(CT):
                last = T.transpose(bank("chan")[:, i * CHAN_ROWS:(i + 1) * CHAN_ROWS], chan_rows[:, i * P:(i + 1) * P],
                                   ident[0:CHAN_ROWS, 0:CHAN_ROWS])
            end(last)
            end(T.transpose(bank("dpar")[:, 0:2 * KT + 1], dpar_rows, ident[0:2 * KT + 1, 0:2 * KT + 1]))
            for k in range(2 * KT):
                last = T.transpose(bank("b1T")[:, k * EXPERTS:(k + 1) * EXPERTS], b1_rows[:, k * P:(k + 1) * P],
                                   ident[0:EXPERTS, 0:EXPERTS])
            end(last)

            def hT_write(hf):
                for k in range(KT):
                    begin(("hT", hf, k))
                    for t in range(4):
                        if not k:
                            pe.wait_ge(normed, 4 * hf + t + 1)
                        last = T.transpose(bank(("hT", hf, k))[:, t * P:(t + 1) * P],
                                           h_res[:, 4 * hf + t, k * P:(k + 1) * P], ident[:, :])
                    end(last)

            def loaded(name):
                i = IN_PIECES.index(name)
                pe.wait_ge(w_loaded[i % FRONT_SLOTS], 16 * (i // FRONT_SLOTS + 1))
                return slot(i % FRONT_SLOTS)

            def in_write(p, c, h):
                name = ("in", p, c, h)
                w = loaded(p)
                begin(name)
                for k in range(KT):
                    last = T.matmul(bank(name), w[:, k, c * P:(c + 1) * P], hT[:, k, h * HALF:(h + 1) * HALF],
                                    start=k == 0, stop=k == KT - 1)
                end(last)

            def v_write(t):
                begin(("v", t))
                for c in range(2):
                    w = loaded(f"v{c}")
                    for k in range(KT):
                        last = T.matmul(bank(("v", t))[:, c * PIECE:(c + 1) * PIECE], hT[:, k, t * P:(t + 1) * P],
                                        w[:, k, :], start=k == 0, stop=k == KT - 1)
                end(last)

            def gate_write(i):
                pe.wait_ge(gate_w_loaded, 16 * 2 * CT * 2)
                pe.wait_ge(xc_ready, i + 1)
                for w, wn in enumerate(("a", "x")):
                    for h in range(2):
                        begin(("gate", i, wn, h))
                        end(T.matmul(bank(("gate", i, wn, h)), gate_w[:, w, i, :], xc[:, h * HALF:(h + 1) * HALF],
                                     start=True, stop=True))

            def channel_sum(kind, src):
                for h in range(2):
                    begin((kind, h))
                    if kind == "var":
                        pe.wait_ge(squared, h + 1)
                    for i in range(CT):
                        last = T.matmul(bank((kind, h)), chan_mean[:, :], src[:, i, h * HALF:(h + 1) * HALF],
                                        start=i == 0, stop=i == CT - 1)
                    end(last)

            hT_write(0)
            was_read(pe, ("hT", 0, KT - 1))
            was_read(pe, ("hT", 0, KT - 2))
            for p in ("cf_a", "cf_b"):
                for c in range(CT):
                    in_write(p, c, 0)
            hT_write(1)
            was_read(pe, ("hT", 1, KT - 1))
            was_read(pe, ("hT", 1, KT - 2))
            for p in ("cf_a", "cf_b"):
                for c in range(CT):
                    in_write(p, c, 1)
            for p in ("lru_x", "lru_y"):
                for c in range(CT):
                    for h in range(2):
                        in_write(p, c, h)
            for t in range(4):
                v_write(t)
            pe.wait_ge(const_ready, 2)
            pe.wait_ge(conv_out, 1)
            channel_sum("mean", cfb)
            v_write(4)
            v_write(5)
            gate_write(0)
            v_write(6)
            v_write(7)
            channel_sum("var", cfa)
            for c in range(CT):
                for h in range(2):
                    in_write("q0", c, h)
            gate_write(1)
            for p in ("q1", "k0", "k1"):
                for c in range(CT):
                    for h in range(2):
                        in_write(p, c, h)

            def scores(u):
                h, q = UNITS[u]
                for c in range(2):
                    if u:
                        pe.wait_ge(score_read, 2 * (u - 1) + c + 1)
                    for b in range(q // 4 + 1):
                        nk = min(HALF, (q + 1) * P - b * HALF)
                        last = T.matmul(ps[:, 2 * c + b, 0:nk], qT[DK * c:DK * (c + 1), h, q * P:(q + 1) * P],
                                        kT[DK * c:DK * (c + 1), h, b * HALF:b * HALF + nk], start=True, stop=True)
                    last.then_inc(score_full, 1)

            def attend(u):
                h, q = UNITS[u]
                pe.wait_ge(map_ready, u + 1)
                for g in range(q // 4 + 1):
                    begin(("pT", h, q, g))
                    for k in range(4 * g, min(4 * g + 4, q + 1)):
                        last = T.transpose(bank(("pT", h, q, g))[:, (k % 4) * P:(k % 4 + 1) * P],
                                           maps[:, u % 2, 0, k * P:(k + 1) * P], ident[:, :])
                    end(last)

            def values(u):
                h, q = UNITS[u]
                begin(("o", h, q))
                was_read(pe, ("pT", h, q, q // 4))
                for k in range(q + 1):
                    last = T.matmul(bank(("o", h, q))[:, 0:P], pT[:, u % 2, k, :], v[:, k, h * DV:(h + 1) * DV],
                                    start=k == 0, stop=k == q)
                end(last)

            was_read(pe, ("in", "k1", 1, 1))
            scores(0)
            for u in range(len(UNITS)):
                if u + 1 < len(UNITS):
                    scores(u + 1)
                attend(u)
                values(u)
            for h in range(HEADS):
                pe.wait_ge(o_scaled, h + 1)
                for g in range(2):
                    begin(("oT", h, g))
                    for q in range(4 * g, 4 * g + 4):
                        last = T.transpose(bank(("oT", h, g))[:, (q % 4) * P:(q % 4 + 1) * P],
                                           oT[:, h, q * P:(q + 1) * P], ident[:, :])
                    end(last)

            def mix_write(t):
                for c in range(2):
                    begin(("mix", t, c))
                    for i in (2 * c, 2 * c + 1):
                        if not t:
                            pe.wait_ge(w_loaded[i], BEFORE[i])
                        for k in range(KT):
                            src = oT[:, k, :] if k < 4 else lrx[:, k - 4, :] if k < 6 else cfb[:, k - 6, :]
                            last = T.matmul(bank(("mix", t, c))[:, (i % 2) * PIECE:(i % 2 + 1) * PIECE],
                                            src[:, t * P:(t + 1) * P], slot(i)[:, k, :], start=k == 0, stop=k == KT - 1)
                    end(last)

            def route(t):
                pe.wait_ge(h1_ready, t + 1)
                for g in range(2):
                    begin(("h1T", t, g))
                    for k in range(4 * g, 4 * g + 4):
                        last = T.transpose(bank(("h1T", t, g))[:, (k % 4) * P:(k % 4 + 1) * P],
                                           h_res[:, t, k * P:(k + 1) * P], ident[:, :])
                    end(last)
                begin(("logit", t))
                was_read(pe, ("h1T", t, 1))
                for k in range(KT):
                    last = T.matmul(bank(("logit", t))[:, 0:EXPERTS], h1T[:, k, :], router[:, k, :],
                                    start=k == 0, stop=k == KT - 1)
                end(last)

            was_read(pe, ("oT", HEADS - 1, 1))
            pe.wait_ge(cf_ready, CT)
            pe.wait_ge(lru_ready, CT)
            for t in range(TT + 1):
                if t < TT:
                    mix_write(t)
                if t:
                    route(t - 1)

            begin("rank")
            pe.wait_ge(mask_ready, 1)
            for t in range(TT + 1):
                dst = bank("rank")[:, t * EXPERTS:(t + 1) * EXPERTS]
                for s in range(t):
                    last = T.matmul(dst, ones[:, :], mask_b[:, s, :], start=s == 0, stop=t == TT and s == TT - 1)
                if t < TT:
                    last = T.matmul(dst, before[:, :], mask_b[:, t, :], start=t == 0, stop=True)
            end(last)

            def slots_write(g):
                pe.wait_ge(pick_ready, g + 1)
                for th in range(2):
                    for t in range(TT):
                        last = T.matmul(ps[:, 7, th:th + 1], pick[:, t, th * P:(th + 1) * P], token_no[:, t:t + 1],
                                        start=t == 0, stop=t == TT - 1)
                last.then_inc(slots_full, 1)

            def xT_write(g, j):
                th, kh = j // 2, j % 2
                b = (4, 5, 6, 4)[j]
                for k in range(4 * kh, 4 * kh + 4):
                    last = T.transpose(ps[:, b, (k % 4) * P:(k % 4 + 1) * P], x_rows[:, th, k * P:(k + 1) * P], ident[:, :])
                last.then_inc(xT_full, 1)

            was_read(pe, "rank")
            slots_write(0)
            for t in range(TT):
                begin(("gT", t))
                if not t:
                    pe.wait_ge(gate_m_ready, 1)
                end(T.transpose(bank(("gT", t))[0:EXPERTS, 0:P], gate_m[:, t, :], ident[:, :]))
                was_read(pe, ("gT", t))
                if not t:
                    pe.wait_ge(b2_loaded, 16)
                for c in range(2):
                    begin(("b2", t, c))
                    end(T.matmul(bank(("b2", t, c)), gate_t[:, t % 2, :], b2_rows[:, c * HALF:(c + 1) * HALF],
                                 start=True, stop=True))
            was_read(pe, ("b2", TT - 1, 1))
            pe.wait_ge(x_got, 32)
            for j in range(4):
                if j == 3:
                    pe.wait_ge(xT_read, 1)
                xT_write(0, j)

            total = pe.value_load(ends_i[0:1, EXPERTS - 1:EXPERTS], min_val=EXPERTS, max_val=MAX_BLOCKS)
            with pe.Fori(0, total) as g:
                left = pe.value_load(left_i[0:1, bass.ds(g, 1)], min_val=-BIG, max_val=BIG)
                expert = pe.value_load(expert_i[0:1, bass.ds(g, 1)], min_val=0, max_val=EXPERTS - 1)

                def body(w):
                    def piece(p):
                        pe.wait_ge(w_loaded[p], expert * 16 + (BEFORE[p] + 16))
                        if p < 4:
                            pe.wait_ge(yT_ready, g * 4 + (p + 1))
                        else:
                            pe.wait_ge(hidden_read, g * 8 + (p - 3))
                        src = xT if p < 8 else actT
                        for f in range(2):
                            for k in range(KT):
                                if p == 8 and f == 0 and k % 2 == 0:
                                    pe.wait_ge(act_ready, g * 4 + (k // 2 + 1))
                                last = T.matmul(ps[:, p % 4, f * CAP:f * CAP + w], slot(p)[:, k, f * P:(f + 1) * P],
                                                src[:, k, 0:w], start=k == 0, stop=k == KT - 1)
                        last.then_inc(piece_done, 1)

                    def rows(q):
                        b = (4, 5, 6, 5)[q]
                        pe.wait_ge(yT_ready, g * 4 + (5 + q))
                        for th in range(2 if w > P else 1):
                            m = P if th == 0 else w - P
                            for f in range(2):
                                last = T.transpose(ps[0:m, b, th * CAP + f * P:th * CAP + (f + 1) * P],
                                                   yT[:, 2 * q + f, th * P:th * P + m], ident[:, :])
                        last.then_inc(y_full, 1)

                    pe.wait_ge(xT_read, g * 4 + 4)
                    for p in range(4):
                        piece(p)
                    slots_write(g + 1)
                    for p in range(4, 8):
                        piece(p)
                    piece(8)
                    piece(9)
                    rows(0)
                    piece(10)
                    pe.wait_ge(y_read, g * 4 + 1)
                    rows(1)
                    piece(11)
                    rows(2)
                    pe.wait_ge(x_got, g * 32 + 64)
                    for j in range(4):
                        if j < 3:
                            pe.wait_ge(y_read, g * 4 + (j + 2))
                        else:
                            pe.wait_ge(xT_read, g * 4 + 5)
                        xT_write(g + 1, j)
                    pe.wait_ge(xT_read, g * 4 + 6)
                    rows(3)

                by_width(pe, left, body)


_OUT = (1, S, D)


def kernel(**inputs):
    import numpy as np
    import concourse.bacc as bacc
    from concourse.bass_utils import run_bass_kernel_spmd

    names = ["x", "ln_in_g", "ln_in_b", "w_in", "lam_q1", "lam_k1", "lam_q2", "lam_k2", "subln_g",
             "lru_conv_w", "lru_conv_b", "lru_wa", "lru_ba", "lru_wx", "lru_bx", "lru_lambda",
             "cf_conv_w", "cf_conv_b", "cf_ln_g", "cf_ln_b", "w_out", "ln1_g", "ln1_b",
             "router_w", "router_b", "moe_w1", "moe_b1", "moe_w2", "moe_b2", "ln2_g", "ln2_b"]
    nc = bacc.Bacc("TRN2", target_bir_lowering=False, num_devices=1)
    arrays, args = {}, []
    for name in names:
        a = np.ascontiguousarray(inputs[name])
        arrays[f"in_{name}"] = a
        args.append(nc.dram_tensor(f"in_{name}", a.shape, mybir.dt.from_np(a.dtype), kind="ExternalInput").ap())
    out = nc.dram_tensor("out", _OUT, F32, kind="ExternalOutput").ap()
    hybrid_layer(nc, *args, out)
    result = run_bass_kernel_spmd(nc, [arrays], core_ids=[0])
    return result.results[0]["out"]
```

```python
import math
from contextlib import ExitStack

import concourse.bass as bass
from concourse import mybir

F32 = mybir.dt.float32
F32R = mybir.dt.float32r
F16 = mybir.dt.float16
BF16 = mybir.dt.bfloat16
I32 = mybir.dt.int32
U32 = mybir.dt.uint32
ALU = mybir.AluOpType
ACT = mybir.ActivationFunctionType
AX = mybir.AxisListType

P = 128
D = 1024
S = 1024
KT = D // P
TT = S // P
HALF = 512
EPS = 1e-5
ALPHA = 2.0 ** 0.25

HEADS = 4
DK = D // 16
DV = 2 * DK
SCALE = DK ** -0.5
SLOPES = [2.0 ** (-8.0 * (h + 1) / HEADS) for h in range(HEADS)]
LAM_INIT = 0.8 - 0.6 * math.exp(0.0)
MASKED = -1.0e30

GROUP = D // 4
CT = GROUP // P
LRU_TAPS, CF_TAPS = 4, 31
LRU_C = 8.0

EXPERTS = 32
TOP_K = 4
LIMIT = 7.0
SWIGLU_ALPHA = 1.702
CAP = 256
PIECE = 256
HK = KT // 2
PIECES = 12
RAW = 3
SPLIT = 4
MAX_BLOCKS = (S * TOP_K + EXPERTS * CAP) // CAP
TABLE = MAX_BLOCKS + 1
TILES = (1, 2)
BIG = 1 << 20

IN_PIECES = ["cf_a", "cf_b", "lru_x", "lru_y", "v0", "v1", "q0", "q1", "k0", "k1"]
IN_COLUMN = {"q0": 0, "q1": 256, "k0": 512, "k1": 768, "v0": 1024, "v1": 1280,
             "lru_x": 1536, "lru_y": 1792, "cf_a": 2048, "cf_b": 2304}
FRONT_SLOTS = 4

ROW_LRU_W, ROW_LRU_B, ROW_BA, ROW_BX, ROW_LAMBDA = 0, 4, 5, 6, 7
ROW_CF_W, ROW_CF_B, ROW_CF_G, ROW_CF_BETA, CHAN_ROWS = 8, 39, 40, 41, 42


def evacuation_jobs():
    jobs = [("chan", "act"), ("dpar", "act")]
    jobs += [(("hT", 0, k), "act" if k % 2 else "dve") for k in range(KT)]
    jobs += [(("in", p, c, 0), "act") for p in ("cf_a", "cf_b") for c in range(CT)]
    jobs += [(("hT", 1, k), "act" if k % 2 else "dve") for k in range(KT)]
    jobs += [(("in", p, c, 1), "act") for p in ("cf_a", "cf_b") for c in range(CT)]
    jobs += [(("in", p, c, h), "act") for p in ("lru_x", "lru_y") for c in range(CT) for h in range(2)]
    jobs += [(("v", t), "act") for t in range(4)]
    jobs += [(("mean", h), "dve") for h in range(2)]
    jobs += [(("v", t), "act") for t in (4, 5)]
    jobs += [(("gate", 0, w, h), "act") for w in ("a", "x") for h in range(2)]
    jobs += [(("v", t), "act") for t in (6, 7)]
    jobs += [(("var", h), "act") for h in range(2)]
    jobs += [(("in", "q0", c, h), "act") for c in range(CT) for h in range(2)]
    jobs += [(("gate", 1, w, h), "act") for w in ("a", "x") for h in range(2)]
    jobs += [(("in", p, c, h), "act") for p in ("q1", "k0", "k1") for c in range(CT) for h in range(2)]
    units = [(h, q) for h in range(HEADS) for q in range(TT)]
    for h, q in units:
        jobs += [(("pT", h, q, g), "act") for g in range(q // 4 + 1)]
        jobs += [(("o", h, q), "dve")]
    jobs += [(("oT", h, g), "act") for h in range(HEADS) for g in range(2)]
    for t in range(TT + 1):
        if t < TT:
            jobs += [(("mix", t, c), "dve") for c in range(2)]
        if t:
            jobs += [(("h1T", t - 1, g), "act") for g in range(2)] + [(("logit", t - 1), "dve")]
    jobs += [("rank", "dve")]
    for t in range(TT):
        jobs += [(("gT", t), "act")] + [(("b2", t, c), "dve") for c in range(2)]
    return jobs


def hybrid_layer(nc, x, ln_in_g, ln_in_b, w_in, lam_q1, lam_k1, lam_q2, lam_k2, subln_g,
                 lru_conv_w, lru_conv_b, lru_wa, lru_ba, lru_wx, lru_bx, lru_lambda,
                 cf_conv_w, cf_conv_b, cf_ln_g, cf_ln_b, w_out, ln1_g, ln1_b,
                 router_w, router_b, moe_w1, moe_b1, moe_w2, moe_b2, ln2_g, ln2_b, out):
    JOBS = evacuation_jobs()
    NUMBER = {name: n for n, (name, _) in enumerate(JOBS)}
    ORDINAL = {}
    for engine in ("act", "dve"):
        for n, name in enumerate(name for name, by in JOBS if by == engine):
            ORDINAL[name] = n
    READER = dict(JOBS)
    UNITS = [(h, q) for h in range(HEADS) for q in range(TT)]

    h1_rows = nc.dram_tensor("h1_rows", [S, D], F32).ap()
    b1_parts = nc.dram_tensor("b1_parts", [EXPERTS, 2, 2 * D], F32).ap()
    y_rows = nc.dram_tensor("y_rows", [S * TOP_K + CAP, D], F32).ap()

    x_tiles = x[0].rearrange("(t p) d -> p t d", p=P)
    out_tiles = out[0].rearrange("(t p) d -> p t d", p=P)
    h1_tiles = h1_rows.rearrange("(t p) d -> p t d", p=P)
    w_in_v = w_in[0].rearrange("(k p) n -> p k n", p=P)
    w_out_v = w_out[0].rearrange("(k p) n -> p k n", p=P)
    w1_v = moe_w1[0].rearrange("e (k p) n -> e p k n", p=P)
    w2_v = moe_w2[0].rearrange("e (k p) n -> e p k n", p=P)

    ctx = ExitStack()
    with ctx:
        at = {}

        def sb(name, shape, dt=F32):
            tensor = ctx.enter_context(nc.sbuf_tensor(name, shape, dt))
            at[name] = nc.sbuf_base - 4 * math.prod(shape[1:])
            return tensor

        def sem(name):
            return ctx.enter_context(nc.semaphore(name))

        ring = sb("ring", [P, PIECES, KT * PIECE])
        h_res = sb("h_res", [P, TT, D])
        big = sb("big", [P, KT, S])
        scr = sb("scr", [P, 4, S])
        cfb = sb("cfb", [P, CT, S])
        lrx = sb("lrx", [P, CT, S])

        def slot(s):
            return ring[:, s, :].rearrange("p (k n) -> p k n", k=KT)

        x_in = ring[:, 6:10, :].rearrange("p s (t d) -> p (s t) d", d=D)
        b1_rows = ring[0:EXPERTS, 10, :]
        chan_rows = ring[0:CHAN_ROWS, 11, 0:GROUP]
        dpar_rows = ring[0:2 * KT + 1, 11, GROUP:GROUP + P]
        lam_in = ring[:, 11, HALF:HALF + 4 * DK].rearrange("p (a n) -> p a n", a=4)
        qT = ring[:, 6:8, :].rearrange("p s (h t) -> p (s h) t", h=2)
        kT = ring[:, 8:10, :].rearrange("p s (h t) -> p (s h) t", h=2)
        v = ring[:, 10:12, :].rearrange("p s (t n) -> p (s t) n", n=HALF)
        lry = ring[:, 4, :].rearrange("p (i s) -> p i s", i=CT)
        cfa = ring[:, 5, :].rearrange("p (i s) -> p i s", i=CT)
        pT = ring[:, 5, :].rearrange("p (b k q) -> p b k q", b=2, k=TT)
        hT = big
        oT = big[:, 0:HEADS, :]
        maps = big[:, HEADS:, :].rearrange("p (b c) s -> p b c s", b=2)
        norm_rows = scr[:, 0:2, :]
        xc, ga, gx, mul = (scr[:, i, :] for i in range(4))
        alibi = scr[:, 2, :]
        h1T = big[:, 4, :].rearrange("p (k q) -> p k q", k=KT)
        one_hot = big[:, 5, :].rearrange("p (k t e) -> p k t e", k=TOP_K, e=EXPERTS)
        cmp = big[:, 6:8, :].rearrange("p a s -> p (a s)")[:, 0:TABLE * EXPERTS]\
            .rearrange("p (g e) -> p g e", e=EXPERTS)
        b2_rows = scr[0:EXPERTS, 3, :]
        by_expert = big[:, 4, :].rearrange("p (a t e) -> p a t e", a=4, e=EXPERTS)
        mask, gate_m, rows_at = by_expert[:, 0], by_expert[:, 1], by_expert[:, 2]
        gate_t = big[0:EXPERTS, 3, 0:2 * P].rearrange("p (a n) -> p a n", a=2)
        mask_b = big[:, 4, 3 * TT * EXPERTS:].bitcast(BF16)[:, 0:TT * EXPERTS].rearrange("p (t e) -> p t e", e=EXPERTS)
        def alias(name, base, base_name, first, shape):
            row = 4 * math.prod(base.shape[2:])
            return nc.alloc_sbuf_tensor_at(name, shape, F32R, offset=at[base_name] + first * row)

        high = alias("high", ring, "ring", 4, [P, SPLIT, HK, HALF])
        low = alias("low", ring, "ring", 8, [P, SPLIT, HK, HALF])
        xT_high, xT_low, act_high, act_low = (
            alias(name, big, "big", 2 * i, [P, KT, CAP]) for i, name in enumerate(("xT_high", "xT_low", "act_high", "act_low")))
        b1_now = alias("b1_now", cfb, "cfb", 0, [P, 2 * D])
        raw = ring[:, 0:RAW, :].rearrange("p s (k n) -> p s k n", k=HK)
        b1_split = [low[0:EXPERTS, i].rearrange("p k n -> p (k n)") for i in range(2)]
        x_rows = ring[:, RAW, :].rearrange("p (t d) -> p t d", d=D)
        y_out = lrx
        glu = scr[:, 0, :].rearrange("p (t n) -> p t n", t=2)
        sig = scr[:, 1, :].rearrange("p (t n) -> p t n", t=2)
        lin = scr[:, 3, :].rearrange("p (t n) -> p t n", t=2)
        pick = scr[:, 2, :].bitcast(F16).rearrange("p (t s) -> p t s", t=TT)
        y_got = big[:, :, :].rearrange("p (b k) s -> p b k s", b=2)

        ident = sb("ident", [P, P])
        eps_t = sb("eps_t", [P, 1])
        pad = sb("pad", [P, 16])
        chan_mean = sb("chan_mean", [P, P])
        before = sb("before", [P, P], BF16)
        ones = sb("ones", [P, P], BF16)
        chan = sb("chan", [P, CT, CHAN_ROWS])
        dpar = sb("dpar", [P, 2 * KT + 1])
        ones_r = sb("ones_r", [P, P], F32R)
        gate_w = sb("gate_w", [P, 2, CT, P])
        router = sb("router", [P, KT, EXPERTS])
        router_bias = sb("router_bias", [P, EXPERTS])
        lam_s = sb("lam_s", [P, 8])
        soft = sb("soft", [P, 6, CT])
        decay = sb("decay", [P, 2, CT])
        gain_o = sb("gain_o", [P, 1])
        stats = sb("stats", [P, 2, 12])
        mv = sb("mv", [P, TT, 2])
        std = sb("std", [P, TT])
        inv = sb("inv", [P, TT])
        shift = sb("shift", [P, TT])
        top = sb("top", [P, 2, 2])
        ntop = sb("ntop", [P, 2, 2])
        mass = sb("mass", [P, 2, 2])
        rmass = sb("rmass", [P, 2, 2])
        coef = sb("coef", [P, 2, 1])
        o_sq = sb("o_sq", [P, HEADS * TT])
        o_std = sb("o_std", [P, HEADS * TT])
        o_inv = sb("o_inv", [P, HEADS * TT])
        sq_out = sb("sq_out", [P, P])
        logits = sb("logits", [P, TT, EXPERTS])
        best = sb("best", [P, TT, 8])
        best_at = sb("best_at", [P, TT, 8], U32)
        chosen = sb("chosen", [P, TT, TOP_K])
        gates = sb("gates", [P, TT, TOP_K])
        gsum = sb("gsum", [P, TT])
        rank_of = sb("rank_of", [P, EXPERTS, TT])
        rank_now = sb("rank_now", [P, TT])
        count = sb("count", [P, EXPERTS])
        blocks = sb("blocks", [P, EXPERTS])
        ends = sb("ends", [P, EXPERTS])
        starts = sb("starts", [P, EXPERTS])
        dest = sb("dest", [P, TT, TOP_K])
        dest_i = sb("dest_i", [P, TT, TOP_K], I32)
        expert_f = sb("expert_f", [P, TABLE])
        offset_f = sb("offset_f", [P, TABLE])
        left_f = sb("left_f", [P, TABLE])
        expert_i = sb("expert_i", [1, TABLE], I32)
        left_i = sb("left_i", [1, TABLE], I32)
        row_f = sb("row_f", [P, 2, TABLE])
        row_i = sb("row_i", [1, TABLE], I32)
        ones_t = sb("ones_t", [P, TABLE])
        first = sb("first", [P, EXPERTS])
        ends_i = sb("ends_i", [1, EXPERTS], I32)
        token_no = sb("token_no", [P, TT], F16)
        iota_e = sb("iota_e", [P, EXPERTS])
        iota_g = sb("iota_g", [P, TABLE])
        iota_s = sb("iota_s", [P, CAP], F16)
        token_at = sb("token_at", [P, 2], I32)

        ps = ctx.enter_context(nc.psum_tensor("ps", [P, 8, HALF], F32))

        def bank(name):
            return ps[:, 4 + NUMBER[name] % 4, :]

        x_loaded = [sem(f"x_loaded{i}") for i in range(4)]
        params_loaded = sem("params_loaded")
        gate_w_loaded = sem("gate_w_loaded")
        gather_go = sem("gather_go")
        w_loaded = [sem(f"w_loaded{i}") for i in range(FRONT_SLOTS)]
        raw_loaded = [sem(f"raw_loaded{i}") for i in range(RAW)]
        norm_loaded = [sem(f"norm_loaded{i}") for i in range(3)]
        b2_loaded = sem("b2_loaded")
        const_ready = sem("const_ready")
        pool_step = sem("pool_step")
        dve_step = sem("dve_step")
        act_step = sem("act_step")
        job_full = sem("job_full")
        read_by = {"act": sem("read_by_act"), "dve": sem("read_by_dve")}
        eps_ready = sem("eps_ready")
        mean_ready = sem("mean_ready")
        std_ready = sem("std_ready")
        norm_ready = sem("norm_ready")
        normed = sem("normed")
        h_rows_ready = sem("h_rows_ready")
        glu_cf = sem("glu_cf")
        conv_out = sem("conv_out")
        squared = sem("squared")
        cf_scaled = sem("cf_scaled")
        cf_ready = sem("cf_ready")
        xc_ready = sem("xc_ready")
        decays = sem("decays")
        one_minus = sem("one_minus")
        root = sem("root")
        lru_ready = sem("lru_ready")
        decay_ready = sem("decay_ready")
        soft_s = sem("soft_s")
        lam_s1 = sem("lam_s1")
        alibi_ready = sem("alibi_ready")
        score_full = sem("score_full")
        score_read = sem("score_read")
        top_ready = sem("top_ready")
        exp_ready = sem("exp_ready")
        map_ready = sem("map_ready")
        o_ready = sem("o_ready")
        o_root = sem("o_root")
        o_scaled = sem("o_scaled")
        mix_mean = sem("mix_mean")
        mix_std = sem("mix_std")
        mix_norm = sem("mix_norm")
        mix_normed = sem("mix_normed")
        h1_gain = sem("h1_gain")
        h1_ready = sem("h1_ready")
        h1_stored = sem("h1_stored")
        gate_diff = sem("gate_diff")
        gate_exp = sem("gate_exp")
        mask_ready = sem("mask_ready")
        gate_m_ready = sem("gate_m_ready")
        tables_ready = sem("tables_ready")
        resid_ready = sem("resid_ready")
        pick_ready = sem("pick_ready")
        slots_full = sem("slots_full")
        slots_ready = sem("slots_ready")
        x_got = sem("x_got")
        xT_full = sem("xT_full")
        xT_read = sem("xT_read")
        high_ready = sem("high_ready")
        low_by_dve = sem("low_by_dve")
        low_by_pool = sem("low_by_pool")
        xT_high_ready = sem("xT_high_ready")
        act_rows = sem("act_rows")
        aT_full = sem("aT_full")
        aT_high_ready = sem("aT_high_ready")
        aT_read = sem("aT_read")
        piece_done = sem("piece_done")
        hidden_read = sem("hidden_read")
        sig_ready = sem("sig_ready")
        swish_step = sem("swish_step")
        y_read = sem("y_read")
        y_stored = sem("y_stored")
        rank_step = sem("rank_step")
        b1_high = sem("b1_high")
        b1_low = sem("b1_low")
        b1_stored = sem("b1_stored")
        b1_loaded = sem("b1_loaded")
        ones_r_ready = sem("ones_r_ready")
        got = [sem(f"got{i}") for i in range(8)]
        summed = sem("summed")
        fin_std = sem("fin_std")
        fin_norm = sem("fin_norm")
        fin_normed = sem("fin_normed")
        fin_gain = sem("fin_gain")
        out_ready = sem("out_ready")
        out_stored = sem("out_stored")

        def by_tiles(eng, left, body):
            with eng.If(left < P + 1):
                body(TILES[0])
            with eng.Else():
                body(TILES[1])

        LAST_USE = {p: ("v", TT - 1) if p[0] == "v" else ("in", p, CT - 1, 1) for p in IN_PIECES}
        USES = [sum(n % FRONT_SLOTS == i for n in range(len(IN_PIECES))) for i in range(FRONT_SLOTS)]
        BEFORE = [16 * (uses + 1) for uses in USES]
        PARAM_LOADS = 16 * 19

        def by_pool(n):
            return n % RAW == RAW - 1

        def raw_count(g, n):
            return g * (16 * PIECES // RAW) + 16 * (n // RAW + 1)

        def high_count(g, n):
            return g * PIECES + (n + 1)

        def wait_low(eng, g, n):
            if by_pool(n):
                eng.wait_ge(low_by_pool, g * (PIECES // RAW) + (n // RAW + 1))
            else:
                eng.wait_ge(low_by_dve, g * (2 * PIECES // RAW) + (2 * (n // RAW) + n % RAW + 1))

        def split_low(eng, ops, g, n):
            eng.wait_ge(high_ready, high_count(g, n))
            ops.tensor_tensor(low[:, n % SPLIT], raw[:, n % RAW], high[:, n % SPLIT].bitcast(F32),
                              ALU.subtract).then_inc(low_by_pool if by_pool(n) else low_by_dve, 1)

        block = ctx.enter_context(nc.Block())

        def full(eng, name):
            eng.wait_ge(job_full, NUMBER[name] + 1)

        def was_read(eng, name):
            eng.wait_ge(read_by[READER[name]], ORDINAL[name] + 1)


        @block.sync
        def _(sp):
            def w_in_piece(i):
                name = IN_PIECES[i]
                if i >= FRONT_SLOTS:
                    full(sp, LAST_USE[IN_PIECES[i - FRONT_SLOTS]])
                c = IN_COLUMN[name]
                sp.dma_start(slot(i % FRONT_SLOTS), w_in_v[:, :, c:c + PIECE]).then_inc(w_loaded[i % FRONT_SLOTS], 16)

            for i in range(4):
                sp.dma_start(x_in[:, 2 * i:2 * i + 2, :], x_tiles[:, 2 * i:2 * i + 2, :]).then_inc(x_loaded[i], 16)
            for i in range(len(IN_PIECES)):
                w_in_piece(i)
                if i == 1:
                    sp.dma_start(norm_rows[:, 0, :], ln_in_g.partition_broadcast(P)).then_inc(norm_loaded[0], 16)
                    sp.dma_start(norm_rows[:, 1, :], ln_in_b.partition_broadcast(P)).then_inc(norm_loaded[0], 16)
            for i in range(4):
                last = max(n for n in range(len(IN_PIECES)) if n % FRONT_SLOTS == i)
                full(sp, LAST_USE[IN_PIECES[last]])
                sp.dma_start(slot(i), w_out_v[:, :, i * PIECE:(i + 1) * PIECE]).then_inc(w_loaded[i], 16)
            full(sp, ("o",) + UNITS[-1])
            sp.wait_ge(score_read, 2 * len(UNITS))
            sp.dma_start(norm_rows[:, 0, :], ln1_g[0].partition_broadcast(P)).then_inc(norm_loaded[1], 16)
            sp.dma_start(norm_rows[:, 1, :], ln1_b[0].partition_broadcast(P)).then_inc(norm_loaded[1], 16)
            sp.dma_start(b2_rows, moe_b2[0]).then_inc(b2_loaded, 16)

            def expert_piece(e, n):
                p = n % PIECES
                if p < 8:
                    c, kh = (p // 2 % 2) * D + (p // 4) * HALF, p % 2
                    src = w1_v[e, :, HK * kh:HK * (kh + 1), c:c + HALF]
                else:
                    c, kh = (p % 2) * HALF, (p - 8) // 2
                    src = w2_v[e, :, HK * kh:HK * (kh + 1), c:c + HALF]
                if not isinstance(e, int):
                    src = src.rearrange("a p k n -> (a p) k n")
                sp.dma_start(raw[:, n % RAW], src).then_inc(raw_loaded[n % RAW], 16)

            for t in range(TT):
                sp.wait_ge(h1_ready, t + 1)
                sp.dma_start(h1_tiles[:, t, :], h_res[:, t, :]).then_inc(h1_stored, 16)
            full(sp, ("mix", TT - 1, 1))
            for n in range(RAW):
                expert_piece(0, n)
            sp.wait_ge(tables_ready, 1)
            total = sp.value_load(ends_i[0:1, EXPERTS - 1:EXPERTS], min_val=EXPERTS, max_val=MAX_BLOCKS)
            with sp.Fori(0, total) as g:
                now = sp.value_load(expert_i[0:1, bass.ds(g, 1)], min_val=0, max_val=EXPERTS - 1)
                after = sp.value_load(expert_i[0:1, bass.ds(g + 1, 1)], min_val=0, max_val=EXPERTS - 1)
                for n in range(RAW, RAW + PIECES):
                    wait_low(sp, g, n - RAW)
                    expert_piece(bass.ds(now if n < PIECES else after, 1), n)
            wait_low(sp, total, 0)
            expert_piece(0, RAW)
            sp.wait_ge(y_stored, total * 32 + 32)
            sp.dma_start(norm_rows[:, 0, :], ln2_g[0].partition_broadcast(P)).then_inc(norm_loaded[2], 16)
            sp.dma_start(norm_rows[:, 1, :], ln2_b[0].partition_broadcast(P)).then_inc(norm_loaded[2], 16)
            for t in range(TT):
                sp.wait_ge(out_ready, t + 1)
                sp.dma_start(out_tiles[:, t, :], h_res[:, t, :]).then_inc(out_stored, 16)
            sp.wait_ge(out_stored, 16 * TT)
            sp.wait_ge(h1_stored, 16 * TT)

        @block.gpsimd
        def _(pool):
            n = [0]

            def step(ins):
                n[0] += 1
                ins.then_inc(pool_step, 1)
                pool.wait_ge(pool_step, n[0])

            step(nc.gpsimd.memset(ident[:, :], 0.0))
            nc.gpsimd.affine_select(out=ident[:, :], in_=ident[:, :], compare_op=ALU.not_equal, fill=1.0,
                                    base=0, pattern=[[-1, P]], channel_multiplier=1).then_inc(const_ready, 1)
            step(nc.gpsimd.memset(gate_w[:, :, :, :], 0.0))
            for w, src in enumerate((lru_wa, lru_wx)):
                for i in range(CT):
                    for b in range(2):
                        pool.dma_start(gate_w[64 * b:64 * b + 64, w, i, 64 * b:64 * b + 64],
                                       src[0, 2 * i + b]).then_inc(gate_w_loaded, 16)
            nc.gpsimd.memset(chan_mean[:, :], 1.0 / GROUP)
            nc.gpsimd.memset(ones_t[:, :], 1.0)
            step(nc.gpsimd.memset(ones[:, :], 1.0))
            nc.gpsimd.affine_select(out=before[:, :], in_=ones[:, :], compare_op=ALU.is_gt, fill=0.0,
                                    base=0, pattern=[[1, P]], channel_multiplier=-1)
            nc.gpsimd.iota(iota_e[:, :], pattern=[[1, EXPERTS]], base=0, channel_multiplier=0,
                           allow_small_or_imprecise_dtypes=True)
            nc.gpsimd.iota(iota_g[:, :], pattern=[[1, TABLE]], base=0, channel_multiplier=0,
                           allow_small_or_imprecise_dtypes=True)
            nc.gpsimd.iota(iota_s[:, :], pattern=[[1, CAP]], base=0, channel_multiplier=0,
                           allow_small_or_imprecise_dtypes=True)
            nc.gpsimd.iota(token_no[:, :], pattern=[[P, TT]], base=0, channel_multiplier=1,
                           allow_small_or_imprecise_dtypes=True).then_inc(const_ready, 1)

            pool.wait_ge(b1_high, 1)
            nc.gpsimd.tensor_tensor(b1_split[1], b1_rows, b1_split[0].bitcast(F32), ALU.subtract).then_inc(b1_low, 1)

            pool.wait_ge(norm_loaded[0], 32)
            full(pool, ("hT", 1, KT - 1))
            for t in range(TT):
                step(nc.gpsimd.tensor_tensor(h_res[:, t, :], h_res[:, t, :], norm_rows[:, 0, :], ALU.mult))
                nc.gpsimd.tensor_tensor(h_res[:, t, :], h_res[:, t, :], norm_rows[:, 1, :],
                                        ALU.add).then_inc(h_rows_ready, 1)

            pool.wait_ge(lru_ready, 2)
            step(nc.gpsimd.iota(alibi, pattern=[[1, S]], base=-(S - P), channel_multiplier=-1,
                                allow_small_or_imprecise_dtypes=True))
            step(nc.gpsimd.affine_select(out=alibi, in_=alibi, compare_op=ALU.is_ge, fill=MASKED,
                                         base=S - P, pattern=[[-1, S]], channel_multiplier=1))
            for h in range(HEADS):
                if h >= 2:
                    pool.wait_ge(score_read, 2 * TT * (h - 1))
                nc.gpsimd.tensor_scalar(scr[:, h % 2, :], alibi, SLOPES[h] / SCALE, None,
                                        ALU.mult).then_inc(alibi_ready, 1)

            def held():
                pool.sem_inc(gather_go, 1)

            def gather(g):
                for th in range(2):
                    pool.indirect_dma_start(
                        out=x_rows[:, th, :], out_offset=None, in_=h1_rows[:, :],
                        in_offset=bass.IndirectOffsetOnAxis(ap=token_at[:, th:th + 1], axis=0)
                    ).then_inc(x_got, 16)

            pool.wait_ge(h1_stored, 16 * TT)
            full(pool, ("mix", TT - 1, 1))
            split_low(pool, nc.gpsimd, 0, 2)
            pool.wait_ge(b1_stored, 32)
            pool.dma_start(b1_now[0:2, :], b1_parts[0, :, :]).then_inc(b1_loaded, 16)
            pool.wait_ge(slots_ready, 1)
            gather(0)
            pool.wait_ge(tables_ready, 1)
            total = pool.value_load(ends_i[0:1, EXPERTS - 1:EXPERTS], min_val=EXPERTS, max_val=MAX_BLOCKS)
            with pool.Fori(0, total) as g:
                split_low(pool, nc.gpsimd, g, 5)
                pool.wait_ge(xT_full, g * 2 + 2)
                pool.wait_ge(slots_ready, g + 2)
                held()
                gather(g + 1)
                split_low(pool, nc.gpsimd, g, 8)
                split_low(pool, nc.gpsimd, g, 11)
                after = pool.value_load(expert_i[0:1, bass.ds(g + 1, 1)], min_val=0, max_val=EXPERTS - 1)
                pool.wait_ge(piece_done, g * PIECES + 7)
                held()
                pool.dma_start(b1_now[0:2, :], b1_parts[bass.ds(after, 1), :, :].rearrange("a r n -> (a r) n"))\
                    .then_inc(b1_loaded, 16)
                split_low(pool, nc.gpsimd, g, 14)

            pool.wait_ge(xT_read, total * 2 + 2)
            pool.wait_ge(x_got, total * 32 + 32)
            pool.wait_ge(b1_loaded, total * 16 + 16)
            pool.wait_ge(y_stored, total * 32 + 32)
            held()
            for t in range(TT):
                if t >= 2:
                    pool.wait_ge(summed, t - 1)
                for k in range(TOP_K):
                    pool.indirect_dma_start(
                        out=y_got[:, t % 2, k, :], out_offset=None, in_=y_rows[0:S * TOP_K, :],
                        in_offset=bass.IndirectOffsetOnAxis(ap=dest_i[:, t, k:k + 1], axis=0)
                    ).then_inc(got[4 * (t % 2) + k], 16)

        @block.scalar
        def _(act):
            n = [0]

            def step(ins):
                n[0] += 1
                ins.then_inc(act_step, 1)
                act.wait_ge(act_step, n[0])

            loads = [
                (chan_rows[ROW_LRU_W:ROW_LRU_W + LRU_TAPS, :], lru_conv_w[0]), (chan_rows[ROW_LRU_B:ROW_LRU_B + 1, :], lru_conv_b),
                (chan_rows[ROW_BA:ROW_BA + 1, :], lru_ba), (chan_rows[ROW_BX:ROW_BX + 1, :], lru_bx),
                (chan_rows[ROW_LAMBDA:ROW_LAMBDA + 1, :], lru_lambda),
                (chan_rows[ROW_CF_W:ROW_CF_W + CF_TAPS, :], cf_conv_w[0]), (chan_rows[ROW_CF_B:ROW_CF_B + 1, :], cf_conv_b),
                (chan_rows[ROW_CF_G:ROW_CF_G + 1, :], cf_ln_g), (chan_rows[ROW_CF_BETA:ROW_CF_BETA + 1, :], cf_ln_b),
                (dpar_rows[0:KT, :], ln_in_g.rearrange("(k p) -> k p", p=P)),
                (dpar_rows[KT:2 * KT, :], ln_in_b.rearrange("(k p) -> k p", p=P)),
                (dpar_rows[2 * KT:2 * KT + 1, :], subln_g), (b1_rows, moe_b1[0]),
                (router[:, :, :], router_w[0].rearrange("(k p) e -> p k e", p=P)),
                (router_bias[:, :], router_b[0].partition_broadcast(P)),
            ] + [(lam_in[:, i, :], a[0].partition_broadcast(P)) for i, a in enumerate((lam_q1, lam_k1, lam_q2, lam_k2))]
            for dst, src in loads:
                act.dma_start(dst, src).then_inc(params_loaded, 16)

            def finish(ins, name):
                ins.then_inc(read_by["act"], 1)

            act.wait_ge(eps_ready, 1)
            for hf in range(2):
                act.wait_ge(mean_ready, hf + 1)
                nc.scalar.activation(std[:, 4 * hf:4 * hf + 4], mv[:, 4 * hf:4 * hf + 4, 1], ACT.Sqrt,
                                     bias=eps_t[:, 0:1]).then_inc(std_ready, 1)
                act.wait_ge(norm_ready, hf + 1)
                for t in range(4 * hf, 4 * hf + 4):
                    nc.scalar.activation(h_res[:, t, :], x_in[:, t, :], ACT.Identity, bias=shift[:, t:t + 1],
                                         scale=inv[:, t:t + 1]).then_inc(normed, 1)

            full(act, "chan")
            finish(nc.scalar.copy(chan[:, :, :], bank("chan")[:, 0:CT * CHAN_ROWS].rearrange("p (i r) -> p i r", i=CT)), "chan")
            full(act, "dpar")
            finish(nc.scalar.copy(dpar[:, :], bank("dpar")[:, 0:2 * KT + 1]), "dpar")
            act.wait_ge(read_by["act"], ORDINAL["dpar"] + 1)
            step(nc.scalar.mul(gain_o[:, :], dpar[:, 2 * KT:2 * KT + 1], 1.0 - LAM_INIT))

            def hT_read(hf, k):
                full(act, ("hT", hf, k))
                finish(nc.scalar.activation(hT[:, k, hf * HALF:(hf + 1) * HALF], bank(("hT", hf, k)), ACT.Identity,
                                            bias=dpar[:, KT + k:KT + k + 1], scale=dpar[:, k:k + 1]), None)

            lam_c = chan[:, :, ROW_LAMBDA]
            act.wait_ge(soft_s, 1)
            nc.scalar.activation(soft[:, 1, :], soft[:, 0, :], ACT.Exp).then_inc(soft_s, 1)
            act.wait_ge(soft_s, 3)
            nc.scalar.activation(soft[:, 3, :], soft[:, 2, :], ACT.Ln).then_inc(soft_s, 1)
            act.wait_ge(lam_s1, 1)
            nc.scalar.activation(lam_s[:, 2:4], lam_s[:, 0:2], ACT.Exp).then_inc(lam_s1, 1)

            for k in range(1, KT, 2):
                hT_read(0, k)
            nc.scalar.copy(b1_split[0], b1_rows).then_inc(b1_high, 1)
            act.wait_ge(const_ready, 2)
            nc.scalar.copy(ones_r[0:2, :], ones[0:2, :]).then_inc(ones_r_ready, 1)

            def in_read(p, c, h):
                name = ("in", p, c, h)
                cols = slice(h * HALF, (h + 1) * HALF)
                full(act, name)
                if p == "cf_a":
                    finish(nc.scalar.copy(cfa[:, c, cols], bank(name)), name)
                elif p == "cf_b":
                    finish(nc.scalar.activation(cfb[:, c, cols], bank(name), ACT.Sigmoid), name)
                elif p == "lru_x":
                    finish(nc.scalar.copy(lrx[:, c, cols], bank(name)), name)
                elif p == "lru_y":
                    finish(nc.scalar.activation(lry[:, c, cols], bank(name), ACT.Gelu_apprx_tanh), name)
                else:
                    dst = qT if p[0] == "q" else kT
                    if (p, c, h) == ("k0", 0, 0):
                        act.wait_ge(b1_stored, 32)
                    finish(nc.scalar.copy(dst[:, 2 * int(p[1]) + c, cols], bank(name)), name)

            def v_read(t):
                full(act, ("v", t))
                finish(nc.scalar.copy(v[:, t, :], bank(("v", t))), None)

            def gate_read(i):
                for w, dst, row in (("a", ga, ROW_BA), ("x", gx, ROW_BX)):
                    for h in range(2):
                        full(act, ("gate", i, w, h))
                        if i and w == "a" and not h:
                            act.wait_ge(lru_ready, i)
                        finish(nc.scalar.activation(dst[:, h * HALF:(h + 1) * HALF], bank(("gate", i, w, h)),
                                                    ACT.Sigmoid, bias=chan[:, i, row:row + 1]), None)
                act.wait_ge(read_by["act"], ORDINAL[("gate", i, "x", 1)] + 1)
                if not i:
                    act.wait_ge(decay_ready, 1)
                step(nc.scalar.activation(mul, ga, ACT.Exp, scale=decay[:, 1, i:i + 1]))
                nc.scalar.activation(ga, ga, ACT.Exp, scale=decay[:, 0, i:i + 1]).then_inc(decays, 1)
                act.wait_ge(one_minus, i + 1)
                nc.scalar.activation(mul, mul, ACT.Sqrt).then_inc(root, 1)

            for p in ("cf_a", "cf_b"):
                for c in range(CT):
                    in_read(p, c, 0)
            for k in range(1, KT, 2):
                hT_read(1, k)
            for p in ("cf_a", "cf_b"):
                for c in range(CT):
                    in_read(p, c, 1)
            for p in ("lru_x", "lru_y"):
                for c in range(CT):
                    for h in range(2):
                        in_read(p, c, h)
            act.wait_ge(b1_low, 1)
            for i in range(2):
                act.dma_start(b1_parts[:, i, :], b1_split[i].bitcast(F32)).then_inc(b1_stored, 16)
            for t in range(6):
                v_read(t)
            gate_read(0)
            for h in range(2):
                was_read(act, ("mean", h))
                nc.scalar.activation(cfa[:, :, h * HALF:(h + 1) * HALF], cfb[:, :, h * HALF:(h + 1) * HALF],
                                     ACT.Square).then_inc(squared, 1)
            v_read(6)
            v_read(7)
            for h in range(2):
                if not h:
                    full(act, ("var", 1))
                finish(nc.scalar.activation(cfa[:, 0, h * HALF:(h + 1) * HALF], bank(("var", h)), ACT.Sqrt,
                                            bias=eps_t[:, 0:1]), None)
            for c in range(CT):
                for h in range(2):
                    in_read("q0", c, h)
            gate_read(1)
            act.wait_ge(cf_scaled, 1)
            for i in range(CT):
                nc.scalar.activation(cfb[:, i, :], cfb[:, i, :], ACT.Silu, bias=chan[:, i, ROW_CF_BETA:ROW_CF_BETA + 1],
                                     scale=chan[:, i, ROW_CF_G:ROW_CF_G + 1]).then_inc(cf_ready, 1)
            for p in ("q1", "k0", "k1"):
                for c in range(CT):
                    for h in range(2):
                        in_read(p, c, h)

            def exps(u):
                h, q = UNITS[u]
                act.wait_ge(top_ready, u + 1)
                for c in range(2):
                    m = maps[:, u % 2, c, 0:(q + 1) * P]
                    nc.scalar.activation(m, m, ACT.Exp, bias=ntop[:, u % 2, c:c + 1], scale=SCALE,
                                         accum_out=mass[:, u % 2, c:c + 1]).then_inc(exp_ready, 1)

            def map_read(u):
                h, q = UNITS[u]
                for g in range(q // 4 + 1):
                    k = min(4, q + 1 - 4 * g)
                    full(act, ("pT", h, q, g))
                    finish(nc.scalar.copy(pT[:, u % 2, 4 * g:4 * g + k, :],
                                          bank(("pT", h, q, g))[:, 0:k * P].rearrange("p (k q) -> p k q", q=P)), None)

            for u in range(len(UNITS)):
                exps(u)
                if u:
                    map_read(u - 1)
            map_read(len(UNITS) - 1)
            act.wait_ge(o_ready, HEADS * TT)
            nc.scalar.activation(o_std[:, :], o_sq[:, :], ACT.Sqrt, bias=eps_t[:, 0:1], scale=1.0 / DV).then_inc(o_root, 1)
            for h in range(HEADS):
                for g in range(2):
                    full(act, ("oT", h, g))
                    finish(nc.scalar.activation(oT[:, h, g * HALF:(g + 1) * HALF], bank(("oT", h, g)), ACT.Copy,
                                                scale=gain_o[:, 0:1]), None)

            def h1T_read(t):
                for g in range(2):
                    full(act, ("h1T", t, g))
                    finish(nc.scalar.copy(h1T[:, 4 * g:4 * g + 4, :],
                                          bank(("h1T", t, g)).rearrange("p (k q) -> p k q", q=P)), None)

            for t in range(TT):
                act.wait_ge(mix_mean, t + 1)
                nc.scalar.activation(std[:, t:t + 1], mv[:, t, 1:2], ACT.Sqrt, bias=eps_t[:, 0:1]).then_inc(mix_std, 1)
                act.wait_ge(mix_norm, t + 1)
                nc.scalar.activation(h_res[:, t, :], h_res[:, t, :], ACT.Identity, bias=shift[:, t:t + 1],
                                     scale=inv[:, t:t + 1]).then_inc(mix_normed, 1)
                if t:
                    h1T_read(t - 1)
            h1T_read(TT - 1)

            def split_high(g, n):
                act.wait_ge(raw_loaded[n % RAW], raw_count(g, n))
                if n >= SPLIT:
                    act.wait_ge(piece_done, g * PIECES + (n - SPLIT + 1))
                nc.scalar.copy(high[:, n % SPLIT], raw[:, n % RAW]).then_inc(high_ready, 1)

            def xT_read_high(g, th):
                act.wait_ge(xT_full, g * 2 + (th + 1))
                nc.scalar.copy(xT_high[:, :, th * P:(th + 1) * P],
                               ps[:, 4 + 2 * th:6 + 2 * th, :].rearrange("p b (k n) -> p (b k) n", n=P))\
                    .then_inc(xT_high_ready, 1)

            for n in range(RAW):
                split_high(0, n)
            act.wait_ge(gate_diff, 1)
            nc.scalar.activation(gates[:, :, :], gates[:, :, :], ACT.Exp).then_inc(gate_exp, 1)
            for t in range(TT):
                full(act, ("gT", t))
                finish(nc.scalar.copy(gate_t[:, t % 2, :], bank(("gT", t))[0:EXPERTS, 0:P]), None)

            nc.scalar.copy(pad[:, 3:4], eps_t[:, :]).then_inc(y_read, 2)
            nc.scalar.copy(pad[:, 4:5], eps_t[:, :]).then_inc(y_stored, 32)
            split_high(0, RAW)
            for th in range(2):
                xT_read_high(0, th)
            act.wait_ge(tables_ready, 1)
            total = act.value_load(ends_i[0:1, EXPERTS - 1:EXPERTS], min_val=EXPERTS, max_val=MAX_BLOCKS)
            with act.Fori(0, total) as g:
                left = act.value_load(left_i[0:1, bass.ds(g, 1)], min_val=-BIG, max_val=BIG)
                row = act.value_load(row_i[0:1, bass.ds(g, 1)], min_val=0, max_val=S * TOP_K)

                def body(tiles):
                    def sigmoid(c):
                        act.wait_ge(hidden_read, g * 4 + (2 * c + 1))
                        if c:
                            act.wait_ge(act_rows, g * 2 + c)
                        nc.scalar.activation(sig[:, 0:tiles, :], glu[:, 0:tiles, :], ACT.Sigmoid,
                                             scale=SWIGLU_ALPHA).then_inc(sig_ready, 1)

                    def aT_read_high(c):
                        act.wait_ge(aT_full, g * 2 + (c + 1))
                        dst = act_high[:, HK * c:HK * (c + 1), 0:tiles * P].rearrange("p k (t n) -> p t k n", n=P)
                        src = ps[:, 4 + 2 * c:4 + 2 * c + tiles, :].rearrange("p t (k n) -> p t k n", n=P)
                        nc.scalar.copy(dst, src).then_inc(aT_high_ready, 1)

                    def y_take(c):
                        act.wait_ge(piece_done, g * PIECES + (11 + c))
                        nc.scalar.copy(y_out[:, 0:tiles, c * HALF:(c + 1) * HALF],
                                       ps[:, 2 * c:2 * c + tiles, :]).then_inc(y_read, 1)

                    split_high(g, 4)
                    split_high(g, 5)
                    sigmoid(0)
                    split_high(g, 6)
                    split_high(g, 7)
                    split_high(g, 8)
                    split_high(g, 9)
                    aT_read_high(0)
                    sigmoid(1)
                    split_high(g, 10)
                    split_high(g, 11)
                    for th in range(2):
                        xT_read_high(g + 1, th)
                    split_high(g, 12)
                    aT_read_high(1)
                    split_high(g, 13)
                    act.wait_ge(y_stored, g * 32 + 32)
                    y_take(0)
                    split_high(g, 14)
                    y_take(1)
                    split_high(g, 15)
                    act.wait_ge(y_read, g * 2 + 4)
                    if tiles > 1:
                        act.dma_start(y_rows[bass.ds(row + P, P), :], y_out[:, 1, :]).then_inc(y_stored, 16)
                    else:
                        act.sem_inc(y_stored, 16)
                    act.dma_start(y_rows[bass.ds(row, P), :], y_out[:, 0, :]).then_inc(y_stored, 16)

                by_tiles(act, left, body)

            for t in range(TT):
                act.wait_ge(summed, t + 1)
                nc.scalar.activation(std[:, t:t + 1], mv[:, t, 1:2], ACT.Sqrt, bias=eps_t[:, 0:1]).then_inc(fin_std, 1)
                act.wait_ge(fin_norm, t + 1)
                nc.scalar.activation(h_res[:, t, :], h_res[:, t, :], ACT.Identity, bias=shift[:, t:t + 1],
                                     scale=inv[:, t:t + 1]).then_inc(fin_normed, 1)

        @block.vector
        def _(dve):
            V = nc.vector
            n = [0]

            def mark(ins):
                n[0] += 1
                ins.then_inc(dve_step, 1)

            def settle(behind=0):
                dve.wait_ge(dve_step, n[0] - behind)

            def step(ins):
                mark(ins)
                settle()

            def finish(ins):
                ins.then_inc(read_by["dve"], 1)

            V.memset(eps_t[:, :], EPS).then_inc(eps_ready, 1)

            def row_stats(src, t):
                for c in range(2):
                    mark(V.bn_stats(stats[:, t % 2, 6 * c:6 * c + 6], src[:, c * HALF:(c + 1) * HALF]))
                settle()
                return V.bn_aggr(mv[:, t, :], stats[:, t % 2, :])

            def norm_terms(a, b):
                step(V.reciprocal(inv[:, a:b], std[:, a:b]))
                return V.scalar_tensor_tensor(shift[:, a:b], mv[:, a:b, 0], -1.0, inv[:, a:b], ALU.mult, ALU.mult)

            for hf in range(2):
                for t in range(4 * hf, 4 * hf + 4):
                    dve.wait_ge(x_loaded[t // 2], 16)
                    last = row_stats(x_in[:, t, :], t)
                    if t % 4 < 3:
                        mark(last)
                    else:
                        last.then_inc(mean_ready, 1)
                dve.wait_ge(mean_ready, hf + 1)
                dve.wait_ge(std_ready, hf + 1)
                norm_terms(4 * hf, 4 * hf + 4).then_inc(norm_ready, 1)

            dve.wait_ge(params_loaded, PARAM_LOADS)
            for i in range(2):
                ins = V.tensor_tensor_reduce(out=sq_out[:, 0:DK], in0=lam_in[:, 2 * i, :], in1=lam_in[:, 2 * i + 1, :],
                                             scale=1.0, scalar=0.0, op0=ALU.mult, op1=ALU.add,
                                             accum_out=lam_s[:, i:i + 1])
                if i:
                    ins.then_inc(lam_s1, 1)
                else:
                    step(ins)
            was_read(dve, "dpar")
            was_read(dve, "chan")
            lam_c = chan[:, :, ROW_LAMBDA]
            step(V.tensor_scalar(soft[:, 4, :], lam_c, -1.0, None, ALU.mult))
            V.tensor_tensor(soft[:, 0, :], lam_c, soft[:, 4, :], ALU.min).then_inc(soft_s, 1)
            dve.wait_ge(soft_s, 2)
            V.tensor_scalar(soft[:, 2, :], soft[:, 1, :], 1.0, None, ALU.add).then_inc(soft_s, 1)
            dve.wait_ge(soft_s, 4)
            step(V.tensor_scalar(soft[:, 5, :], soft[:, 2, :], -1.0, 1e-30, ALU.add, ALU.max))
            step(V.reciprocal(soft[:, 5, :], soft[:, 5, :]))
            step(V.tensor_tensor(soft[:, 5, :], soft[:, 5, :], soft[:, 3, :], ALU.mult))
            step(V.scalar_tensor_tensor(soft[:, 2, :], soft[:, 2, :], 1.0, soft[:, 5, :], ALU.is_equal, ALU.add))
            step(V.tensor_tensor(soft[:, 2, :], soft[:, 2, :], soft[:, 1, :], ALU.mult))
            step(V.scalar_tensor_tensor(soft[:, 2, :], soft[:, 4, :], 0.0, soft[:, 2, :], ALU.max, ALU.add))
            V.tensor_scalar(decay[:, 0, :], soft[:, 2, :], -LRU_C, None, ALU.mult)
            V.tensor_scalar(decay[:, 1, :], soft[:, 2, :], -2.0 * LRU_C, None, ALU.mult).then_inc(decay_ready, 1)
            dve.wait_ge(lam_s1, 2)
            step(V.tensor_tensor(lam_s[:, 4:5], lam_s[:, 3:4], lam_s[:, 2:3], ALU.subtract))
            step(V.tensor_scalar(lam_s[:, 5:6], lam_s[:, 4:5], -LAM_INIT, None, ALU.add))
            neg_lam = lam_s[:, 5:6]

            def hT_read(hf, k):
                full(dve, ("hT", hf, k))
                finish(V.tensor_scalar(hT[:, k, hf * HALF:(hf + 1) * HALF], bank(("hT", hf, k)),
                                       dpar[:, k:k + 1], dpar[:, KT + k:KT + k + 1], ALU.mult, ALU.add))

            for hf in range(2):
                for k in range(0, KT, 2):
                    hT_read(hf, k)

            was_read(dve, ("in", "cf_b", 1, 1))
            for i in range(CT):
                mark(V.tensor_tensor(cfa[:, i, :], cfa[:, i, :], cfb[:, i, :], ALU.mult))
            settle()

            def tap(out_t, in_t, i, row, back, first_bias=None):
                w = chan[:, i, row:row + 1]
                if first_bias is not None:
                    return V.tensor_scalar(out_t, in_t, w, chan[:, i, first_bias:first_bias + 1], ALU.mult, ALU.add)
                return V.scalar_tensor_tensor(out_t[:, back:], in_t[:, :S - back], w, out_t[:, back:], ALU.mult, ALU.add)

            for j in range(CF_TAPS):
                for i in range(CT):
                    if j:
                        settle(behind=1)
                    mark(tap(cfb[:, i, :], cfa[:, i, :], i, ROW_CF_W + CF_TAPS - 1 - j, j, None if j else ROW_CF_B))
            settle(behind=1)
            settle()
            V.engine_nop().then_inc(conv_out, 1)

            def lru_conv(i):
                for j in range(LRU_TAPS):
                    ins = tap(xc, lrx[:, i, :], i, ROW_LRU_W + LRU_TAPS - 1 - j, j, None if j else ROW_LRU_B)
                    if j < LRU_TAPS - 1:
                        step(ins)
                    else:
                        ins.then_inc(xc_ready, 1)

            def lru(i):
                dve.wait_ge(decays, i + 1)
                step(V.tensor_scalar(mul, mul, -1.0, 1.0, ALU.mult, ALU.add))
                V.tensor_scalar(mul, mul, 1e-30, None, ALU.max).then_inc(one_minus, 1)
                step(V.tensor_tensor(gx, gx, xc, ALU.mult))
                dve.wait_ge(root, i + 1)
                step(V.tensor_tensor(gx, gx, mul, ALU.mult))
                step(V.tensor_tensor_scan(lrx[:, i, :], ga, gx, 0.0, ALU.mult, ALU.add))
                V.tensor_tensor(lrx[:, i, :], lrx[:, i, :], lry[:, i, :], ALU.mult).then_inc(lru_ready, 1)

            was_read(dve, ("in", "lru_y", 1, 1))
            dve.wait_ge(h_rows_ready, TT)
            lru_conv(0)
            for h in range(2):
                full(dve, ("mean", h))
                cols = slice(h * HALF, (h + 1) * HALF)
                mark(V.tensor_tensor(cfb[:, 0, cols], cfb[:, 0, cols], bank(("mean", h)), ALU.subtract))
                finish(V.tensor_tensor(cfb[:, 1, cols], cfb[:, 1, cols], bank(("mean", h)), ALU.subtract))
            dve.wait_ge(xc_ready, 1)
            lru(0)
            was_read(dve, ("var", 1))
            step(V.reciprocal(cfa[:, 0, :], cfa[:, 0, :]))
            was_read(dve, ("mean", 1))
            mark(V.tensor_tensor(cfb[:, 0, :], cfb[:, 0, :], cfa[:, 0, :], ALU.mult))
            V.tensor_tensor(cfb[:, 1, :], cfb[:, 1, :], cfa[:, 0, :], ALU.mult).then_inc(cf_scaled, 1)
            lru_conv(1)
            dve.wait_ge(xc_ready, 2)
            lru(1)

            def score_read_unit(u):
                h, q = UNITS[u]
                nk = (q + 1) * P
                dve.wait_ge(alibi_ready, h + 1)
                if u >= 2:
                    full(dve, ("o",) + UNITS[u - 2])
                for c in range(2):
                    dve.wait_ge(score_full, 2 * u + c + 1)
                    V.tensor_tensor_reduce(
                        out=maps[:, u % 2, c, 0:nk],
                        in0=ps[:, 2 * c:2 * c + 2, :].rearrange("p b n -> p (b n)")[:, 0:nk],
                        in1=scr[:, h % 2, S - nk:S], scale=1.0, scalar=-3.0e38, op0=ALU.add, op1=ALU.max,
                        accum_out=top[:, u % 2, c:c + 1]).then_inc(score_read, 1)
                dve.wait_ge(score_read, 2 * u + 2)
                V.tensor_scalar(ntop[:, u % 2, :], top[:, u % 2, :], -SCALE, None, ALU.mult).then_inc(top_ready, 1)

            def combine(u):
                h, q = UNITS[u]
                nk = (q + 1) * P
                dve.wait_ge(exp_ready, 2 * u + 2)
                step(V.reciprocal(rmass[:, u % 2, :], mass[:, u % 2, :]))
                step(V.scalar_tensor_tensor(coef[:, u % 2, :], mass[:, u % 2, 0:1], neg_lam, rmass[:, u % 2, 1:2],
                                            ALU.mult, ALU.mult))
                V.scalar_tensor_tensor(maps[:, u % 2, 0, 0:nk], maps[:, u % 2, 1, 0:nk], coef[:, u % 2, :],
                                       maps[:, u % 2, 0, 0:nk], ALU.mult, ALU.add).then_inc(map_ready, 1)

            def o_read(u):
                h, q = UNITS[u]
                o = oT[:, h, q * P:(q + 1) * P]
                full(dve, ("o", h, q))
                finish(V.tensor_scalar(o, bank(("o", h, q))[:, 0:P], rmass[:, u % 2, 0:1], None, ALU.mult))
                was_read(dve, ("o", h, q))
                V.tensor_tensor_reduce(out=sq_out[:, :], in0=o, in1=o, scale=1.0, scalar=0.0, op0=ALU.mult,
                                       op1=ALU.add, accum_out=o_sq[:, u:u + 1]).then_inc(o_ready, 1)

            score_read_unit(0)
            for u in range(len(UNITS)):
                if u + 1 < len(UNITS):
                    score_read_unit(u + 1)
                combine(u)
                if u:
                    o_read(u - 1)
            o_read(len(UNITS) - 1)
            dve.wait_ge(o_root, 1)
            step(V.reciprocal(o_inv[:, :], o_std[:, :]))
            for h in range(HEADS):
                o = oT[:, h, :].rearrange("p (q n) -> p q n", n=P)
                V.tensor_tensor(o, o, o_inv[:, h * TT:(h + 1) * TT].unsqueeze(2).broadcast_to([P, TT, P]),
                                ALU.mult).then_inc(o_scaled, 1)

            def mix_read(t):
                for c in range(2):
                    full(dve, ("mix", t, c))
                    cols = slice(c * HALF, (c + 1) * HALF)
                    finish(V.scalar_tensor_tensor(h_res[:, t, cols], h_res[:, t, cols], ALPHA,
                                                  bank(("mix", t, c)), ALU.mult, ALU.add))
                was_read(dve, ("mix", t, 1))
                row_stats(h_res[:, t, :], t).then_inc(mix_mean, 1)
                dve.wait_ge(mix_mean, t + 1)
                dve.wait_ge(mix_std, t + 1)
                norm_terms(t, t + 1).then_inc(mix_norm, 1)
                dve.wait_ge(norm_loaded[1], 32)
                dve.wait_ge(mix_normed, t + 1)
                step(V.tensor_tensor(h_res[:, t, :], h_res[:, t, :], norm_rows[:, 0, :], ALU.mult))
                V.tensor_tensor(h_res[:, t, :], h_res[:, t, :], norm_rows[:, 1, :], ALU.add).then_inc(h1_ready, 1)

            def logit_read(t):
                full(dve, ("logit", t))
                finish(V.tensor_tensor(logits[:, t, :], bank(("logit", t))[:, 0:EXPERTS], router_bias[:, :], ALU.add))
                was_read(dve, ("logit", t))
                step(V.max(best[:, t, :], logits[:, t, :]))
                step(V.max_index(best_at[:, t, :], best[:, t, :], logits[:, t, :]))

            for t in range(TT):
                mix_read(t)
                if t:
                    logit_read(t - 1)
            logit_read(TT - 1)

            V.tensor_tensor(gates[:, :, :], best[:, :, 0:TOP_K], best[:, :, 0:1].broadcast_to([P, TT, TOP_K]),
                            ALU.subtract).then_inc(gate_diff, 1)
            step(V.tensor_copy(chosen[:, :, :], best_at[:, :, 0:TOP_K]))
            wide = [P, TT, EXPERTS]
            for k in range(TOP_K):
                mark(V.tensor_tensor(one_hot[:, k, :, :], iota_e[:, :].unsqueeze(1).broadcast_to(wide),
                                     chosen[:, :, k:k + 1].broadcast_to(wide), ALU.is_equal))
            settle()
            step(V.tensor_tensor(mask[:, :, :], one_hot[:, 0, :, :], one_hot[:, 1, :, :], ALU.add))
            step(V.tensor_tensor(mask[:, :, :], mask[:, :, :], one_hot[:, 2, :, :], ALU.add))
            step(V.tensor_tensor(mask[:, :, :], mask[:, :, :], one_hot[:, 3, :, :], ALU.add))
            V.tensor_copy(mask_b[:, :, :], mask[:, :, :]).then_inc(mask_ready, 1)
            full(dve, "rank")
            ranks = bank("rank")[:, 0:TT * EXPERTS].rearrange("p (t e) -> p t e", e=EXPERTS)
            step(V.tensor_copy(count[:, :], bank("rank")[:, TT * EXPERTS:(TT + 1) * EXPERTS]))
            step(V.tensor_scalar(blocks[:, :], count[:, :], float(CAP), 1.0, ALU.is_gt, ALU.add))
            step(V.scalar_tensor_tensor(blocks[:, :], count[:, :], 2.0 * CAP, blocks[:, :], ALU.is_gt, ALU.add))
            step(V.scalar_tensor_tensor(blocks[:, :], count[:, :], 3.0 * CAP, blocks[:, :], ALU.is_gt, ALU.add))
            step(V.tensor_tensor_scan(ends[:, :], ones_t[:, 0:EXPERTS], blocks[:, :], 0.0, ALU.mult, ALU.add))
            mark(V.tensor_tensor(starts[:, :], ends[:, :], blocks[:, :], ALU.subtract))
            mark(V.tensor_copy(ends_i[:, :], ends[0:1, :]))
            table = [P, TABLE, EXPERTS]
            step(V.tensor_tensor(cmp, ends[:, :].unsqueeze(1).broadcast_to(table),
                                 iota_g[:, :].unsqueeze(2).broadcast_to(table), ALU.is_le))
            step(V.tensor_reduce(expert_f[:, :], cmp, AX.X, ALU.add))
            step(V.tensor_scalar(expert_f[:, :], expert_f[:, :], EXPERTS - 1.0, None, ALU.min))
            mark(V.tensor_copy(expert_i[:, :], expert_f[0:1, :]))
            step(V.tensor_tensor(cmp, iota_e[:, :].unsqueeze(1).broadcast_to(table),
                                 expert_f[:, :].unsqueeze(2).broadcast_to(table), ALU.is_equal))
            step(V.tensor_tensor(cmp, cmp, starts[:, :].unsqueeze(1).broadcast_to(table), ALU.mult))
            step(V.tensor_reduce(offset_f[:, :], cmp, AX.X, ALU.add))
            step(V.tensor_tensor(offset_f[:, :], offset_f[:, :], iota_g[:, :], ALU.subtract))
            step(V.tensor_scalar(offset_f[:, :], offset_f[:, :], float(CAP), None, ALU.mult))
            step(V.tensor_tensor(cmp, iota_e[:, :].unsqueeze(1).broadcast_to(table),
                                 expert_f[:, :].unsqueeze(2).broadcast_to(table), ALU.is_equal))
            step(V.tensor_tensor(cmp, cmp, count[:, :].unsqueeze(1).broadcast_to(table), ALU.mult))
            step(V.tensor_reduce(left_f[:, :], cmp, AX.X, ALU.add))
            step(V.tensor_tensor(left_f[:, :], left_f[:, :], offset_f[:, :], ALU.add))
            mark(V.tensor_copy(left_i[:, :], left_f[0:1, :]))
            step(V.tensor_scalar(row_f[:, 0, :], left_f[:, :], float(CAP), None, ALU.min))
            step(V.tensor_tensor_scan(row_f[:, 1, :], ones_t[:, :], row_f[:, 0, :], 0.0, ALU.mult, ALU.add))
            step(V.tensor_tensor(row_f[:, 1, :], row_f[:, 1, :], row_f[:, 0, :], ALU.subtract))
            mark(V.tensor_copy(row_i[:, :], row_f[0:1, 1, :]))
            step(V.scalar_tensor_tensor(rank_of[:, :, :].rearrange("p e t -> p t e"), ranks, 1.0, mask[:, :, :],
                                        ALU.add, ALU.mult))
            step(V.tensor_scalar(rank_of[:, :, :], rank_of[:, :, :], -1.0, None, ALU.add))
            step(V.tensor_tensor_scan(first[:, :], ones_t[:, 0:EXPERTS], count[:, :], 0.0, ALU.mult, ALU.add))
            step(V.tensor_tensor(first[:, :], first[:, :], count[:, :], ALU.subtract))
            finish(V.tensor_tensor(rows_at[:, :, :], ranks, first[:, :].unsqueeze(1).broadcast_to(wide), ALU.add))
            was_read(dve, "rank")
            for k in range(TOP_K):
                step(V.tensor_tensor(cmp[:, 0:TT, :], one_hot[:, k, :, :], rows_at[:, :, :], ALU.mult))
                step(V.tensor_reduce(dest[:, :, k], cmp[:, 0:TT, :], AX.X, ALU.add))
            step(V.tensor_copy(dest_i[:, :, :], dest[:, :, :]))
            V.engine_nop().then_inc(tables_ready, 1)

            def pick_block(g, expert):
                own = rank_of[:, bass.ds(expert, 1), :].rearrange("p e t -> p (e t)")
                V.tensor_scalar(rank_now[:, :], own, offset_f[:, bass.ds(g, 1)], None, ALU.add).then_inc(rank_step, 1)
                dve.wait_ge(rank_step, g + 1)
                wide_s = [P, TT, CAP]
                V.tensor_tensor(pick, iota_s[:, :].unsqueeze(1).broadcast_to(wide_s),
                                rank_now[:, :].unsqueeze(2).broadcast_to(wide_s), ALU.is_equal).then_inc(pick_ready, 1)

            def slots_read(g):
                dve.wait_ge(slots_full, g + 1)
                V.tensor_copy(token_at[:, :], ps[:, 7, 0:2]).then_inc(slots_ready, 1)

            def xT_read_low(g):
                for th in range(2):
                    dve.wait_ge(xT_high_ready, g * 2 + (th + 1))
                    V.tensor_tensor(xT_low[:, :, th * P:(th + 1) * P],
                                    ps[:, 4 + 2 * th:6 + 2 * th, :].rearrange("p b (k n) -> p (b k) n", n=P),
                                    xT_high[:, :, th * P:(th + 1) * P].bitcast(F32), ALU.subtract).then_inc(xT_read, 1)

            expert = dve.value_load(expert_i[0:1, 0:1], min_val=0, max_val=EXPERTS - 1)
            pick_block(0, expert)
            slots_read(0)
            split_low(dve, V, 0, 0)
            split_low(dve, V, 0, 1)
            dve.wait_ge(gate_exp, 1)
            step(V.tensor_reduce(gsum[:, :], gates[:, :, :], AX.X, ALU.add))
            step(V.reciprocal(gsum[:, :], gsum[:, :]))
            step(V.tensor_tensor(gates[:, :, :], gates[:, :, :], gsum[:, :].unsqueeze(2).broadcast_to([P, TT, TOP_K]), ALU.mult))
            for k in range(TOP_K):
                mark(V.tensor_tensor(one_hot[:, k, :, :], one_hot[:, k, :, :], gates[:, :, k:k + 1].broadcast_to(wide), ALU.mult))
            settle()
            step(V.tensor_tensor(gate_m[:, :, :], one_hot[:, 0, :, :], one_hot[:, 1, :, :], ALU.add))
            step(V.tensor_tensor(gate_m[:, :, :], gate_m[:, :, :], one_hot[:, 2, :, :], ALU.add))
            V.tensor_tensor(gate_m[:, :, :], gate_m[:, :, :], one_hot[:, 3, :, :], ALU.add).then_inc(gate_m_ready, 1)
            dve.wait_ge(h1_stored, 16 * TT)
            for t in range(TT):
                for c in range(2):
                    full(dve, ("b2", t, c))
                    cols = slice(c * HALF, (c + 1) * HALF)
                    finish(V.scalar_tensor_tensor(h_res[:, t, cols], h_res[:, t, cols], ALPHA, bank(("b2", t, c)),
                                                  ALU.mult, ALU.add))
            split_low(dve, V, 0, 3)
            xT_read_low(0)

            total = dve.value_load(ends_i[0:1, EXPERTS - 1:EXPERTS], min_val=EXPERTS, max_val=MAX_BLOCKS)
            with dve.Fori(0, total) as g:
                left = dve.value_load(left_i[0:1, bass.ds(g, 1)], min_val=-BIG, max_val=BIG)
                after = dve.value_load(expert_i[0:1, bass.ds(g + 1, 1)], min_val=0, max_val=EXPERTS - 1)

                def body(tiles):
                    def clip(c, part):
                        dve.wait_ge(piece_done, g * PIECES + (4 * c + 2 * part + 2))
                        dst = (glu, lin)[part]
                        V.tensor_scalar(dst[:, 0:tiles, :], ps[:, 2 * part:2 * part + tiles, :], LIMIT,
                                        -LIMIT if part else None, ALU.min,
                                        ALU.max if part else ALU.bypass).then_inc(hidden_read, 1)

                    def product(c):
                        dve.wait_ge(sig_ready, g * 2 + (c + 1))
                        V.tensor_tensor(sig[:, 0:tiles, :], sig[:, 0:tiles, :], glu[:, 0:tiles, :],
                                        ALU.mult).then_inc(swish_step, 1)
                        dve.wait_ge(hidden_read, g * 4 + (2 * c + 2))
                        dve.wait_ge(swish_step, g * 2 + (c + 1))
                        V.scalar_tensor_tensor(lin[:, 0:tiles, :], lin[:, 0:tiles, :], 1.0, sig[:, 0:tiles, :],
                                               ALU.add, ALU.mult).then_inc(act_rows, 1)

                    def aT_read_low(c):
                        dve.wait_ge(aT_high_ready, g * 2 + (c + 1))
                        part = act_low[:, HK * c:HK * (c + 1), 0:tiles * P].rearrange("p k (t n) -> p t k n", n=P)
                        src = ps[:, 4 + 2 * c:4 + 2 * c + tiles, :].rearrange("p t (k n) -> p t k n", n=P)
                        rounded = act_high[:, HK * c:HK * (c + 1), 0:tiles * P].bitcast(F32)\
                            .rearrange("p k (t n) -> p t k n", n=P)
                        V.tensor_tensor(part, src, rounded, ALU.subtract).then_inc(aT_read, 1)

                    pick_block(g + 1, after)
                    split_low(dve, V, g, 4)
                    clip(0, 0)
                    split_low(dve, V, g, 6)
                    clip(0, 1)
                    product(0)
                    slots_read(g + 1)
                    split_low(dve, V, g, 7)
                    clip(1, 0)
                    aT_read_low(0)
                    split_low(dve, V, g, 9)
                    split_low(dve, V, g, 10)
                    clip(1, 1)
                    product(1)
                    xT_read_low(g + 1)
                    split_low(dve, V, g, 12)
                    aT_read_low(1)
                    split_low(dve, V, g, 13)
                    split_low(dve, V, g, 15)

                by_tiles(dve, left, body)

            dve.wait_ge(norm_loaded[2], 32)
            for t in range(TT + 1):
                if t < TT:
                    for k in range(TOP_K):
                        dve.wait_ge(got[4 * (t % 2) + k], 16 * (t // 2 + 1))
                        step(V.scalar_tensor_tensor(h_res[:, t, :], y_got[:, t % 2, k, :], gates[:, t, k:k + 1],
                                                    h_res[:, t, :], ALU.mult, ALU.add))
                    row_stats(h_res[:, t, :], t).then_inc(summed, 1)
                    dve.wait_ge(summed, t + 1)
                    dve.wait_ge(fin_std, t + 1)
                    norm_terms(t, t + 1).then_inc(fin_norm, 1)
                if t:
                    dve.wait_ge(fin_normed, t)
                    step(V.tensor_tensor(h_res[:, t - 1, :], h_res[:, t - 1, :], norm_rows[:, 0, :], ALU.mult))
                    V.tensor_tensor(h_res[:, t - 1, :], h_res[:, t - 1, :], norm_rows[:, 1, :], ALU.add).then_inc(out_ready, 1)

        @block.tensor
        def _(pe):
            T = nc.tensor

            def begin(name):
                if NUMBER[name] >= 4:
                    was_read(pe, JOBS[NUMBER[name] - 4][0])

            def end(ins):
                ins.then_inc(job_full, 1)

            pe.wait_ge(const_ready, 1)
            pe.wait_ge(params_loaded, PARAM_LOADS)
            for i in range(CT):
                last = T.transpose(bank("chan")[:, i * CHAN_ROWS:(i + 1) * CHAN_ROWS], chan_rows[:, i * P:(i + 1) * P],
                                   ident[0:CHAN_ROWS, 0:CHAN_ROWS])
            end(last)
            end(T.transpose(bank("dpar")[:, 0:2 * KT + 1], dpar_rows, ident[0:2 * KT + 1, 0:2 * KT + 1]))
            def hT_write(hf):
                for k in range(KT):
                    begin(("hT", hf, k))
                    for t in range(4):
                        if not k:
                            pe.wait_ge(normed, 4 * hf + t + 1)
                        last = T.transpose(bank(("hT", hf, k))[:, t * P:(t + 1) * P],
                                           h_res[:, 4 * hf + t, k * P:(k + 1) * P], ident[:, :])
                    end(last)

            def loaded(name):
                i = IN_PIECES.index(name)
                pe.wait_ge(w_loaded[i % FRONT_SLOTS], 16 * (i // FRONT_SLOTS + 1))
                return slot(i % FRONT_SLOTS)

            def in_write(p, c, h):
                name = ("in", p, c, h)
                w = loaded(p)
                begin(name)
                for k in range(KT):
                    last = T.matmul(bank(name), w[:, k, c * P:(c + 1) * P], hT[:, k, h * HALF:(h + 1) * HALF],
                                    start=k == 0, stop=k == KT - 1)
                end(last)

            def v_write(t):
                begin(("v", t))
                for c in range(2):
                    w = loaded(f"v{c}")
                    for k in range(KT):
                        last = T.matmul(bank(("v", t))[:, c * PIECE:(c + 1) * PIECE], hT[:, k, t * P:(t + 1) * P],
                                        w[:, k, :], start=k == 0, stop=k == KT - 1)
                end(last)

            def gate_write(i):
                pe.wait_ge(gate_w_loaded, 16 * 2 * CT * 2)
                pe.wait_ge(xc_ready, i + 1)
                for w, wn in enumerate(("a", "x")):
                    for h in range(2):
                        begin(("gate", i, wn, h))
                        end(T.matmul(bank(("gate", i, wn, h)), gate_w[:, w, i, :], xc[:, h * HALF:(h + 1) * HALF],
                                     start=True, stop=True))

            def channel_sum(kind, src):
                for h in range(2):
                    begin((kind, h))
                    if kind == "var":
                        pe.wait_ge(squared, h + 1)
                    for i in range(CT):
                        last = T.matmul(bank((kind, h)), chan_mean[:, :], src[:, i, h * HALF:(h + 1) * HALF],
                                        start=i == 0, stop=i == CT - 1)
                    end(last)

            hT_write(0)
            was_read(pe, ("hT", 0, KT - 1))
            was_read(pe, ("hT", 0, KT - 2))
            for p in ("cf_a", "cf_b"):
                for c in range(CT):
                    in_write(p, c, 0)
            hT_write(1)
            was_read(pe, ("hT", 1, KT - 1))
            was_read(pe, ("hT", 1, KT - 2))
            for p in ("cf_a", "cf_b"):
                for c in range(CT):
                    in_write(p, c, 1)
            for p in ("lru_x", "lru_y"):
                for c in range(CT):
                    for h in range(2):
                        in_write(p, c, h)
            for t in range(4):
                v_write(t)
            pe.wait_ge(const_ready, 2)
            pe.wait_ge(conv_out, 1)
            channel_sum("mean", cfb)
            v_write(4)
            v_write(5)
            gate_write(0)
            v_write(6)
            v_write(7)
            channel_sum("var", cfa)
            for c in range(CT):
                for h in range(2):
                    in_write("q0", c, h)
            gate_write(1)
            for p in ("q1", "k0", "k1"):
                for c in range(CT):
                    for h in range(2):
                        in_write(p, c, h)

            def scores(u):
                h, q = UNITS[u]
                for c in range(2):
                    if u:
                        pe.wait_ge(score_read, 2 * (u - 1) + c + 1)
                    for b in range(q // 4 + 1):
                        nk = min(HALF, (q + 1) * P - b * HALF)
                        last = T.matmul(ps[:, 2 * c + b, 0:nk], qT[DK * c:DK * (c + 1), h, q * P:(q + 1) * P],
                                        kT[DK * c:DK * (c + 1), h, b * HALF:b * HALF + nk], start=True, stop=True)
                    last.then_inc(score_full, 1)

            def attend(u):
                h, q = UNITS[u]
                pe.wait_ge(map_ready, u + 1)
                for g in range(q // 4 + 1):
                    begin(("pT", h, q, g))
                    for k in range(4 * g, min(4 * g + 4, q + 1)):
                        last = T.transpose(bank(("pT", h, q, g))[:, (k % 4) * P:(k % 4 + 1) * P],
                                           maps[:, u % 2, 0, k * P:(k + 1) * P], ident[:, :])
                    end(last)

            def values(u):
                h, q = UNITS[u]
                begin(("o", h, q))
                was_read(pe, ("pT", h, q, q // 4))
                for k in range(q + 1):
                    last = T.matmul(bank(("o", h, q))[:, 0:P], pT[:, u % 2, k, :], v[:, k, h * DV:(h + 1) * DV],
                                    start=k == 0, stop=k == q)
                end(last)

            was_read(pe, ("in", "k1", 1, 1))
            scores(0)
            for u in range(len(UNITS)):
                if u + 1 < len(UNITS):
                    scores(u + 1)
                attend(u)
                values(u)
            for h in range(HEADS):
                pe.wait_ge(o_scaled, h + 1)
                for g in range(2):
                    begin(("oT", h, g))
                    for q in range(4 * g, 4 * g + 4):
                        last = T.transpose(bank(("oT", h, g))[:, (q % 4) * P:(q % 4 + 1) * P],
                                           oT[:, h, q * P:(q + 1) * P], ident[:, :])
                    end(last)

            def mix_write(t):
                for c in range(2):
                    begin(("mix", t, c))
                    for i in (2 * c, 2 * c + 1):
                        if not t:
                            pe.wait_ge(w_loaded[i], BEFORE[i])
                        for k in range(KT):
                            src = oT[:, k, :] if k < 4 else lrx[:, k - 4, :] if k < 6 else cfb[:, k - 6, :]
                            last = T.matmul(bank(("mix", t, c))[:, (i % 2) * PIECE:(i % 2 + 1) * PIECE],
                                            src[:, t * P:(t + 1) * P], slot(i)[:, k, :], start=k == 0, stop=k == KT - 1)
                    end(last)

            def route(t):
                pe.wait_ge(h1_ready, t + 1)
                for g in range(2):
                    begin(("h1T", t, g))
                    for k in range(4 * g, 4 * g + 4):
                        last = T.transpose(bank(("h1T", t, g))[:, (k % 4) * P:(k % 4 + 1) * P],
                                           h_res[:, t, k * P:(k + 1) * P], ident[:, :])
                    end(last)
                begin(("logit", t))
                was_read(pe, ("h1T", t, 1))
                for k in range(KT):
                    last = T.matmul(bank(("logit", t))[:, 0:EXPERTS], h1T[:, k, :], router[:, k, :],
                                    start=k == 0, stop=k == KT - 1)
                end(last)

            was_read(pe, ("oT", HEADS - 1, 1))
            pe.wait_ge(cf_ready, CT)
            pe.wait_ge(lru_ready, CT)
            for t in range(TT + 1):
                if t < TT:
                    mix_write(t)
                if t:
                    route(t - 1)

            begin("rank")
            pe.wait_ge(mask_ready, 1)
            for t in range(TT + 1):
                dst = bank("rank")[:, t * EXPERTS:(t + 1) * EXPERTS]
                for s in range(t):
                    last = T.matmul(dst, ones[:, :], mask_b[:, s, :], start=s == 0, stop=t == TT and s == TT - 1)
                if t < TT:
                    last = T.matmul(dst, before[:, :], mask_b[:, t, :], start=t == 0, stop=True)
            end(last)

            def slots_write(g):
                pe.wait_ge(pick_ready, g + 1)
                for th in range(2):
                    for t in range(TT):
                        last = T.matmul(ps[:, 7, th:th + 1], pick[:, t, th * P:(th + 1) * P], token_no[:, t:t + 1],
                                        start=t == 0, stop=t == TT - 1)
                last.then_inc(slots_full, 1)

            def xT_write(th):
                for k in range(KT):
                    last = T.transpose(ps[:, 4 + 2 * th + k // 4, (k % 4) * P:(k % 4 + 1) * P],
                                       x_rows[:, th, k * P:(k + 1) * P], ident[:, :])
                last.then_inc(xT_full, 1)

            was_read(pe, "rank")
            slots_write(0)
            for t in range(TT):
                begin(("gT", t))
                if not t:
                    pe.wait_ge(gate_m_ready, 1)
                end(T.transpose(bank(("gT", t))[0:EXPERTS, 0:P], gate_m[:, t, :], ident[:, :]))
                was_read(pe, ("gT", t))
                if not t:
                    pe.wait_ge(b2_loaded, 16)
                for c in range(2):
                    begin(("b2", t, c))
                    end(T.matmul(bank(("b2", t, c)), gate_t[:, t % 2, :], b2_rows[:, c * HALF:(c + 1) * HALF],
                                 start=True, stop=True))
            was_read(pe, ("b2", TT - 1, 1))
            pe.wait_ge(x_got, 32)
            for th in range(2):
                xT_write(th)

            pe.wait_ge(ones_r_ready, 1)
            total = pe.value_load(ends_i[0:1, EXPERTS - 1:EXPERTS], min_val=EXPERTS, max_val=MAX_BLOCKS)
            with pe.Fori(0, total) as g:
                left = pe.value_load(left_i[0:1, bass.ds(g, 1)], min_val=-BIG, max_val=BIG)

                def body(tiles):
                    def piece(p):
                        wait_low(pe, g, p)
                        if p < 8:
                            part, kh, (x_high, x_low) = p // 2 % 2, p % 2, (xT_high, xT_low)
                            if not kh and p < 4:
                                pe.wait_ge(y_read, g * 2 + (part + 1))
                            elif not kh:
                                pe.wait_ge(hidden_read, g * 4 + (part + 1))
                        else:
                            part, kh, (x_high, x_low) = p % 2, (p - 8) // 2, (act_high, act_low)
                            if not kh:
                                pe.wait_ge(hidden_read, g * 4 + (part + 3))
                            if not part:
                                pe.wait_ge(aT_read, g * 2 + (kh + 1))
                        for t in range(tiles):
                            dst = ps[:, 2 * part + t, :]
                            if p < 8 and not kh:
                                c = part * D + (p // 4) * HALF
                                if not p and not t:
                                    pe.wait_ge(b1_loaded, g * 16 + 16)
                                T.matmul(dst, ones_r[0:2, :], b1_now[0:2, c:c + HALF], start=True, stop=False)
                            for k in range(HK):
                                tokens = (slice(None), HK * kh + k, slice(t * P, (t + 1) * P))
                                w_high, w_low = high[:, p % SPLIT, k, :], low[:, p % SPLIT, k, :]
                                T.matmul(dst, x_high[tokens], w_high, start=p >= 8 and not kh and not k, stop=False)
                                T.matmul(dst, x_high[tokens], w_low, start=False, stop=False)
                                last = T.matmul(dst, x_low[tokens], w_high, start=False, stop=kh == 1 and k == HK - 1)
                        last.then_inc(piece_done, 1)

                    def aT_write(c):
                        pe.wait_ge(act_rows, g * 2 + (c + 1))
                        for t in range(tiles):
                            for k in range(HK):
                                last = T.transpose(ps[:, 4 + 2 * c + t, k * P:(k + 1) * P],
                                                   lin[:, t, k * P:(k + 1) * P], ident[:, :])
                        last.then_inc(aT_full, 1)

                    pe.wait_ge(xT_read, g * 2 + 2)
                    for p in range(4):
                        piece(p)
                    slots_write(g + 1)
                    piece(4)
                    piece(5)
                    aT_write(0)
                    piece(6)
                    piece(7)
                    pe.wait_ge(x_got, g * 32 + 64)
                    pe.wait_ge(aT_read, g * 2 + 1)
                    for th in range(2):
                        xT_write(th)
                    piece(8)
                    pe.wait_ge(xT_read, g * 2 + 4)
                    aT_write(1)
                    piece(9)
                    piece(10)
                    piece(11)

                by_tiles(pe, left, body)


_OUT = (1, S, D)


def kernel(**inputs):
    import numpy as np
    import concourse.bacc as bacc
    from concourse.bass_utils import run_bass_kernel_spmd

    names = ["x", "ln_in_g", "ln_in_b", "w_in", "lam_q1", "lam_k1", "lam_q2", "lam_k2", "subln_g",
             "lru_conv_w", "lru_conv_b", "lru_wa", "lru_ba", "lru_wx", "lru_bx", "lru_lambda",
             "cf_conv_w", "cf_conv_b", "cf_ln_g", "cf_ln_b", "w_out", "ln1_g", "ln1_b",
             "router_w", "router_b", "moe_w1", "moe_b1", "moe_w2", "moe_b2", "ln2_g", "ln2_b"]
    nc = bacc.Bacc("TRN2", target_bir_lowering=False, num_devices=1)
    arrays, args = {}, []
    for name in names:
        a = np.ascontiguousarray(inputs[name])
        arrays[f"in_{name}"] = a
        args.append(nc.dram_tensor(f"in_{name}", a.shape, mybir.dt.from_np(a.dtype), kind="ExternalInput").ap())
    out = nc.dram_tensor("out", _OUT, F32, kind="ExternalOutput").ap()
    hybrid_layer(nc, *args, out)
    result = run_bass_kernel_spmd(nc, [arrays], core_ids=[0])
    return result.results[0]["out"]
```

```python
import math
from contextlib import ExitStack

import concourse.bass as bass
from concourse import mybir

F32 = mybir.dt.float32
F32R = mybir.dt.float32r
F16 = mybir.dt.float16
BF16 = mybir.dt.bfloat16
I32 = mybir.dt.int32
U32 = mybir.dt.uint32
ALU = mybir.AluOpType
ACT = mybir.ActivationFunctionType
AX = mybir.AxisListType

P = 128
D = 1024
S = 1024
KT = D // P
TT = S // P
HALF = 512
EPS = 1e-5
ALPHA = 2.0 ** 0.25

HEADS = 4
DK = D // 16
DV = 2 * DK
SCALE = DK ** -0.5
SLOPES = [2.0 ** (-8.0 * (h + 1) / HEADS) for h in range(HEADS)]
LAM_INIT = 0.8 - 0.6 * math.exp(0.0)
MASKED = -1.0e30

GROUP = D // 4
CT = GROUP // P
LRU_TAPS, CF_TAPS = 4, 31
LRU_C = 8.0

EXPERTS = 32
TOP_K = 4
LIMIT = 7.0
SWIGLU_ALPHA = 1.702
CAP = 256
PIECE = 256
HK = KT // 2
PIECES = 12
RAW = 6
POOL_TURN = 3
SPLIT = 4
GOT = 5
MAX_BLOCKS = (S * TOP_K + EXPERTS * CAP) // CAP
TABLE = MAX_BLOCKS + 1
TILES = (1, 2)
BIG = 1 << 20

IN_PIECES = ["cf_a", "cf_b", "lru_x", "lru_y", "v0", "v1", "q0", "q1", "k0", "k1"]
IN_COLUMN = {"q0": 0, "q1": 256, "k0": 512, "k1": 768, "v0": 1024, "v1": 1280,
             "lru_x": 1536, "lru_y": 1792, "cf_a": 2048, "cf_b": 2304}
FRONT_SLOTS = 4

ROW_LRU_W, ROW_LRU_B, ROW_BA, ROW_BX, ROW_LAMBDA = 0, 4, 5, 6, 7
ROW_CF_W, ROW_CF_B, ROW_CF_G, ROW_CF_BETA, CHAN_ROWS = 8, 39, 40, 41, 42


def evacuation_jobs():
    jobs = [("dpar", "act")]
    jobs += [(("hT", 0, k), "act" if k % 2 else "dve") for k in range(KT)]
    jobs += [(("in", p, c, 0), "act") for p in ("cf_a", "cf_b") for c in range(CT)]
    jobs += [(("hT", 1, k), "act" if k % 2 else "dve") for k in range(KT)] + [("chan", "act")]
    jobs += [(("in", p, c, 1), "act") for p in ("cf_a", "cf_b") for c in range(CT)]
    jobs += [(("in", p, c, h), "act") for p in ("lru_x", "lru_y") for c in range(CT) for h in range(2)]
    jobs += [(("v", t), "act") for t in range(4)]
    jobs += [(("mean", h), "dve") for h in range(2)]
    jobs += [(("v", t), "act") for t in (4, 5)]
    jobs += [(("gate", 0, w, h), "act") for w in ("a", "x") for h in range(2)]
    jobs += [(("v", t), "act") for t in (6, 7)]
    jobs += [(("var", h), "act") for h in range(2)]
    jobs += [(("in", "q0", c, h), "act") for c in range(CT) for h in range(2)]
    jobs += [(("gate", 1, w, h), "act") for w in ("a", "x") for h in range(2)]
    jobs += [(("in", p, c, h), "act") for p in ("q1", "k0", "k1") for c in range(CT) for h in range(2)]
    units = [(h, q) for h in range(HEADS) for q in range(TT)]
    for u, (h, q) in enumerate(units):
        jobs += [(("pT", h, q, g), "act") for g in range(q // 4 + 1)]
        if u:
            jobs += [(("o",) + units[u - 1], "dve")]
    jobs += [(("o",) + units[-1], "dve")]
    jobs += [(("oT", h, g), "act") for h in range(HEADS) for g in range(2)]
    for t in range(TT + 1):
        if t < TT:
            jobs += [(("mix", t, c), "dve") for c in range(2)]
        if t:
            jobs += [(("h1T", t - 1, g), "act") for g in range(2)] + [(("logit", t - 1), "dve")]
    jobs += [("rank", "dve")]
    return jobs


def hybrid_layer(nc, x, ln_in_g, ln_in_b, w_in, lam_q1, lam_k1, lam_q2, lam_k2, subln_g,
                 lru_conv_w, lru_conv_b, lru_wa, lru_ba, lru_wx, lru_bx, lru_lambda,
                 cf_conv_w, cf_conv_b, cf_ln_g, cf_ln_b, w_out, ln1_g, ln1_b,
                 router_w, router_b, moe_w1, moe_b1, moe_w2, moe_b2, ln2_g, ln2_b, out):
    JOBS = evacuation_jobs()
    NUMBER = {name: n for n, (name, _) in enumerate(JOBS)}
    ORDINAL = {}
    for engine in ("act", "dve"):
        for n, name in enumerate(name for name, by in JOBS if by == engine):
            ORDINAL[name] = n
    READER = dict(JOBS)
    UNITS = [(h, q) for h in range(HEADS) for q in range(TT)]

    h1_rows = nc.dram_tensor("h1_rows", [S, D], F32).ap()
    b1_parts = nc.dram_tensor("b1_parts", [EXPERTS, 2, 2 * D], F32).ap()
    b2_parts = nc.dram_tensor("b2_parts", [EXPERTS, 2, D], F32).ap()
    y_rows = nc.dram_tensor("y_rows", [S * TOP_K + CAP, D], F32).ap()

    x_tiles = x[0].rearrange("(t p) d -> p t d", p=P)
    out_tiles = out[0].rearrange("(t p) d -> p t d", p=P)
    h1_tiles = h1_rows.rearrange("(t p) d -> p t d", p=P)
    w_in_v = w_in[0].rearrange("(k p) n -> p k n", p=P)
    w_out_v = w_out[0].rearrange("(k p) n -> p k n", p=P)
    w1_v = moe_w1[0].rearrange("e (k p) n -> e p k n", p=P)
    w2_v = moe_w2[0].rearrange("e (k p) n -> e p k n", p=P)

    ctx = ExitStack()
    with ctx:
        at = {}

        def sb(name, shape, dt=F32):
            tensor = ctx.enter_context(nc.sbuf_tensor(name, shape, dt))
            at[name] = nc.sbuf_base - 4 * math.prod(shape[1:])
            return tensor

        def sem(name):
            return ctx.enter_context(nc.semaphore(name))

        ring = sb("ring", [P, PIECES, KT * PIECE])
        h_res = sb("h_res", [P, TT, D])
        big = sb("big", [P, KT, S])
        scr = sb("scr", [P, 4, S])
        cfb = sb("cfb", [P, CT, S])
        lrx = sb("lrx", [P, CT, S])

        def slot(s):
            return ring[:, s, :].rearrange("p (k n) -> p k n", k=KT)

        x_in = ring[:, 6:10, :].rearrange("p s (t d) -> p (s t) d", d=D)
        b1_rows = ring[0:EXPERTS, 10, :]
        b2_rows = ring[0:EXPERTS, 11, D:2 * D]
        chan_rows = ring[0:CHAN_ROWS, 11, 0:GROUP]
        dpar_rows = ring[0:2 * KT + 1, 11, GROUP:GROUP + P]
        lam_in = ring[:, 11, HALF:HALF + 4 * DK].rearrange("p (a n) -> p a n", a=4)
        qT = ring[:, 6:8, :].rearrange("p s (h t) -> p (s h) t", h=2)
        kT = ring[:, 8:10, :].rearrange("p s (h t) -> p (s h) t", h=2)
        v = ring[:, 10:12, :].rearrange("p s (t n) -> p (s t) n", n=HALF)
        lry = ring[:, 4, :].rearrange("p (i s) -> p i s", i=CT)
        cfa = ring[:, 5, :].rearrange("p (i s) -> p i s", i=CT)
        pT = ring[:, 5, :].rearrange("p (b k q) -> p b k q", b=2, k=TT)
        hT = big
        oT = big[:, 0:HEADS, :]
        maps = big[:, HEADS:, :].rearrange("p (b c) s -> p b c s", b=2)
        norm_rows = scr[:, 0:2, :]
        xc, ga, gx, mul = (scr[:, i, :] for i in range(4))
        alibi = scr[:, 2, :]
        h1T = big[:, 4, :].rearrange("p (k q) -> p k q", k=KT)
        one_hot = big[:, 5, :].rearrange("p (k t e) -> p k t e", k=TOP_K, e=EXPERTS)
        cmp = big[:, 6:8, :].rearrange("p a s -> p (a s)")[:, 0:TABLE * EXPERTS]\
            .rearrange("p (g e) -> p g e", e=EXPERTS)
        by_expert = big[:, 4, :].rearrange("p (a t e) -> p a t e", a=4, e=EXPERTS)
        mask, ranks, rows_at = by_expert[:, 0], by_expert[:, 1], by_expert[:, 2]
        mask_b = big[:, 4, 3 * TT * EXPERTS:].bitcast(BF16)[:, 0:TT * EXPERTS].rearrange("p (t e) -> p t e", e=EXPERTS)
        def alias(name, base, base_name, first, shape):
            row = 4 * math.prod(base.shape[2:])
            return nc.alloc_sbuf_tensor_at(name, shape, F32R, offset=at[base_name] + first * row)

        high = alias("high", ring, "ring", 4, [P, SPLIT, HK, HALF])
        low = alias("low", ring, "ring", 8, [P, SPLIT, HK, HALF])
        xT_high, xT_low, act_high, act_low = (
            alias(name, big, "big", 2 * i, [P, KT, CAP]) for i, name in enumerate(("xT_high", "xT_low", "act_high", "act_low")))
        bias_now = alias("bias_now", cfb, "cfb", 0, [P, 2, 2, HALF])
        raw = [ring[:, i, :].rearrange("p (k n) -> p k n", k=HK) for i in range(3)] + \
            [h_res[:, 2 * i:2 * i + 2, :].rearrange("p a (b n) -> p (a b) n", n=HALF) for i in range(3)]
        b1_split = [low[0:EXPERTS, i].rearrange("p k n -> p (k n)") for i in range(2)]
        b2_split = [high[0:EXPERTS, 2].rearrange("p k n -> p (k n)")[:, i * D:(i + 1) * D] for i in range(2)]
        x_rows = ring[:, 3, :].rearrange("p (t d) -> p t d", d=D)
        y_out = lrx
        glu = scr[:, 0, :].rearrange("p (t n) -> p t n", t=2)
        sig = scr[:, 1, :].rearrange("p (t n) -> p t n", t=2)
        lin = scr[:, 3, :].rearrange("p (t n) -> p t n", t=2)
        pick = scr[:, 2, :].bitcast(F16).rearrange("p (t s) -> p t s", t=TT)
        y_got = [big[:, 4 * i:4 * i + 4, :] for i in range(2)] + \
            [ring[:, 4 + 2 * i:6 + 2 * i, :].rearrange("p s (h d) -> p (s h) d", h=2) for i in range(GOT - 2)]

        ident = sb("ident", [P, P])
        eps_t = sb("eps_t", [P, 1])
        pad = sb("pad", [P, 16])
        chan_mean = sb("chan_mean", [P, P])
        before = sb("before", [P, P], BF16)
        ones = sb("ones", [P, P], BF16)
        chan = sb("chan", [P, CT, CHAN_ROWS])
        dpar = sb("dpar", [P, 2 * KT + 1])
        ones_r = sb("ones_r", [P, P], F32R)
        gate_w = sb("gate_w", [P, 2, CT, P])
        b2_now = [alias("b2_left", gate_w, "gate_w", 0, [P, HALF]), sb("b2_right", [P, HALF], F32R)]
        router = sb("router", [P, KT, EXPERTS])
        router_bias = sb("router_bias", [P, EXPERTS])
        lam_s = sb("lam_s", [P, 8])
        soft = sb("soft", [P, 6, CT])
        decay = sb("decay", [P, 2, CT])
        gain_o = sb("gain_o", [P, 1])
        stats = sb("stats", [P, 2, 12])
        mv = sb("mv", [P, TT, 2])
        std = sb("std", [P, TT])
        inv = sb("inv", [P, TT])
        shift = sb("shift", [P, TT])
        top = sb("top", [P, 2, 2])
        ntop = sb("ntop", [P, 2, 2])
        mass = sb("mass", [P, 2, 2])
        rmass = sb("rmass", [P, 4, 2])
        coef = sb("coef", [P, 2, 1])
        o_sq = sb("o_sq", [P, HEADS * TT])
        o_std = sb("o_std", [P, HEADS * TT])
        o_inv = sb("o_inv", [P, HEADS * TT])
        sq_out = sb("sq_out", [P, P])
        logits = sb("logits", [P, TT, EXPERTS])
        best = sb("best", [P, TT, 8])
        best_at = sb("best_at", [P, TT, 8], U32)
        chosen = sb("chosen", [P, TT, TOP_K])
        gates = sb("gates", [P, TT, TOP_K])
        gsum = sb("gsum", [P, TT])
        rank_of = sb("rank_of", [P, EXPERTS, TT])
        rank_now = sb("rank_now", [P, TT])
        count = sb("count", [P, EXPERTS])
        blocks = sb("blocks", [P, EXPERTS])
        ends = sb("ends", [P, EXPERTS])
        starts = sb("starts", [P, EXPERTS])
        dest = sb("dest", [P, TT, TOP_K])
        dest_i = sb("dest_i", [P, TT, TOP_K], I32)
        expert_f = sb("expert_f", [P, TABLE])
        offset_f = sb("offset_f", [P, TABLE])
        left_f = sb("left_f", [P, TABLE])
        expert_i = sb("expert_i", [1, TABLE], I32)
        left_i = sb("left_i", [1, TABLE], I32)
        row_f = sb("row_f", [P, 2, TABLE])
        row_i = sb("row_i", [1, TABLE], I32)
        ones_t = sb("ones_t", [P, TABLE])
        first = sb("first", [P, EXPERTS])
        ends_i = sb("ends_i", [1, EXPERTS], I32)
        token_no = sb("token_no", [P, TT], F16)
        iota_e = sb("iota_e", [P, EXPERTS])
        iota_g = sb("iota_g", [P, TABLE])
        iota_s = sb("iota_s", [P, CAP], F16)
        token_at = sb("token_at", [P, 2], I32)

        ps = ctx.enter_context(nc.psum_tensor("ps", [P, 8, HALF], F32))

        def bank(name):
            return ps[:, 4 + NUMBER[name] % 4, :]

        x_loaded = [sem(f"x_loaded{i}") for i in range(4)]
        dpar_loaded = sem("dpar_loaded")
        params_loaded = sem("params_loaded")
        gate_w_loaded = sem("gate_w_loaded")
        gather_go = sem("gather_go")
        w_loaded = [sem(f"w_loaded{i}") for i in range(FRONT_SLOTS)]
        raw_loaded = [sem(f"raw_loaded{i}") for i in range(RAW)]
        norm_loaded = [sem(f"norm_loaded{i}") for i in range(3)]
        const_ready = sem("const_ready")
        pool_step = sem("pool_step")
        dve_step = sem("dve_step")
        act_step = sem("act_step")
        job_full = sem("job_full")
        read_by = {"act": sem("read_by_act"), "dve": sem("read_by_dve")}
        eps_ready = sem("eps_ready")
        mean_ready = sem("mean_ready")
        std_ready = sem("std_ready")
        norm_ready = sem("norm_ready")
        normed = sem("normed")
        h_rows_ready = sem("h_rows_ready")
        glu_cf = sem("glu_cf")
        conv_out = sem("conv_out")
        squared = sem("squared")
        cf_scaled = sem("cf_scaled")
        cf_ready = sem("cf_ready")
        xc_ready = sem("xc_ready")
        decays = sem("decays")
        one_minus = sem("one_minus")
        root = sem("root")
        lru_ready = sem("lru_ready")
        decay_ready = sem("decay_ready")
        soft_s = sem("soft_s")
        lam_s1 = sem("lam_s1")
        alibi_ready = sem("alibi_ready")
        score_full = sem("score_full")
        score_read = sem("score_read")
        top_ready = sem("top_ready")
        exp_ready = sem("exp_ready")
        map_ready = sem("map_ready")
        o_ready = sem("o_ready")
        o_root = sem("o_root")
        o_scaled = sem("o_scaled")
        mix_mean = sem("mix_mean")
        mix_std = sem("mix_std")
        mix_norm = sem("mix_norm")
        mix_normed = sem("mix_normed")
        h1_gain = sem("h1_gain")
        h1_ready = sem("h1_ready")
        h1_stored = sem("h1_stored")
        gate_diff = sem("gate_diff")
        gate_exp = sem("gate_exp")
        mask_ready = sem("mask_ready")
        alpha_ready = sem("alpha_ready")
        tables_ready = sem("tables_ready")
        resid_ready = sem("resid_ready")
        pick_ready = sem("pick_ready")
        slots_full = sem("slots_full")
        slots_ready = sem("slots_ready")
        x_got = sem("x_got")
        xT_full = sem("xT_full")
        xT_read = sem("xT_read")
        high_ready = sem("high_ready")
        low_by_dve = sem("low_by_dve")
        low_by_pool = sem("low_by_pool")
        xT_high_ready = sem("xT_high_ready")
        act_rows = sem("act_rows")
        aT_full = sem("aT_full")
        aT_high_ready = sem("aT_high_ready")
        aT_read = sem("aT_read")
        piece_done = sem("piece_done")
        hidden_read = sem("hidden_read")
        sig_ready = sem("sig_ready")
        swish_step = sem("swish_step")
        y_read = sem("y_read")
        y_stored = sem("y_stored")
        rank_step = sem("rank_step")
        b1_high = sem("b1_high")
        b1_low = sem("b1_low")
        b1_stored = sem("b1_stored")
        b1_loaded = sem("b1_loaded")
        b2_loaded = sem("b2_loaded")
        ones_r_ready = sem("ones_r_ready")
        got = [sem(f"got{i}") for i in range(GOT * TOP_K)]
        summed = sem("summed")
        fin_std = sem("fin_std")
        fin_norm = sem("fin_norm")
        fin_normed = sem("fin_normed")
        fin_gain = sem("fin_gain")
        out_ready = sem("out_ready")
        out_stored = sem("out_stored")

        def by_tiles(eng, g, body):
            left, left_after = (eng.value_load(left_i[0:1, bass.ds(at, 1)], min_val=-BIG, max_val=BIG)
                                for at in (g, g + 1))
            with eng.If(left < P + 1):
                with eng.If(left_after < P + 1):
                    body(TILES[0], TILES[0])
                with eng.Else():
                    body(TILES[0], TILES[1])
            with eng.Else():
                with eng.If(left_after < P + 1):
                    body(TILES[1], TILES[0])
                with eng.Else():
                    body(TILES[1], TILES[1])

        LAST_USE = {p: ("v", TT - 1) if p[0] == "v" else ("in", p, CT - 1, 1) for p in IN_PIECES}
        USES = [sum(n % FRONT_SLOTS == i for n in range(len(IN_PIECES))) for i in range(FRONT_SLOTS)]
        BEFORE = [16 * (uses + 1) for uses in USES]
        PARAM_LOADS = 16 * 17

        def by_pool(n):
            return n % POOL_TURN == POOL_TURN - 1

        def raw_count(g, n):
            return g * (16 * PIECES // RAW) + 16 * (n // RAW + 1)

        def high_count(g, n):
            return g * PIECES + (n + 1)

        def wait_low(eng, g, n):
            if by_pool(n):
                eng.wait_ge(low_by_pool, g * (PIECES // POOL_TURN) + (n // POOL_TURN + 1))
            else:
                eng.wait_ge(low_by_dve, g * (2 * PIECES // POOL_TURN) + (2 * (n // POOL_TURN) + n % POOL_TURN + 1))

        def split_low(eng, ops, g, n):
            eng.wait_ge(high_ready, high_count(g, n))
            ops.tensor_tensor(low[:, n % SPLIT], raw[n % RAW], high[:, n % SPLIT].bitcast(F32),
                              ALU.subtract).then_inc(low_by_pool if by_pool(n) else low_by_dve, 1)

        block = ctx.enter_context(nc.Block())

        def full(eng, name):
            eng.wait_ge(job_full, NUMBER[name] + 1)

        def was_read(eng, name):
            eng.wait_ge(read_by[READER[name]], ORDINAL[name] + 1)


        @block.sync
        def _(sp):
            def w_in_piece(i):
                name = IN_PIECES[i]
                if i >= FRONT_SLOTS:
                    full(sp, LAST_USE[IN_PIECES[i - FRONT_SLOTS]])
                c = IN_COLUMN[name]
                sp.dma_start(slot(i % FRONT_SLOTS), w_in_v[:, :, c:c + PIECE]).then_inc(w_loaded[i % FRONT_SLOTS], 16)

            for i in range(4):
                sp.dma_start(x_in[:, 2 * i:2 * i + 2, :], x_tiles[:, 2 * i:2 * i + 2, :]).then_inc(x_loaded[i], 16)
            for i in range(len(IN_PIECES)):
                w_in_piece(i)
                if i == 1:
                    sp.dma_start(norm_rows[:, 0, :], ln_in_g.partition_broadcast(P)).then_inc(norm_loaded[0], 16)
                    sp.dma_start(norm_rows[:, 1, :], ln_in_b.partition_broadcast(P)).then_inc(norm_loaded[0], 16)
            for i in range(4):
                last = max(n for n in range(len(IN_PIECES)) if n % FRONT_SLOTS == i)
                full(sp, LAST_USE[IN_PIECES[last]])
                sp.dma_start(slot(i), w_out_v[:, :, i * PIECE:(i + 1) * PIECE]).then_inc(w_loaded[i], 16)
            full(sp, ("o",) + UNITS[-1])
            sp.wait_ge(score_read, 2 * len(UNITS))
            sp.dma_start(norm_rows[:, 0, :], ln1_g[0].partition_broadcast(P)).then_inc(norm_loaded[1], 16)
            sp.dma_start(norm_rows[:, 1, :], ln1_b[0].partition_broadcast(P)).then_inc(norm_loaded[1], 16)

            def expert_piece(e, n):
                p = n % PIECES
                if p < 8:
                    c, kh = (p // 2 % 2) * D + (p // 4) * HALF, p % 2
                    src = w1_v[e, :, HK * kh:HK * (kh + 1), c:c + HALF]
                else:
                    c, kh = (p % 2) * HALF, (p - 8) // 2
                    src = w2_v[e, :, HK * kh:HK * (kh + 1), c:c + HALF]
                if not isinstance(e, int):
                    src = src.rearrange("a p k n -> (a p) k n")
                sp.dma_start(raw[n % RAW], src).then_inc(raw_loaded[n % RAW], 16)

            for t in range(TT):
                sp.wait_ge(h1_ready, t + 1)
                sp.dma_start(h1_tiles[:, t, :], h_res[:, t, :]).then_inc(h1_stored, 16)
            full(sp, ("mix", TT - 1, 1))
            for n in range(3):
                expert_piece(0, n)
            sp.wait_ge(h1_stored, 16 * TT)
            full(sp, ("h1T", TT - 1, 1))
            for n in range(3, RAW):
                expert_piece(0, n)
            sp.wait_ge(tables_ready, 1)
            total = sp.value_load(ends_i[0:1, EXPERTS - 1:EXPERTS], min_val=EXPERTS, max_val=MAX_BLOCKS)
            with sp.Fori(0, total) as g:
                now = sp.value_load(expert_i[0:1, bass.ds(g, 1)], min_val=0, max_val=EXPERTS - 1)
                after = sp.value_load(expert_i[0:1, bass.ds(g + 1, 1)], min_val=0, max_val=EXPERTS - 1)
                for n in range(RAW, RAW + PIECES):
                    wait_low(sp, g, n - RAW)
                    expert_piece(bass.ds(now if n < PIECES else after, 1), n)
            sp.wait_ge(y_stored, total * 32 + 32)
            sp.dma_start(norm_rows[:, 0, :], ln2_g[0].partition_broadcast(P)).then_inc(norm_loaded[2], 16)
            wait_low(sp, total, 3)
            sp.dma_start(norm_rows[:, 1, :], ln2_b[0].partition_broadcast(P)).then_inc(norm_loaded[2], 16)
            for i in range(3):
                sp.wait_ge(raw_loaded[3 + i], total * 32 + 16)
                sp.dma_start(h_res[:, 2 * i:2 * i + 2, :], h1_tiles[:, 2 * i:2 * i + 2, :]).then_inc(x_loaded[i], 16)
            for t in range(TT):
                sp.wait_ge(out_ready, t + 1)
                sp.dma_start(out_tiles[:, t, :], h_res[:, t, :]).then_inc(out_stored, 16)
            sp.wait_ge(out_stored, 16 * TT)
            sp.wait_ge(h1_stored, 16 * TT)

        @block.gpsimd
        def _(pool):
            n = [0]

            def step(ins):
                n[0] += 1
                ins.then_inc(pool_step, 1)
                pool.wait_ge(pool_step, n[0])

            step(nc.gpsimd.memset(ident[:, :], 0.0))
            nc.gpsimd.affine_select(out=ident[:, :], in_=ident[:, :], compare_op=ALU.not_equal, fill=1.0,
                                    base=0, pattern=[[-1, P]], channel_multiplier=1).then_inc(const_ready, 1)
            step(nc.gpsimd.memset(gate_w[:, :, :, :], 0.0))
            for w, src in enumerate((lru_wa, lru_wx)):
                for i in range(CT):
                    for b in range(2):
                        pool.dma_start(gate_w[64 * b:64 * b + 64, w, i, 64 * b:64 * b + 64],
                                       src[0, 2 * i + b]).then_inc(gate_w_loaded, 16)
            nc.gpsimd.memset(chan_mean[:, :], 1.0 / GROUP)
            nc.gpsimd.memset(ones_t[:, :], 1.0)
            step(nc.gpsimd.memset(ones[:, :], 1.0))
            nc.gpsimd.affine_select(out=before[:, :], in_=ones[:, :], compare_op=ALU.is_gt, fill=0.0,
                                    base=0, pattern=[[1, P]], channel_multiplier=-1)
            nc.gpsimd.iota(iota_e[:, :], pattern=[[1, EXPERTS]], base=0, channel_multiplier=0,
                           allow_small_or_imprecise_dtypes=True)
            nc.gpsimd.iota(iota_g[:, :], pattern=[[1, TABLE]], base=0, channel_multiplier=0,
                           allow_small_or_imprecise_dtypes=True)
            nc.gpsimd.iota(iota_s[:, :], pattern=[[1, CAP]], base=0, channel_multiplier=0,
                           allow_small_or_imprecise_dtypes=True)
            nc.gpsimd.iota(token_no[:, :], pattern=[[P, TT]], base=0, channel_multiplier=1,
                           allow_small_or_imprecise_dtypes=True).then_inc(const_ready, 1)

            pool.wait_ge(b1_high, 1)
            nc.gpsimd.tensor_tensor(b1_split[1], b1_rows, b1_split[0].bitcast(F32), ALU.subtract)
            nc.gpsimd.tensor_tensor(b2_split[1], b2_rows, b2_split[0].bitcast(F32), ALU.subtract).then_inc(b1_low, 1)

            pool.wait_ge(norm_loaded[0], 32)
            full(pool, ("hT", 1, KT - 1))
            for t in range(TT):
                step(nc.gpsimd.tensor_tensor(h_res[:, t, :], h_res[:, t, :], norm_rows[:, 0, :], ALU.mult))
                nc.gpsimd.tensor_tensor(h_res[:, t, :], h_res[:, t, :], norm_rows[:, 1, :],
                                        ALU.add).then_inc(h_rows_ready, 1)

            pool.wait_ge(lru_ready, 2)
            step(nc.gpsimd.iota(alibi, pattern=[[1, S]], base=-(S - P), channel_multiplier=-1,
                                allow_small_or_imprecise_dtypes=True))
            step(nc.gpsimd.affine_select(out=alibi, in_=alibi, compare_op=ALU.is_ge, fill=MASKED,
                                         base=S - P, pattern=[[-1, S]], channel_multiplier=1))
            for h in range(HEADS):
                if h >= 2:
                    pool.wait_ge(score_read, 2 * TT * (h - 1))
                nc.gpsimd.tensor_scalar(scr[:, h % 2, :], alibi, SLOPES[h] / SCALE, None,
                                        ALU.mult).then_inc(alibi_ready, 1)

            def held():
                pool.sem_inc(gather_go, 1)

            def gather(g):
                for th in range(2):
                    pool.indirect_dma_start(
                        out=x_rows[:, th, :], out_offset=None, in_=h1_rows[:, :],
                        in_offset=bass.IndirectOffsetOnAxis(ap=token_at[:, th:th + 1], axis=0)
                    ).then_inc(x_got, 16)

            def load_b1(src):
                pool.dma_start(bias_now[0:2, :, :, :], src.rearrange("r (a h n) -> r a h n", a=2, h=2))\
                    .then_inc(b1_loaded, 16)

            pool.wait_ge(h1_stored, 16 * TT)
            full(pool, ("mix", TT - 1, 1))
            pool.wait_ge(b1_stored, 64)
            load_b1(b1_parts[0, :, :])
            split_low(pool, nc.gpsimd, 0, 0)
            split_low(pool, nc.gpsimd, 0, 1)
            pool.wait_ge(slots_ready, 1)
            gather(0)
            split_low(pool, nc.gpsimd, 0, 2)
            split_low(pool, nc.gpsimd, 0, 3)
            pool.wait_ge(tables_ready, 1)
            total = pool.value_load(ends_i[0:1, EXPERTS - 1:EXPERTS], min_val=EXPERTS, max_val=MAX_BLOCKS)
            with pool.Fori(0, total) as g:
                now = pool.value_load(expert_i[0:1, bass.ds(g, 1)], min_val=0, max_val=EXPERTS - 1)
                after = pool.value_load(expert_i[0:1, bass.ds(g + 1, 1)], min_val=0, max_val=EXPERTS - 1)

                def of(parts, e):
                    return parts[bass.ds(e, 1), :, :].rearrange("a r n -> (a r) n")

                pool.wait_ge(y_read, g * 2 + 2)
                held()
                for c in range(2):
                    pool.dma_start(b2_now[c][0:2, :], of(b2_parts, now)[:, c * HALF:(c + 1) * HALF]).then_inc(b2_loaded, 16)
                split_low(pool, nc.gpsimd, g, 5)
                pool.wait_ge(xT_full, g + 1)
                pool.wait_ge(slots_ready, g + 2)
                held()
                gather(g + 1)
                split_low(pool, nc.gpsimd, g, 8)
                pool.wait_ge(piece_done, g * PIECES + 7)
                held()
                load_b1(of(b1_parts, after))
                split_low(pool, nc.gpsimd, g, 11)
                split_low(pool, nc.gpsimd, g, 14)

            pool.wait_ge(xT_read, total + 1)
            pool.wait_ge(x_got, total * 32 + 32)
            pool.wait_ge(b1_loaded, total * 16 + 16)
            pool.wait_ge(low_by_dve, total * 8 + 3)
            pool.wait_ge(low_by_pool, total * 4 + 1)
            pool.wait_ge(y_stored, total * 32 + 32)
            held()

            def gather_rows(t):
                if t >= GOT:
                    pool.wait_ge(summed, t - GOT + 1)
                for k in range(TOP_K):
                    pool.indirect_dma_start(
                        out=y_got[t % GOT][:, k, :], out_offset=None, in_=y_rows[0:S * TOP_K, :],
                        in_offset=bass.IndirectOffsetOnAxis(ap=dest_i[:, t, k:k + 1], axis=0)
                    ).then_inc(got[TOP_K * (t % GOT) + k], 16)

            for t in range(GOT):
                gather_rows(t)
            for t in range(TT):
                if t + GOT < TT:
                    gather_rows(t + GOT)
                if not t:
                    pool.wait_ge(norm_loaded[2], 32)
                pool.wait_ge(fin_normed, t + 1)
                nc.gpsimd.tensor_tensor(h_res[:, t, :], h_res[:, t, :], norm_rows[:, 0, :], ALU.mult).then_inc(fin_gain, 1)

        @block.scalar
        def _(act):
            n = [0]

            def step(ins):
                n[0] += 1
                ins.then_inc(act_step, 1)
                act.wait_ge(act_step, n[0])

            for dst, src in ((dpar_rows[0:KT, :], ln_in_g.rearrange("(k p) -> k p", p=P)),
                             (dpar_rows[KT:2 * KT, :], ln_in_b.rearrange("(k p) -> k p", p=P)),
                             (dpar_rows[2 * KT:2 * KT + 1, :], subln_g)):
                act.dma_start(dst, src).then_inc(dpar_loaded, 16)
            loads = [
                (chan_rows[ROW_LRU_W:ROW_LRU_W + LRU_TAPS, :], lru_conv_w[0]), (chan_rows[ROW_LRU_B:ROW_LRU_B + 1, :], lru_conv_b),
                (chan_rows[ROW_BA:ROW_BA + 1, :], lru_ba), (chan_rows[ROW_BX:ROW_BX + 1, :], lru_bx),
                (chan_rows[ROW_LAMBDA:ROW_LAMBDA + 1, :], lru_lambda),
                (chan_rows[ROW_CF_W:ROW_CF_W + CF_TAPS, :], cf_conv_w[0]), (chan_rows[ROW_CF_B:ROW_CF_B + 1, :], cf_conv_b),
                (chan_rows[ROW_CF_G:ROW_CF_G + 1, :], cf_ln_g), (chan_rows[ROW_CF_BETA:ROW_CF_BETA + 1, :], cf_ln_b),
                (b1_rows, moe_b1[0]), (b2_rows, moe_b2[0]),
                (router[:, :, :], router_w[0].rearrange("(k p) e -> p k e", p=P)),
                (router_bias[:, :], router_b[0].partition_broadcast(P)),
            ] + [(lam_in[:, i, :], a[0].partition_broadcast(P)) for i, a in enumerate((lam_q1, lam_k1, lam_q2, lam_k2))]
            for dst, src in loads:
                act.dma_start(dst, src).then_inc(params_loaded, 16)

            def finish(ins, name):
                ins.then_inc(read_by["act"], 1)

            act.wait_ge(eps_ready, 1)
            for hf in range(2):
                act.wait_ge(mean_ready, hf + 1)
                nc.scalar.activation(std[:, 4 * hf:4 * hf + 4], mv[:, 4 * hf:4 * hf + 4, 1], ACT.Sqrt,
                                     bias=eps_t[:, 0:1]).then_inc(std_ready, 1)
                act.wait_ge(norm_ready, hf + 1)
                for t in range(4 * hf, 4 * hf + 4):
                    nc.scalar.activation(h_res[:, t, :], x_in[:, t, :], ACT.Identity, bias=shift[:, t:t + 1],
                                         scale=inv[:, t:t + 1]).then_inc(normed, 1)

            full(act, "dpar")
            finish(nc.scalar.copy(dpar[:, :], bank("dpar")[:, 0:2 * KT + 1]), "dpar")
            act.wait_ge(read_by["act"], ORDINAL["dpar"] + 1)
            step(nc.scalar.mul(gain_o[:, :], dpar[:, 2 * KT:2 * KT + 1], 1.0 - LAM_INIT))

            def hT_read(hf, k):
                full(act, ("hT", hf, k))
                finish(nc.scalar.activation(hT[:, k, hf * HALF:(hf + 1) * HALF], bank(("hT", hf, k)), ACT.Identity,
                                            bias=dpar[:, KT + k:KT + k + 1], scale=dpar[:, k:k + 1]), None)

            for k in range(1, KT, 2):
                hT_read(0, k)

            def in_read(p, c, h):
                name = ("in", p, c, h)
                cols = slice(h * HALF, (h + 1) * HALF)
                full(act, name)
                if p == "cf_a":
                    finish(nc.scalar.copy(cfa[:, c, cols], bank(name)), name)
                elif p == "cf_b":
                    finish(nc.scalar.activation(cfb[:, c, cols], bank(name), ACT.Sigmoid), name)
                elif p == "lru_x":
                    finish(nc.scalar.copy(lrx[:, c, cols], bank(name)), name)
                elif p == "lru_y":
                    finish(nc.scalar.activation(lry[:, c, cols], bank(name), ACT.Gelu_apprx_tanh), name)
                else:
                    dst = qT if p[0] == "q" else kT
                    if (p, c, h) == ("q0", 0, 0):
                        act.wait_ge(b1_stored, 64)
                    finish(nc.scalar.copy(dst[:, 2 * int(p[1]) + c, cols], bank(name)), name)

            def v_read(t):
                full(act, ("v", t))
                finish(nc.scalar.copy(v[:, t, :], bank(("v", t))), None)

            def gate_read(i):
                for w, dst, row in (("a", ga, ROW_BA), ("x", gx, ROW_BX)):
                    for h in range(2):
                        full(act, ("gate", i, w, h))
                        if i and w == "a" and not h:
                            act.wait_ge(lru_ready, i)
                        finish(nc.scalar.activation(dst[:, h * HALF:(h + 1) * HALF], bank(("gate", i, w, h)),
                                                    ACT.Sigmoid, bias=chan[:, i, row:row + 1]), None)
                act.wait_ge(read_by["act"], ORDINAL[("gate", i, "x", 1)] + 1)
                if not i:
                    act.wait_ge(decay_ready, 1)
                step(nc.scalar.activation(mul, ga, ACT.Exp, scale=decay[:, 1, i:i + 1]))
                nc.scalar.activation(ga, ga, ACT.Exp, scale=decay[:, 0, i:i + 1]).then_inc(decays, 1)
                act.wait_ge(one_minus, i + 1)
                nc.scalar.activation(mul, mul, ACT.Sqrt).then_inc(root, 1)

            for p in ("cf_a", "cf_b"):
                for c in range(CT):
                    in_read(p, c, 0)
            for k in range(1, KT, 2):
                hT_read(1, k)
            full(act, "chan")
            finish(nc.scalar.copy(chan[:, :, :], bank("chan")[:, 0:CT * CHAN_ROWS].rearrange("p (i r) -> p i r", i=CT)), "chan")
            act.wait_ge(params_loaded, PARAM_LOADS)
            lam_c = chan[:, :, ROW_LAMBDA]
            act.wait_ge(soft_s, 1)
            nc.scalar.activation(soft[:, 1, :], soft[:, 0, :], ACT.Exp).then_inc(soft_s, 1)
            act.wait_ge(soft_s, 3)
            nc.scalar.activation(soft[:, 3, :], soft[:, 2, :], ACT.Ln).then_inc(soft_s, 1)
            act.wait_ge(lam_s1, 1)
            nc.scalar.activation(lam_s[:, 2:4], lam_s[:, 0:2], ACT.Exp).then_inc(lam_s1, 1)
            nc.scalar.copy(b1_split[0], b1_rows)
            nc.scalar.copy(b2_split[0], b2_rows).then_inc(b1_high, 1)
            act.wait_ge(const_ready, 2)
            nc.scalar.copy(ones_r[0:2, :], ones[0:2, :]).then_inc(ones_r_ready, 1)
            for p in ("cf_a", "cf_b"):
                for c in range(CT):
                    in_read(p, c, 1)
            for p in ("lru_x", "lru_y"):
                for c in range(CT):
                    for h in range(2):
                        in_read(p, c, h)
            act.wait_ge(b1_low, 1)
            for i in range(2):
                act.dma_start(b1_parts[:, i, :], b1_split[i].bitcast(F32)).then_inc(b1_stored, 16)
                act.dma_start(b2_parts[:, i, :], b2_split[i].bitcast(F32)).then_inc(b1_stored, 16)
            for t in range(6):
                v_read(t)
            gate_read(0)
            for h in range(2):
                was_read(act, ("mean", h))
                nc.scalar.activation(cfa[:, :, h * HALF:(h + 1) * HALF], cfb[:, :, h * HALF:(h + 1) * HALF],
                                     ACT.Square).then_inc(squared, 1)
            v_read(6)
            v_read(7)
            for h in range(2):
                if not h:
                    full(act, ("var", 1))
                finish(nc.scalar.activation(cfa[:, 0, h * HALF:(h + 1) * HALF], bank(("var", h)), ACT.Sqrt,
                                            bias=eps_t[:, 0:1]), None)
            for c in range(CT):
                for h in range(2):
                    in_read("q0", c, h)
            gate_read(1)
            act.wait_ge(cf_scaled, 1)
            for i in range(CT):
                nc.scalar.activation(cfb[:, i, :], cfb[:, i, :], ACT.Silu, bias=chan[:, i, ROW_CF_BETA:ROW_CF_BETA + 1],
                                     scale=chan[:, i, ROW_CF_G:ROW_CF_G + 1]).then_inc(cf_ready, 1)
            for p in ("q1", "k0", "k1"):
                for c in range(CT):
                    for h in range(2):
                        in_read(p, c, h)

            def exps(u):
                h, q = UNITS[u]
                act.wait_ge(top_ready, u + 1)
                for c in range(2):
                    m = maps[:, u % 2, c, 0:(q + 1) * P]
                    nc.scalar.activation(m, m, ACT.Exp, bias=ntop[:, u % 2, c:c + 1], scale=SCALE,
                                         accum_out=mass[:, u % 2, c:c + 1]).then_inc(exp_ready, 1)

            def map_read(u):
                h, q = UNITS[u]
                for g in range(q // 4 + 1):
                    k = min(4, q + 1 - 4 * g)
                    full(act, ("pT", h, q, g))
                    finish(nc.scalar.copy(pT[:, u % 2, 4 * g:4 * g + k, :],
                                          bank(("pT", h, q, g))[:, 0:k * P].rearrange("p (k q) -> p k q", q=P)), None)

            exps(0)
            for u in range(len(UNITS)):
                if u + 1 < len(UNITS):
                    exps(u + 1)
                map_read(u)
            act.wait_ge(o_ready, HEADS * TT)
            nc.scalar.activation(o_std[:, :], o_sq[:, :], ACT.Sqrt, bias=eps_t[:, 0:1], scale=1.0 / DV).then_inc(o_root, 1)
            for h in range(HEADS):
                for g in range(2):
                    full(act, ("oT", h, g))
                    finish(nc.scalar.activation(oT[:, h, g * HALF:(g + 1) * HALF], bank(("oT", h, g)), ACT.Copy,
                                                scale=gain_o[:, 0:1]), None)

            def h1T_read(t):
                for g in range(2):
                    full(act, ("h1T", t, g))
                    finish(nc.scalar.copy(h1T[:, 4 * g:4 * g + 4, :],
                                          bank(("h1T", t, g)).rearrange("p (k q) -> p k q", q=P)), None)

            for t in range(TT):
                if t:
                    h1T_read(t - 1)
                act.wait_ge(mix_mean, t + 1)
                nc.scalar.activation(std[:, t:t + 1], mv[:, t, 1:2], ACT.Sqrt, bias=eps_t[:, 0:1]).then_inc(mix_std, 1)
                act.wait_ge(mix_norm, t + 1)
                nc.scalar.activation(h_res[:, t, :], h_res[:, t, :], ACT.Identity, bias=shift[:, t:t + 1],
                                     scale=inv[:, t:t + 1]).then_inc(mix_normed, 1)
            h1T_read(TT - 1)

            def split_high(g, n):
                act.wait_ge(raw_loaded[n % RAW], raw_count(g, n))
                if n >= SPLIT:
                    act.wait_ge(piece_done, g * PIECES + (n - SPLIT + 1))
                nc.scalar.copy(high[:, n % SPLIT], raw[n % RAW]).then_inc(high_ready, 1)

            def xT_read_high(g, tiles):
                act.wait_ge(xT_full, g + 1)
                nc.scalar.copy(xT_high[:, :, 0:tiles * P].rearrange("p k (t n) -> p t k n", n=P),
                               ps[:, 4:4 + 2 * tiles, :].rearrange("p (t b) (k n) -> p t (b k) n", b=2, n=P))\
                    .then_inc(xT_high_ready, 1)

            for n in range(3):
                split_high(0, n)
            act.wait_ge(gate_diff, 1)
            nc.scalar.activation(gates[:, :, :], gates[:, :, :], ACT.Exp).then_inc(gate_exp, 1)

            nc.scalar.copy(pad[:, 3:4], eps_t[:, :]).then_inc(y_read, 2)
            nc.scalar.copy(pad[:, 4:5], eps_t[:, :]).then_inc(y_stored, 32)
            split_high(0, 3)
            xT_read_high(0, 2)
            act.wait_ge(tables_ready, 1)
            total = act.value_load(ends_i[0:1, EXPERTS - 1:EXPERTS], min_val=EXPERTS, max_val=MAX_BLOCKS)
            with act.Fori(0, total) as g:
                row = act.value_load(row_i[0:1, bass.ds(g, 1)], min_val=0, max_val=S * TOP_K)

                def body(tiles, ahead):
                    def sigmoid(c):
                        act.wait_ge(hidden_read, g * 4 + (2 * c + 1))
                        if c:
                            act.wait_ge(act_rows, g * 2 + c)
                        nc.scalar.activation(sig[:, 0:tiles, :], glu[:, 0:tiles, :], ACT.Sigmoid,
                                             scale=SWIGLU_ALPHA).then_inc(sig_ready, 1)

                    def aT_read_high(c):
                        act.wait_ge(aT_full, g * 2 + (c + 1))
                        dst = act_high[:, HK * c:HK * (c + 1), 0:tiles * P].rearrange("p k (t n) -> p t k n", n=P)
                        src = ps[:, 4 + 2 * c:4 + 2 * c + tiles, :].rearrange("p t (k n) -> p t k n", n=P)
                        nc.scalar.copy(dst, src).then_inc(aT_high_ready, 1)

                    def y_take(c):
                        act.wait_ge(piece_done, g * PIECES + (11 + c))
                        nc.scalar.copy(y_out[:, 0:tiles, c * HALF:(c + 1) * HALF],
                                       ps[:, 2 * c:2 * c + tiles, :]).then_inc(y_read, 1)

                    split_high(g, 4)
                    split_high(g, 5)
                    sigmoid(0)
                    split_high(g, 6)
                    split_high(g, 7)
                    split_high(g, 8)
                    split_high(g, 9)
                    aT_read_high(0)
                    sigmoid(1)
                    split_high(g, 10)
                    split_high(g, 11)
                    aT_read_high(1)
                    split_high(g, 12)
                    xT_read_high(g + 1, ahead)
                    split_high(g, 13)
                    act.wait_ge(y_stored, g * 32 + 32)
                    y_take(0)
                    split_high(g, 14)
                    y_take(1)
                    split_high(g, 15)
                    act.wait_ge(y_read, g * 2 + 4)
                    if tiles > 1:
                        act.dma_start(y_rows[bass.ds(row + P, P), :], y_out[:, 1, :]).then_inc(y_stored, 16)
                    else:
                        act.sem_inc(y_stored, 16)
                    act.dma_start(y_rows[bass.ds(row, P), :], y_out[:, 0, :]).then_inc(y_stored, 16)

                by_tiles(act, g, body)

            for t in range(TT):
                if t < 6:
                    act.wait_ge(x_loaded[t // 2], 32)
                nc.scalar.mul(h_res[:, t, :], h_res[:, t, :], ALPHA).then_inc(alpha_ready, 1)
            for t in range(TT):
                act.wait_ge(summed, t + 1)
                nc.scalar.activation(std[:, t:t + 1], mv[:, t, 1:2], ACT.Sqrt, bias=eps_t[:, 0:1]).then_inc(fin_std, 1)
                act.wait_ge(fin_norm, t + 1)
                nc.scalar.activation(h_res[:, t, :], h_res[:, t, :], ACT.Identity, bias=shift[:, t:t + 1],
                                     scale=inv[:, t:t + 1]).then_inc(fin_normed, 1)

        @block.vector
        def _(dve):
            V = nc.vector
            n = [0]

            def mark(ins):
                n[0] += 1
                ins.then_inc(dve_step, 1)

            def settle(behind=0):
                dve.wait_ge(dve_step, n[0] - behind)

            def step(ins):
                mark(ins)
                settle()

            def finish(ins):
                ins.then_inc(read_by["dve"], 1)

            V.memset(eps_t[:, :], EPS).then_inc(eps_ready, 1)

            def row_stats(src, t):
                for c in range(2):
                    mark(V.bn_stats(stats[:, t % 2, 6 * c:6 * c + 6], src[:, c * HALF:(c + 1) * HALF]))
                settle()
                return V.bn_aggr(mv[:, t, :], stats[:, t % 2, :])

            def norm_terms(a, b):
                step(V.reciprocal(inv[:, a:b], std[:, a:b]))
                return V.scalar_tensor_tensor(shift[:, a:b], mv[:, a:b, 0], -1.0, inv[:, a:b], ALU.mult, ALU.mult)

            for hf in range(2):
                for t in range(4 * hf, 4 * hf + 4):
                    dve.wait_ge(x_loaded[t // 2], 16)
                    last = row_stats(x_in[:, t, :], t)
                    if t % 4 < 3:
                        mark(last)
                    else:
                        last.then_inc(mean_ready, 1)
                dve.wait_ge(mean_ready, hf + 1)
                dve.wait_ge(std_ready, hf + 1)
                norm_terms(4 * hf, 4 * hf + 4).then_inc(norm_ready, 1)

            was_read(dve, "dpar")

            def hT_read(hf, k):
                full(dve, ("hT", hf, k))
                finish(V.tensor_scalar(hT[:, k, hf * HALF:(hf + 1) * HALF], bank(("hT", hf, k)),
                                       dpar[:, k:k + 1], dpar[:, KT + k:KT + k + 1], ALU.mult, ALU.add))

            for hf in range(2):
                for k in range(0, KT, 2):
                    hT_read(hf, k)

            dve.wait_ge(params_loaded, PARAM_LOADS)
            for i in range(2):
                ins = V.tensor_tensor_reduce(out=sq_out[:, 0:DK], in0=lam_in[:, 2 * i, :], in1=lam_in[:, 2 * i + 1, :],
                                             scale=1.0, scalar=0.0, op0=ALU.mult, op1=ALU.add,
                                             accum_out=lam_s[:, i:i + 1])
                if i:
                    ins.then_inc(lam_s1, 1)
                else:
                    step(ins)
            was_read(dve, "chan")
            lam_c = chan[:, :, ROW_LAMBDA]
            step(V.tensor_scalar(soft[:, 4, :], lam_c, -1.0, None, ALU.mult))
            V.tensor_tensor(soft[:, 0, :], lam_c, soft[:, 4, :], ALU.min).then_inc(soft_s, 1)
            dve.wait_ge(soft_s, 2)
            V.tensor_scalar(soft[:, 2, :], soft[:, 1, :], 1.0, None, ALU.add).then_inc(soft_s, 1)
            dve.wait_ge(soft_s, 4)
            step(V.tensor_scalar(soft[:, 5, :], soft[:, 2, :], -1.0, 1e-30, ALU.add, ALU.max))
            step(V.reciprocal(soft[:, 5, :], soft[:, 5, :]))
            step(V.tensor_tensor(soft[:, 5, :], soft[:, 5, :], soft[:, 3, :], ALU.mult))
            step(V.scalar_tensor_tensor(soft[:, 2, :], soft[:, 2, :], 1.0, soft[:, 5, :], ALU.is_equal, ALU.add))
            step(V.tensor_tensor(soft[:, 2, :], soft[:, 2, :], soft[:, 1, :], ALU.mult))
            step(V.scalar_tensor_tensor(soft[:, 2, :], soft[:, 4, :], 0.0, soft[:, 2, :], ALU.max, ALU.add))
            V.tensor_scalar(decay[:, 0, :], soft[:, 2, :], -LRU_C, None, ALU.mult)
            V.tensor_scalar(decay[:, 1, :], soft[:, 2, :], -2.0 * LRU_C, None, ALU.mult).then_inc(decay_ready, 1)
            dve.wait_ge(lam_s1, 2)
            step(V.tensor_tensor(lam_s[:, 4:5], lam_s[:, 3:4], lam_s[:, 2:3], ALU.subtract))
            step(V.tensor_scalar(lam_s[:, 5:6], lam_s[:, 4:5], -LAM_INIT, None, ALU.add))
            neg_lam = lam_s[:, 5:6]

            was_read(dve, ("in", "cf_b", 1, 1))
            for i in range(CT):
                mark(V.tensor_tensor(cfa[:, i, :], cfa[:, i, :], cfb[:, i, :], ALU.mult))
            settle()

            def tap(out_t, in_t, i, row, back, first_bias=None):
                w = chan[:, i, row:row + 1]
                if first_bias is not None:
                    return V.tensor_scalar(out_t, in_t, w, chan[:, i, first_bias:first_bias + 1], ALU.mult, ALU.add)
                return V.scalar_tensor_tensor(out_t[:, back:], in_t[:, :S - back], w, out_t[:, back:], ALU.mult, ALU.add)

            for j in range(CF_TAPS):
                for i in range(CT):
                    if j:
                        settle(behind=1)
                    mark(tap(cfb[:, i, :], cfa[:, i, :], i, ROW_CF_W + CF_TAPS - 1 - j, j, None if j else ROW_CF_B))
            settle(behind=1)
            settle()
            V.engine_nop().then_inc(conv_out, 1)

            def lru_conv(i):
                for j in range(LRU_TAPS):
                    ins = tap(xc, lrx[:, i, :], i, ROW_LRU_W + LRU_TAPS - 1 - j, j, None if j else ROW_LRU_B)
                    if j < LRU_TAPS - 1:
                        step(ins)
                    else:
                        ins.then_inc(xc_ready, 1)

            def lru(i):
                dve.wait_ge(decays, i + 1)
                step(V.tensor_scalar(mul, mul, -1.0, 1.0, ALU.mult, ALU.add))
                V.tensor_scalar(mul, mul, 1e-30, None, ALU.max).then_inc(one_minus, 1)
                step(V.tensor_tensor(gx, gx, xc, ALU.mult))
                dve.wait_ge(root, i + 1)
                step(V.tensor_tensor(gx, gx, mul, ALU.mult))
                step(V.tensor_tensor_scan(lrx[:, i, :], ga, gx, 0.0, ALU.mult, ALU.add))
                V.tensor_tensor(lrx[:, i, :], lrx[:, i, :], lry[:, i, :], ALU.mult).then_inc(lru_ready, 1)

            was_read(dve, ("in", "lru_y", 1, 1))
            dve.wait_ge(h_rows_ready, TT)
            lru_conv(0)
            for h in range(2):
                full(dve, ("mean", h))
                cols = slice(h * HALF, (h + 1) * HALF)
                mark(V.tensor_tensor(cfb[:, 0, cols], cfb[:, 0, cols], bank(("mean", h)), ALU.subtract))
                finish(V.tensor_tensor(cfb[:, 1, cols], cfb[:, 1, cols], bank(("mean", h)), ALU.subtract))
            dve.wait_ge(xc_ready, 1)
            lru(0)
            was_read(dve, ("var", 1))
            step(V.reciprocal(cfa[:, 0, :], cfa[:, 0, :]))
            was_read(dve, ("mean", 1))
            mark(V.tensor_tensor(cfb[:, 0, :], cfb[:, 0, :], cfa[:, 0, :], ALU.mult))
            V.tensor_tensor(cfb[:, 1, :], cfb[:, 1, :], cfa[:, 0, :], ALU.mult).then_inc(cf_scaled, 1)
            lru_conv(1)
            dve.wait_ge(xc_ready, 2)
            lru(1)

            def score_read_unit(u):
                h, q = UNITS[u]
                nk = (q + 1) * P
                dve.wait_ge(alibi_ready, h + 1)
                if u >= 2:
                    full(dve, ("pT",) + UNITS[u - 2] + (UNITS[u - 2][1] // 4,))
                for c in range(2):
                    dve.wait_ge(score_full, 2 * u + c + 1)
                    V.tensor_tensor_reduce(
                        out=maps[:, u % 2, c, 0:nk],
                        in0=ps[:, 2 * c:2 * c + 2, :].rearrange("p b n -> p (b n)")[:, 0:nk],
                        in1=scr[:, h % 2, S - nk:S], scale=1.0, scalar=-3.0e38, op0=ALU.add, op1=ALU.max,
                        accum_out=top[:, u % 2, c:c + 1]).then_inc(score_read, 1)
                dve.wait_ge(score_read, 2 * u + 2)
                V.tensor_scalar(ntop[:, u % 2, :], top[:, u % 2, :], -SCALE, None, ALU.mult).then_inc(top_ready, 1)

            def combine(u):
                h, q = UNITS[u]
                nk = (q + 1) * P
                dve.wait_ge(exp_ready, 2 * u + 2)
                step(V.reciprocal(rmass[:, u % 4, :], mass[:, u % 2, :]))
                step(V.scalar_tensor_tensor(coef[:, u % 2, :], mass[:, u % 2, 0:1], neg_lam, rmass[:, u % 4, 1:2],
                                            ALU.mult, ALU.mult))
                V.scalar_tensor_tensor(maps[:, u % 2, 0, 0:nk], maps[:, u % 2, 1, 0:nk], coef[:, u % 2, :],
                                       maps[:, u % 2, 0, 0:nk], ALU.mult, ALU.add).then_inc(map_ready, 1)

            def o_read(u):
                h, q = UNITS[u]
                o = oT[:, h, q * P:(q + 1) * P]
                full(dve, ("o", h, q))
                finish(V.tensor_scalar(o, bank(("o", h, q))[:, 0:P], rmass[:, u % 4, 0:1], None, ALU.mult))
                was_read(dve, ("o", h, q))
                V.tensor_tensor_reduce(out=sq_out[:, :], in0=o, in1=o, scale=1.0, scalar=0.0, op0=ALU.mult,
                                       op1=ALU.add, accum_out=o_sq[:, u:u + 1]).then_inc(o_ready, 1)

            score_read_unit(0)
            score_read_unit(1)
            combine(0)
            for u in range(len(UNITS)):
                if u + 1 < len(UNITS):
                    combine(u + 1)
                if u:
                    o_read(u - 1)
                if u + 2 < len(UNITS):
                    score_read_unit(u + 2)
            o_read(len(UNITS) - 1)
            dve.wait_ge(o_root, 1)
            step(V.reciprocal(o_inv[:, :], o_std[:, :]))
            for h in range(HEADS):
                o = oT[:, h, :].rearrange("p (q n) -> p q n", n=P)
                V.tensor_tensor(o, o, o_inv[:, h * TT:(h + 1) * TT].unsqueeze(2).broadcast_to([P, TT, P]),
                                ALU.mult).then_inc(o_scaled, 1)

            def mix_read(t):
                for c in range(2):
                    full(dve, ("mix", t, c))
                    cols = slice(c * HALF, (c + 1) * HALF)
                    finish(V.scalar_tensor_tensor(h_res[:, t, cols], h_res[:, t, cols], ALPHA,
                                                  bank(("mix", t, c)), ALU.mult, ALU.add))
                was_read(dve, ("mix", t, 1))
                row_stats(h_res[:, t, :], t).then_inc(mix_mean, 1)
                dve.wait_ge(mix_mean, t + 1)
                dve.wait_ge(mix_std, t + 1)
                norm_terms(t, t + 1).then_inc(mix_norm, 1)
                dve.wait_ge(norm_loaded[1], 32)
                dve.wait_ge(mix_normed, t + 1)
                step(V.tensor_tensor(h_res[:, t, :], h_res[:, t, :], norm_rows[:, 0, :], ALU.mult))
                V.tensor_tensor(h_res[:, t, :], h_res[:, t, :], norm_rows[:, 1, :], ALU.add).then_inc(h1_ready, 1)

            def logit_read(t):
                full(dve, ("logit", t))
                finish(V.tensor_tensor(logits[:, t, :], bank(("logit", t))[:, 0:EXPERTS], router_bias[:, :], ALU.add))
                was_read(dve, ("logit", t))
                step(V.max(best[:, t, :], logits[:, t, :]))
                step(V.max_index(best_at[:, t, :], best[:, t, :], logits[:, t, :]))

            for t in range(TT):
                mix_read(t)
                if t:
                    logit_read(t - 1)
            logit_read(TT - 1)

            def pick_rows(g, ranks_now):
                wide_s = [P, TT, CAP]
                V.tensor_tensor(pick, iota_s[:, :].unsqueeze(1).broadcast_to(wide_s),
                                ranks_now.unsqueeze(2).broadcast_to(wide_s), ALU.is_equal).then_inc(pick_ready, 1)

            def pick_block(g, expert):
                own = rank_of[:, bass.ds(expert, 1), :].rearrange("p e t -> p (e t)")
                V.tensor_scalar(rank_now[:, :], own, offset_f[:, bass.ds(g, 1)], None, ALU.add).then_inc(rank_step, 1)
                dve.wait_ge(rank_step, g)
                pick_rows(g, rank_now[:, :])

            def slots_read(g):
                dve.wait_ge(slots_full, g + 1)
                V.tensor_copy(token_at[:, :], ps[:, 7, 0:2]).then_inc(slots_ready, 1)

            def xT_read_low(g, tiles):
                dve.wait_ge(xT_high_ready, g + 1)
                V.tensor_tensor(xT_low[:, :, 0:tiles * P].rearrange("p k (t n) -> p t k n", n=P),
                                ps[:, 4:4 + 2 * tiles, :].rearrange("p (t b) (k n) -> p t (b k) n", b=2, n=P),
                                xT_high[:, :, 0:tiles * P].bitcast(F32).rearrange("p k (t n) -> p t k n", n=P),
                                ALU.subtract).then_inc(xT_read, 1)

            V.tensor_tensor(gates[:, :, :], best[:, :, 0:TOP_K], best[:, :, 0:1].broadcast_to([P, TT, TOP_K]),
                            ALU.subtract).then_inc(gate_diff, 1)
            step(V.tensor_copy(chosen[:, :, :], best_at[:, :, 0:TOP_K]))
            wide = [P, TT, EXPERTS]
            for k in range(TOP_K):
                mark(V.tensor_tensor(one_hot[:, k, :, :], iota_e[:, :].unsqueeze(1).broadcast_to(wide),
                                     chosen[:, :, k:k + 1].broadcast_to(wide), ALU.is_equal))
            settle()
            step(V.tensor_tensor(mask[:, :, :], one_hot[:, 0, :, :], one_hot[:, 1, :, :], ALU.add))
            step(V.tensor_tensor(mask[:, :, :], mask[:, :, :], one_hot[:, 2, :, :], ALU.add))
            step(V.tensor_tensor(mask[:, :, :], mask[:, :, :], one_hot[:, 3, :, :], ALU.add))
            V.tensor_copy(mask_b[:, :, :], mask[:, :, :]).then_inc(mask_ready, 1)
            full(dve, "rank")
            mark(V.tensor_copy(ranks, bank("rank")[:, 0:TT * EXPERTS].rearrange("p (t e) -> p t e", e=EXPERTS)))
            finish(V.tensor_copy(count[:, :], bank("rank")[:, TT * EXPERTS:(TT + 1) * EXPERTS]))
            settle()
            step(V.scalar_tensor_tensor(rank_of[:, :, :].rearrange("p e t -> p t e"), ranks, 1.0, mask[:, :, :],
                                        ALU.add, ALU.mult))
            step(V.tensor_scalar(rank_of[:, :, :], rank_of[:, :, :], -1.0, None, ALU.add))
            pick_rows(0, rank_of[:, 0, :])
            was_read(dve, "rank")
            step(V.tensor_scalar(blocks[:, :], count[:, :], float(CAP), 1.0, ALU.is_gt, ALU.add))
            step(V.scalar_tensor_tensor(blocks[:, :], count[:, :], 2.0 * CAP, blocks[:, :], ALU.is_gt, ALU.add))
            step(V.scalar_tensor_tensor(blocks[:, :], count[:, :], 3.0 * CAP, blocks[:, :], ALU.is_gt, ALU.add))
            step(V.tensor_tensor_scan(ends[:, :], ones_t[:, 0:EXPERTS], blocks[:, :], 0.0, ALU.mult, ALU.add))
            mark(V.tensor_tensor(starts[:, :], ends[:, :], blocks[:, :], ALU.subtract))
            mark(V.tensor_copy(ends_i[:, :], ends[0:1, :]))
            slots_read(0)
            table = [P, TABLE, EXPERTS]
            step(V.tensor_tensor(cmp, ends[:, :].unsqueeze(1).broadcast_to(table),
                                 iota_g[:, :].unsqueeze(2).broadcast_to(table), ALU.is_le))
            step(V.tensor_reduce(expert_f[:, :], cmp, AX.X, ALU.add))
            step(V.tensor_scalar(expert_f[:, :], expert_f[:, :], EXPERTS - 1.0, None, ALU.min))
            mark(V.tensor_copy(expert_i[:, :], expert_f[0:1, :]))
            step(V.tensor_tensor(cmp, iota_e[:, :].unsqueeze(1).broadcast_to(table),
                                 expert_f[:, :].unsqueeze(2).broadcast_to(table), ALU.is_equal))
            step(V.tensor_tensor(cmp, cmp, starts[:, :].unsqueeze(1).broadcast_to(table), ALU.mult))
            step(V.tensor_reduce(offset_f[:, :], cmp, AX.X, ALU.add))
            step(V.tensor_tensor(offset_f[:, :], offset_f[:, :], iota_g[:, :], ALU.subtract))
            step(V.tensor_scalar(offset_f[:, :], offset_f[:, :], float(CAP), None, ALU.mult))
            step(V.tensor_tensor(cmp, iota_e[:, :].unsqueeze(1).broadcast_to(table),
                                 expert_f[:, :].unsqueeze(2).broadcast_to(table), ALU.is_equal))
            step(V.tensor_tensor(cmp, cmp, count[:, :].unsqueeze(1).broadcast_to(table), ALU.mult))
            step(V.tensor_reduce(left_f[:, :], cmp, AX.X, ALU.add))
            step(V.tensor_tensor(left_f[:, :], left_f[:, :], offset_f[:, :], ALU.add))
            mark(V.tensor_copy(left_i[:, :], left_f[0:1, :]))
            step(V.tensor_scalar(row_f[:, 0, :], left_f[:, :], float(CAP), None, ALU.min))
            step(V.tensor_tensor_scan(row_f[:, 1, :], ones_t[:, :], row_f[:, 0, :], 0.0, ALU.mult, ALU.add))
            step(V.tensor_tensor(row_f[:, 1, :], row_f[:, 1, :], row_f[:, 0, :], ALU.subtract))
            mark(V.tensor_copy(row_i[:, :], row_f[0:1, 1, :]))
            xT_read_low(0, 2)
            settle()
            V.engine_nop().then_inc(tables_ready, 1)
            step(V.tensor_tensor_scan(first[:, :], ones_t[:, 0:EXPERTS], count[:, :], 0.0, ALU.mult, ALU.add))
            step(V.tensor_tensor(first[:, :], first[:, :], count[:, :], ALU.subtract))
            step(V.tensor_tensor(rows_at[:, :, :], ranks, first[:, :].unsqueeze(1).broadcast_to(wide), ALU.add))
            for k in range(TOP_K):
                step(V.tensor_tensor(cmp[:, 0:TT, :], one_hot[:, k, :, :], rows_at[:, :, :], ALU.mult))
                step(V.tensor_reduce(dest[:, :, k], cmp[:, 0:TT, :], AX.X, ALU.add))
            step(V.tensor_copy(dest_i[:, :, :], dest[:, :, :]))

            dve.wait_ge(gate_exp, 1)
            step(V.tensor_reduce(gsum[:, :], gates[:, :, :], AX.X, ALU.add))
            step(V.reciprocal(gsum[:, :], gsum[:, :]))
            step(V.tensor_tensor(gates[:, :, :], gates[:, :, :], gsum[:, :].unsqueeze(2).broadcast_to([P, TT, TOP_K]), ALU.mult))
            dve.wait_ge(low_by_dve, 3)

            total = dve.value_load(ends_i[0:1, EXPERTS - 1:EXPERTS], min_val=EXPERTS, max_val=MAX_BLOCKS)
            with dve.Fori(0, total) as g:
                after = dve.value_load(expert_i[0:1, bass.ds(g + 1, 1)], min_val=0, max_val=EXPERTS - 1)

                def body(tiles, ahead):
                    def clip(c, part):
                        dve.wait_ge(piece_done, g * PIECES + (4 * c + 2 * part + 2))
                        dst = (glu, lin)[part]
                        V.tensor_scalar(dst[:, 0:tiles, :], ps[:, 2 * part:2 * part + tiles, :], LIMIT,
                                        -LIMIT if part else None, ALU.min,
                                        ALU.max if part else ALU.bypass).then_inc(hidden_read, 1)

                    def product(c):
                        dve.wait_ge(sig_ready, g * 2 + (c + 1))
                        V.tensor_tensor(sig[:, 0:tiles, :], sig[:, 0:tiles, :], glu[:, 0:tiles, :],
                                        ALU.mult).then_inc(swish_step, 1)
                        dve.wait_ge(hidden_read, g * 4 + (2 * c + 2))
                        dve.wait_ge(swish_step, g * 2 + (c + 1))
                        V.scalar_tensor_tensor(lin[:, 0:tiles, :], lin[:, 0:tiles, :], 1.0, sig[:, 0:tiles, :],
                                               ALU.add, ALU.mult).then_inc(act_rows, 1)

                    def aT_read_low(c):
                        dve.wait_ge(aT_high_ready, g * 2 + (c + 1))
                        part = act_low[:, HK * c:HK * (c + 1), 0:tiles * P].rearrange("p k (t n) -> p t k n", n=P)
                        src = ps[:, 4 + 2 * c:4 + 2 * c + tiles, :].rearrange("p t (k n) -> p t k n", n=P)
                        rounded = act_high[:, HK * c:HK * (c + 1), 0:tiles * P].bitcast(F32)\
                            .rearrange("p k (t n) -> p t k n", n=P)
                        V.tensor_tensor(part, src, rounded, ALU.subtract).then_inc(aT_read, 1)

                    split_low(dve, V, g, 4)
                    clip(0, 0)
                    pick_block(g + 1, after)
                    split_low(dve, V, g, 6)
                    clip(0, 1)
                    product(0)
                    slots_read(g + 1)
                    split_low(dve, V, g, 7)
                    clip(1, 0)
                    aT_read_low(0)
                    split_low(dve, V, g, 9)
                    clip(1, 1)
                    product(1)
                    split_low(dve, V, g, 10)
                    aT_read_low(1)
                    split_low(dve, V, g, 12)
                    xT_read_low(g + 1, ahead)
                    split_low(dve, V, g, 13)
                    split_low(dve, V, g, 15)

                by_tiles(dve, g, body)

            for t in range(TT + 1):
                if t < TT:
                    dve.wait_ge(alpha_ready, t + 1)
                    for k in range(TOP_K):
                        dve.wait_ge(got[TOP_K * (t % GOT) + k], 16 * (t // GOT + 1))
                        step(V.scalar_tensor_tensor(h_res[:, t, :], y_got[t % GOT][:, k, :], gates[:, t, k:k + 1],
                                                    h_res[:, t, :], ALU.mult, ALU.add))
                    row_stats(h_res[:, t, :], t).then_inc(summed, 1)
                    dve.wait_ge(summed, t + 1)
                    dve.wait_ge(fin_std, t + 1)
                    norm_terms(t, t + 1).then_inc(fin_norm, 1)
                if t:
                    if t == 1:
                        dve.wait_ge(norm_loaded[2], 32)
                    dve.wait_ge(fin_gain, t)
                    V.tensor_tensor(h_res[:, t - 1, :], h_res[:, t - 1, :], norm_rows[:, 1, :], ALU.add).then_inc(out_ready, 1)

        @block.tensor
        def _(pe):
            T = nc.tensor

            def begin(name):
                if NUMBER[name] >= 4:
                    was_read(pe, JOBS[NUMBER[name] - 4][0])

            def end(ins):
                ins.then_inc(job_full, 1)

            pe.wait_ge(const_ready, 1)
            pe.wait_ge(dpar_loaded, 48)
            end(T.transpose(bank("dpar")[:, 0:2 * KT + 1], dpar_rows, ident[0:2 * KT + 1, 0:2 * KT + 1]))
            def hT_write(hf):
                for k in range(KT):
                    begin(("hT", hf, k))
                    for t in range(4):
                        if not k:
                            pe.wait_ge(normed, 4 * hf + t + 1)
                        last = T.transpose(bank(("hT", hf, k))[:, t * P:(t + 1) * P],
                                           h_res[:, 4 * hf + t, k * P:(k + 1) * P], ident[:, :])
                    end(last)

            def loaded(name):
                i = IN_PIECES.index(name)
                pe.wait_ge(w_loaded[i % FRONT_SLOTS], 16 * (i // FRONT_SLOTS + 1))
                return slot(i % FRONT_SLOTS)

            def in_write(p, c, h):
                name = ("in", p, c, h)
                w = loaded(p)
                begin(name)
                for k in range(KT):
                    last = T.matmul(bank(name), w[:, k, c * P:(c + 1) * P], hT[:, k, h * HALF:(h + 1) * HALF],
                                    start=k == 0, stop=k == KT - 1)
                end(last)

            def v_write(t):
                begin(("v", t))
                for c in range(2):
                    w = loaded(f"v{c}")
                    for k in range(KT):
                        last = T.matmul(bank(("v", t))[:, c * PIECE:(c + 1) * PIECE], hT[:, k, t * P:(t + 1) * P],
                                        w[:, k, :], start=k == 0, stop=k == KT - 1)
                end(last)

            def gate_write(i):
                pe.wait_ge(gate_w_loaded, 16 * 2 * CT * 2)
                pe.wait_ge(xc_ready, i + 1)
                for w, wn in enumerate(("a", "x")):
                    for h in range(2):
                        begin(("gate", i, wn, h))
                        end(T.matmul(bank(("gate", i, wn, h)), gate_w[:, w, i, :], xc[:, h * HALF:(h + 1) * HALF],
                                     start=True, stop=True))

            def channel_sum(kind, src):
                for h in range(2):
                    begin((kind, h))
                    if kind == "var":
                        pe.wait_ge(squared, h + 1)
                    for i in range(CT):
                        last = T.matmul(bank((kind, h)), chan_mean[:, :], src[:, i, h * HALF:(h + 1) * HALF],
                                        start=i == 0, stop=i == CT - 1)
                    end(last)

            hT_write(0)
            was_read(pe, ("hT", 0, KT - 1))
            was_read(pe, ("hT", 0, KT - 2))
            for p in ("cf_a", "cf_b"):
                for c in range(CT):
                    in_write(p, c, 0)
            hT_write(1)
            was_read(pe, ("hT", 1, KT - 1))
            was_read(pe, ("hT", 1, KT - 2))
            pe.wait_ge(params_loaded, PARAM_LOADS)
            begin("chan")
            for i in range(CT):
                last = T.transpose(bank("chan")[:, i * CHAN_ROWS:(i + 1) * CHAN_ROWS], chan_rows[:, i * P:(i + 1) * P],
                                   ident[0:CHAN_ROWS, 0:CHAN_ROWS])
            end(last)
            for p in ("cf_a", "cf_b"):
                for c in range(CT):
                    in_write(p, c, 1)
            for p in ("lru_x", "lru_y"):
                for c in range(CT):
                    for h in range(2):
                        in_write(p, c, h)
            for t in range(4):
                v_write(t)
            pe.wait_ge(const_ready, 2)
            pe.wait_ge(conv_out, 1)
            channel_sum("mean", cfb)
            v_write(4)
            v_write(5)
            gate_write(0)
            v_write(6)
            v_write(7)
            channel_sum("var", cfa)
            for c in range(CT):
                for h in range(2):
                    in_write("q0", c, h)
            gate_write(1)
            for p in ("q1", "k0", "k1"):
                for c in range(CT):
                    for h in range(2):
                        in_write(p, c, h)

            def scores(u):
                h, q = UNITS[u]
                for c in range(2):
                    if u:
                        pe.wait_ge(score_read, 2 * (u - 1) + c + 1)
                    for b in range(q // 4 + 1):
                        nk = min(HALF, (q + 1) * P - b * HALF)
                        last = T.matmul(ps[:, 2 * c + b, 0:nk], qT[DK * c:DK * (c + 1), h, q * P:(q + 1) * P],
                                        kT[DK * c:DK * (c + 1), h, b * HALF:b * HALF + nk], start=True, stop=True)
                    last.then_inc(score_full, 1)

            def attend(u):
                h, q = UNITS[u]
                pe.wait_ge(map_ready, u + 1)
                for g in range(q // 4 + 1):
                    begin(("pT", h, q, g))
                    for k in range(4 * g, min(4 * g + 4, q + 1)):
                        last = T.transpose(bank(("pT", h, q, g))[:, (k % 4) * P:(k % 4 + 1) * P],
                                           maps[:, u % 2, 0, k * P:(k + 1) * P], ident[:, :])
                    end(last)

            def values(u):
                h, q = UNITS[u]
                begin(("o", h, q))
                was_read(pe, ("pT", h, q, q // 4))
                for k in range(q + 1):
                    last = T.matmul(bank(("o", h, q))[:, 0:P], pT[:, u % 2, k, :], v[:, k, h * DV:(h + 1) * DV],
                                    start=k == 0, stop=k == q)
                end(last)

            was_read(pe, ("in", "k1", 1, 1))
            scores(0)
            scores(1)
            for u in range(len(UNITS)):
                attend(u)
                if u:
                    values(u - 1)
                if u + 2 < len(UNITS):
                    scores(u + 2)
            values(len(UNITS) - 1)
            for h in range(HEADS):
                pe.wait_ge(o_scaled, h + 1)
                for g in range(2):
                    begin(("oT", h, g))
                    for q in range(4 * g, 4 * g + 4):
                        last = T.transpose(bank(("oT", h, g))[:, (q % 4) * P:(q % 4 + 1) * P],
                                           oT[:, h, q * P:(q + 1) * P], ident[:, :])
                    end(last)

            def mix_write(t):
                for c in range(2):
                    begin(("mix", t, c))
                    for i in (2 * c, 2 * c + 1):
                        if not t:
                            pe.wait_ge(w_loaded[i], BEFORE[i])
                        for k in range(KT):
                            src = oT[:, k, :] if k < 4 else lrx[:, k - 4, :] if k < 6 else cfb[:, k - 6, :]
                            last = T.matmul(bank(("mix", t, c))[:, (i % 2) * PIECE:(i % 2 + 1) * PIECE],
                                            src[:, t * P:(t + 1) * P], slot(i)[:, k, :], start=k == 0, stop=k == KT - 1)
                    end(last)

            def route(t):
                pe.wait_ge(h1_ready, t + 1)
                for g in range(2):
                    begin(("h1T", t, g))
                    for k in range(4 * g, 4 * g + 4):
                        last = T.transpose(bank(("h1T", t, g))[:, (k % 4) * P:(k % 4 + 1) * P],
                                           h_res[:, t, k * P:(k + 1) * P], ident[:, :])
                    end(last)
                begin(("logit", t))
                was_read(pe, ("h1T", t, 1))
                for k in range(KT):
                    last = T.matmul(bank(("logit", t))[:, 0:EXPERTS], h1T[:, k, :], router[:, k, :],
                                    start=k == 0, stop=k == KT - 1)
                end(last)

            was_read(pe, ("oT", HEADS - 1, 1))
            pe.wait_ge(cf_ready, CT)
            pe.wait_ge(lru_ready, CT)
            for t in range(TT + 1):
                if t < TT:
                    mix_write(t)
                if t:
                    route(t - 1)

            begin("rank")
            pe.wait_ge(mask_ready, 1)
            for t in range(TT + 1):
                dst = bank("rank")[:, t * EXPERTS:(t + 1) * EXPERTS]
                for s in range(t):
                    last = T.matmul(dst, ones[:, :], mask_b[:, s, :], start=s == 0, stop=t == TT and s == TT - 1)
                if t < TT:
                    last = T.matmul(dst, before[:, :], mask_b[:, t, :], start=t == 0, stop=True)
            end(last)

            def slots_write(g):
                pe.wait_ge(pick_ready, g + 1)
                for th in range(2):
                    for t in range(TT):
                        last = T.matmul(ps[:, 7, th:th + 1], pick[:, t, th * P:(th + 1) * P], token_no[:, t:t + 1],
                                        start=t == 0, stop=t == TT - 1)
                last.then_inc(slots_full, 1)

            def xT_write(tiles):
                for th in range(tiles):
                    for k in range(KT):
                        last = T.transpose(ps[:, 4 + 2 * th + k // 4, (k % 4) * P:(k % 4 + 1) * P],
                                           x_rows[:, th, k * P:(k + 1) * P], ident[:, :])
                last.then_inc(xT_full, 1)

            was_read(pe, "rank")
            slots_write(0)
            pe.wait_ge(x_got, 32)
            xT_write(2)

            pe.wait_ge(ones_r_ready, 1)
            pe.wait_ge(tables_ready, 1)
            total = pe.value_load(ends_i[0:1, EXPERTS - 1:EXPERTS], min_val=EXPERTS, max_val=MAX_BLOCKS)
            with pe.Fori(0, total) as g:

                def body(tiles, ahead):
                    def piece(p):
                        wait_low(pe, g, p)
                        if p < 8:
                            part, kh, (x_high, x_low) = p // 2 % 2, p % 2, (xT_high, xT_low)
                            if not kh and p < 4:
                                pe.wait_ge(y_read, g * 2 + (part + 1))
                            elif not kh:
                                pe.wait_ge(hidden_read, g * 4 + (part + 1))
                        else:
                            part, kh, (x_high, x_low) = p % 2, (p - 8) // 2, (act_high, act_low)
                            if not kh:
                                pe.wait_ge(hidden_read, g * 4 + (part + 3))
                            if not part:
                                pe.wait_ge(aT_read, g * 2 + (kh + 1))
                        for t in range(tiles):
                            dst = ps[:, 2 * part + t, :]
                            if p < 8 and not kh:
                                if not p and not t:
                                    pe.wait_ge(b1_loaded, g * 16 + 16)
                                T.matmul(dst, ones_r[0:2, :], bias_now[0:2, part, p // 4, :], start=True, stop=False)
                            for k in range(HK):
                                tokens = (slice(None), HK * kh + k, slice(t * P, (t + 1) * P))
                                w_high, w_low = high[:, p % SPLIT, k, :], low[:, p % SPLIT, k, :]
                                T.matmul(dst, x_high[tokens], w_high, start=p >= 8 and not kh and not k, stop=False)
                                T.matmul(dst, x_high[tokens], w_low, start=False, stop=False)
                                last = T.matmul(dst, x_low[tokens], w_high, start=False,
                                                stop=p < 8 and kh == 1 and k == HK - 1)
                            if p >= 8 and kh:
                                if not part and not t:
                                    pe.wait_ge(b2_loaded, g * 32 + 32)
                                last = T.matmul(dst, ones_r[0:2, :], b2_now[part][0:2, :], start=False, stop=True)
                        last.then_inc(piece_done, 1)

                    def aT_write(c):
                        pe.wait_ge(act_rows, g * 2 + (c + 1))
                        for t in range(tiles):
                            for k in range(HK):
                                last = T.transpose(ps[:, 4 + 2 * c + t, k * P:(k + 1) * P],
                                                   lin[:, t, k * P:(k + 1) * P], ident[:, :])
                        last.then_inc(aT_full, 1)

                    pe.wait_ge(xT_read, g + 1)
                    for p in range(4):
                        piece(p)
                    piece(4)
                    slots_write(g + 1)
                    piece(5)
                    aT_write(0)
                    piece(6)
                    piece(7)
                    piece(8)
                    aT_write(1)
                    piece(9)
                    pe.wait_ge(x_got, g * 32 + 64)
                    pe.wait_ge(aT_read, g * 2 + 2)
                    xT_write(ahead)
                    piece(10)
                    piece(11)

                by_tiles(pe, g, body)


_OUT = (1, S, D)


def kernel(**inputs):
    import numpy as np
    import concourse.bacc as bacc
    from concourse.bass_utils import run_bass_kernel_spmd

    names = ["x", "ln_in_g", "ln_in_b", "w_in", "lam_q1", "lam_k1", "lam_q2", "lam_k2", "subln_g",
             "lru_conv_w", "lru_conv_b", "lru_wa", "lru_ba", "lru_wx", "lru_bx", "lru_lambda",
             "cf_conv_w", "cf_conv_b", "cf_ln_g", "cf_ln_b", "w_out", "ln1_g", "ln1_b",
             "router_w", "router_b", "moe_w1", "moe_b1", "moe_w2", "moe_b2", "ln2_g", "ln2_b"]
    nc = bacc.Bacc("TRN2", target_bir_lowering=False, num_devices=1)
    arrays, args = {}, []
    for name in names:
        a = np.ascontiguousarray(inputs[name])
        arrays[f"in_{name}"] = a
        args.append(nc.dram_tensor(f"in_{name}", a.shape, mybir.dt.from_np(a.dtype), kind="ExternalInput").ap())
    out = nc.dram_tensor("out", _OUT, F32, kind="ExternalOutput").ap()
    hybrid_layer(nc, *args, out)
    result = run_bass_kernel_spmd(nc, [arrays], core_ids=[0])
    return result.results[0]["out"]
```
